# Optimizing a Trainium2 kernel written in Bass

```python
import jax, jax.numpy as jnp
from jax import lax
import numpy as np

D_MODEL = 1024
BATCH = 1
SEQ = 512
DEPTH = 1
DEC_BATCH = 8
DEC_SEQ = 4
PAST_LEN = 2048
PAGE_SIZE = 128

POOL_WINDOWS = (2, 4, 8, 16)
N_POOL_GROUPS = len(POOL_WINDOWS)
POOL_GROUP = D_MODEL // 8
POOL_WIDTH = N_POOL_GROUPS * POOL_GROUP
POOL_BUF = max(POOL_WINDOWS) - 1
N_HEADS = 8
N_KV_HEADS = 2
HEAD_DIM = 64
GROUP = N_HEADS // N_KV_HEADS
Q_WIDTH = N_HEADS * HEAD_DIM
KV_WIDTH = N_KV_HEADS * HEAD_DIM
WINDOW = 128
ROPE_THETA = 10000.0
N_BRANCH = 2
IN_WIDTH = POOL_WIDTH + Q_WIDTH + 2 * KV_WIDTH + N_BRANCH * D_MODEL
D_FF = ((8 * D_MODEL // 3 + 127) // 128) * 128
ALPHA = (2.0 * DEPTH) ** 0.25
BETA = (8.0 * DEPTH) ** -0.25
LN_EPS = 1e-5
NEG_INF = -1e30

kernel_name = "hybrid_pool_swa_macaron_deepnorm_step"

def layer_norm(x, g, b):
    xf = x.astype(jnp.float32)
    mu = jnp.mean(xf, axis=-1, keepdims=True)
    var = jnp.mean(jnp.square(xf - mu), axis=-1, keepdims=True)
    y = (xf - mu) * lax.rsqrt(var + LN_EPS) * g.astype(jnp.float32) + b.astype(jnp.float32)
    return y.astype(x.dtype)

def swiglu(x, w1, w3, w2):
    return (jax.nn.silu(x @ w1) * (x @ w3)) @ w2

def ffn_half_step(x, w1, w3, w2, g, b):
    return layer_norm(ALPHA * x + 0.5 * swiglu(x, w1, w3, w2), g, b)

def rope(x, pos):
    half = HEAD_DIM // 2
    freqs = ROPE_THETA ** (-2.0 * jnp.arange(half, dtype=jnp.float32) / HEAD_DIM)
    ang = pos.astype(jnp.float32)[:, None] * freqs[None, :]
    cos = jnp.cos(ang)[:, None, :]
    sin = jnp.sin(ang)[:, None, :]
    xf = x.astype(jnp.float32)
    x1, x2 = xf[..., :half], xf[..., half:]
    return jnp.concatenate([x1 * cos - x2 * sin, x1 * sin + x2 * cos], axis=-1).astype(x.dtype)

def split_in(h, w_in):
    B, T, _ = h.shape
    z = h @ w_in
    o = 0
    u = z[..., o:o + POOL_WIDTH]; o += POOL_WIDTH
    q = z[..., o:o + Q_WIDTH].reshape(B, T, N_HEADS, HEAD_DIM); o += Q_WIDTH
    k = z[..., o:o + KV_WIDTH].reshape(B, T, N_KV_HEADS, HEAD_DIM); o += KV_WIDTH
    v = z[..., o:o + KV_WIDTH].reshape(B, T, N_KV_HEADS, HEAD_DIM); o += KV_WIDTH
    gates = z[..., o:].reshape(B, T, N_BRANCH, D_MODEL)
    return u, q, k, v, gates

def multiscale_pool(ctx, u, start_pos, w_grp, scale):
    B, T, P = u.shape
    C = ctx.shape[1]
    maxw = max(POOL_WINDOWS)
    full = jnp.concatenate([jnp.zeros((B, maxw, P), jnp.float32),
                            ctx.astype(jnp.float32), u.astype(jnp.float32)], axis=1)
    cs = jnp.cumsum(full, axis=1)
    lo = maxw + C
    cur = cs[:, lo:lo + T]
    pos = start_pos + jnp.arange(T, dtype=jnp.int32)
    uf = u.astype(jnp.float32)
    groups = []
    for g, w in enumerate(POOL_WINDOWS):
        sl = slice(g * POOL_GROUP, (g + 1) * POOL_GROUP)
        win_sum = cur[..., sl] - cs[:, lo - w:lo - w + T, sl]
        cnt = jnp.minimum(pos + 1, w).astype(jnp.float32)[None, :, None]
        groups.append(win_sum / cnt - uf[..., sl])
    z = jnp.stack(groups, axis=2).astype(u.dtype)
    z = jnp.einsum('btgc,gcd->btgd', z, w_grp).reshape(B, T, P)
    return z * scale

def sink_attention(qb, kb, vb, mask, sinks):
    s = jnp.einsum('bnqkgd,bnjkd->bnkgqj', qb, kb,
                   preferred_element_type=jnp.float32) * (HEAD_DIM ** -0.5)
    s = jnp.where(mask[None, :, None, None], s, NEG_INF)
    sink = sinks.astype(jnp.float32)[None, None, :, :, None]
    m = jnp.maximum(jnp.max(s, axis=-1), sink)
    p = jnp.exp(s - m[..., None])
    denom = jnp.sum(p, axis=-1) + jnp.exp(sink - m)
    probs = (p / denom[..., None]).astype(vb.dtype)
    return jnp.einsum('bnkgqj,bnjkd->bnqkgd', probs, vb)

def merge_out(pool_z, attn_o, gates, w_pool_out, w_attn_out, w_out):
    g = jax.nn.sigmoid(gates.astype(jnp.float32)).astype(pool_z.dtype)
    m = g[..., 0, :] * (pool_z @ w_pool_out) + g[..., 1, :] * (attn_o @ w_attn_out)
    return m @ w_out

def mixer_prompt(h, w_in, w_grp, pool_scale, sinks, w_pool_out, w_attn_out, w_out):
    B, S, _ = h.shape
    u, q, k, v, gates = split_in(h, w_in)
    pos = jnp.arange(S, dtype=jnp.int32)
    q = rope(q, pos)
    k = rope(k, pos)
    pool_z = multiscale_pool(jnp.zeros((B, 0, POOL_WIDTH), u.dtype), u, 0, w_grp, pool_scale)
    nb = S // WINDOW
    qb = q.reshape(B, nb, WINDOW, N_KV_HEADS, GROUP, HEAD_DIM)
    kb = k.reshape(B, nb, WINDOW, N_KV_HEADS, HEAD_DIM)
    vb = v.reshape(B, nb, WINDOW, N_KV_HEADS, HEAD_DIM)
    kk = jnp.concatenate([jnp.concatenate([jnp.zeros_like(kb[:, :1]), kb[:, :-1]], axis=1), kb], axis=2)
    vv = jnp.concatenate([jnp.concatenate([jnp.zeros_like(vb[:, :1]), vb[:, :-1]], axis=1), vb], axis=2)
    blk = jnp.arange(nb, dtype=jnp.int32)[:, None] * WINDOW
    qpos = blk + jnp.arange(WINDOW, dtype=jnp.int32)[None, :]
    kpos = blk - WINDOW + jnp.arange(2 * WINDOW, dtype=jnp.int32)[None, :]
    diff = qpos[:, :, None] - kpos[:, None, :]
    mask = (diff >= 0) & (diff <= WINDOW) & (kpos[:, None, :] >= 0)
    attn = sink_attention(qb, kk, vv, mask, sinks.reshape(N_KV_HEADS, GROUP))
    attn_o = attn.reshape(B, S, Q_WIDTH)
    m = merge_out(pool_z, attn_o, gates, w_pool_out, w_attn_out, w_out)
    wb = min(WINDOW, S)
    return m, u[:, S - POOL_BUF:], k[:, S - wb:], v[:, S - wb:]

def mixer_sample(h, pool_ctx, k_ctx, v_ctx, w_in, w_grp, pool_scale, sinks,
                 w_pool_out, w_attn_out, w_out):
    Bd, T, _ = h.shape
    wb = k_ctx.shape[1]
    u, q, k, v, gates = split_in(h, w_in)
    pos = PAST_LEN + jnp.arange(T, dtype=jnp.int32)
    q = rope(q, pos)
    k = rope(k, pos)
    pool_z = multiscale_pool(pool_ctx, u, PAST_LEN, w_grp, pool_scale)
    k_all = jnp.concatenate([k_ctx, k], axis=1)
    v_all = jnp.concatenate([v_ctx, v], axis=1)
    kpos = PAST_LEN - wb + jnp.arange(wb + T, dtype=jnp.int32)
    diff = pos[:, None] - kpos[None, :]
    mask = ((diff >= 0) & (diff <= WINDOW) & (kpos[None, :] >= 0))[None]
    qb = q.reshape(Bd, 1, T, N_KV_HEADS, GROUP, HEAD_DIM)
    attn = sink_attention(qb, k_all[:, None], v_all[:, None], mask, sinks.reshape(N_KV_HEADS, GROUP))
    attn_o = attn.reshape(Bd, T, Q_WIDTH)
    m = merge_out(pool_z, attn_o, gates, w_pool_out, w_attn_out, w_out)
    u_all = jnp.concatenate([pool_ctx, u], axis=1)
    return m, u_all[:, u_all.shape[1] - POOL_BUF:], k_all[:, T:], v_all[:, T:]

def setup_inputs(seed: int = 0) -> dict:
    key = jax.random.key(seed)
    ks = jax.random.split(key, 32)
    f32 = jnp.float32
    wb = min(WINDOW, PAST_LEN)

    def nrm(k, shape, scale):
        return jax.random.normal(k, shape, f32) * scale

    L = DEPTH
    return {
        "x_prompt": nrm(ks[0], (BATCH, SEQ, D_MODEL), 1.0),
        "x_sample": nrm(ks[1], (DEC_BATCH, DEC_SEQ, D_MODEL), 1.0),
        "cache_pool_u": nrm(ks[2], (L, DEC_BATCH, POOL_BUF, POOL_WIDTH), 1.0),
        "cache_k_win": nrm(ks[3], (L, DEC_BATCH, wb, N_KV_HEADS, HEAD_DIM), 1.0),
        "cache_v_win": nrm(ks[4], (L, DEC_BATCH, wb, N_KV_HEADS, HEAD_DIM), 1.0),
        "w_in": nrm(ks[5], (L, D_MODEL, IN_WIDTH), D_MODEL ** -0.5),
        "pool_w_grp": nrm(ks[6], (L, N_POOL_GROUPS, POOL_GROUP, POOL_GROUP), POOL_GROUP ** -0.5),
        "pool_scale": 1.0 + nrm(ks[7], (L, POOL_WIDTH), 0.1),
        "attn_sinks": nrm(ks[8], (L, N_HEADS), 0.5),
        "w_pool_out": nrm(ks[9], (L, POOL_WIDTH, D_MODEL), POOL_WIDTH ** -0.5),
        "w_attn_out": nrm(ks[10], (L, Q_WIDTH, D_MODEL), Q_WIDTH ** -0.5),
        "w_out": nrm(ks[11], (L, D_MODEL, D_MODEL), BETA * D_MODEL ** -0.5),
        "ffn1_w1": nrm(ks[12], (L, D_MODEL, D_FF), D_MODEL ** -0.5),
        "ffn1_w3": nrm(ks[13], (L, D_MODEL, D_FF), D_MODEL ** -0.5),
        "ffn1_w2": nrm(ks[14], (L, D_FF, D_MODEL), BETA * D_FF ** -0.5),
        "ffn2_w1": nrm(ks[15], (L, D_MODEL, D_FF), D_MODEL ** -0.5),
        "ffn2_w3": nrm(ks[16], (L, D_MODEL, D_FF), D_MODEL ** -0.5),
        "ffn2_w2": nrm(ks[17], (L, D_FF, D_MODEL), BETA * D_FF ** -0.5),
        "ln1_g": 1.0 + nrm(ks[18], (L, D_MODEL), 0.02),
        "ln1_b": nrm(ks[19], (L, D_MODEL), 0.02),
        "ln2_g": 1.0 + nrm(ks[20], (L, D_MODEL), 0.02),
        "ln2_b": nrm(ks[21], (L, D_MODEL), 0.02),
        "ln3_g": 1.0 + nrm(ks[22], (L, D_MODEL), 0.02),
        "ln3_b": nrm(ks[23], (L, D_MODEL), 0.02),
    }

def reference(x_prompt, x_sample, cache_pool_u, cache_k_win, cache_v_win,
              w_in, pool_w_grp, pool_scale, attn_sinks, w_pool_out, w_attn_out, w_out,
              ffn1_w1, ffn1_w3, ffn1_w2, ffn2_w1, ffn2_w3, ffn2_w2,
              ln1_g, ln1_b, ln2_g, ln2_b, ln3_g, ln3_b):
    xp, xs = x_prompt, x_sample
    pu_l, pk_l, pv_l, su_l, sk_l, sv_l = [], [], [], [], [], []
    for l in range(DEPTH):
        hp = ffn_half_step(xp, ffn1_w1[l], ffn1_w3[l], ffn1_w2[l], ln1_g[l], ln1_b[l])
        hs = ffn_half_step(xs, ffn1_w1[l], ffn1_w3[l], ffn1_w2[l], ln1_g[l], ln1_b[l])
        mp, pu, pk, pv = mixer_prompt(hp, w_in[l], pool_w_grp[l], pool_scale[l], attn_sinks[l],
                                      w_pool_out[l], w_attn_out[l], w_out[l])
        ms, su, sk, sv = mixer_sample(hs, cache_pool_u[l], cache_k_win[l], cache_v_win[l],
                                      w_in[l], pool_w_grp[l], pool_scale[l], attn_sinks[l],
                                      w_pool_out[l], w_attn_out[l], w_out[l])
        hp = layer_norm(ALPHA * hp + mp, ln2_g[l], ln2_b[l])
        hs = layer_norm(ALPHA * hs + ms, ln2_g[l], ln2_b[l])
        xp = ffn_half_step(hp, ffn2_w1[l], ffn2_w3[l], ffn2_w2[l], ln3_g[l], ln3_b[l])
        xs = ffn_half_step(hs, ffn2_w1[l], ffn2_w3[l], ffn2_w2[l], ln3_g[l], ln3_b[l])
        pu_l.append(pu); pk_l.append(pk); pv_l.append(pv)
        su_l.append(su); sk_l.append(sk); sv_l.append(sv)
    pool_u_prompt = jnp.stack(pu_l, axis=0)
    k_win_prompt = jnp.stack(pk_l, axis=0)
    v_win_prompt = jnp.stack(pv_l, axis=0)
    pool_u_sample = jnp.stack(su_l, axis=0)
    k_win_sample = jnp.stack(sk_l, axis=0)
    v_win_sample = jnp.stack(sv_l, axis=0)
    return (xp, xs, pool_u_prompt, k_win_prompt, v_win_prompt, pool_u_sample, k_win_sample, v_win_sample)


_drawn_inputs = setup_inputs


def setup_inputs(seed=0):
    import zlib

    import numpy as np

    out = dict(_drawn_inputs(seed))
    spreads = {}
    factors = {'attn_sinks': 48.981,
     'ln1_g': 2.865,
     'ln1_b': 2.783,
     'ln2_g': 7.78,
     'ln2_b': 16.409,
     'ln3_g': 22.589,
     'ln3_b': 23.235}
    for name, (base, spread) in spreads.items():
        noise = np.random.default_rng([zlib.crc32(name.encode()), seed]).standard_normal(out[name].shape)
        drawn = base * np.exp(spread * noise) if base else spread * noise
        out[name] = __import__('jax').numpy.asarray(drawn.astype(out[name].dtype))
    for name, factor in factors.items():
        out[name] = (out[name] * factor).astype(out[name].dtype)
    return out
```

```python
from contextlib import ExitStack

import numpy as np

import concourse.bass as bass
from concourse import mybir

P = 128
D = 1024
KD = D // P
SEQ = 512
DB, DS = 8, 4
NS = DB * DS
T = SEQ + NS
C = T // 2
PAST = 2048
FF = 2816
KF = FF // P // 2
POOLW = 512
WINDOWS = (2, 4, 8, 16)
NG = len(WINDOWS)
BUF = 15
SEG = BUF + DS
LINE = BUF + SEQ + DB * SEG
H, KV, HD = 8, 2, 64
GQ = H // KV
WIN = 128
NBLK = SEQ // WIN
CTXK = DB * WIN
SKEYS = CTXK + NS
QOFF, KOFF = POOLW, POOLW + H * HD
VOFF, GOFF = KOFF + KV * HD, KOFF + 2 * KV * HD
ALPHA = 2.0 ** 0.25
EPS = 1e-5
THETA = 10000.0
NEG = -1e30

SLOTS = 4
RAWS = 2
LAG = 2
UP, DOWN = 2 * KF, KD
MIX1 = 42
FFN_UNITS = 2 * (UP + DOWN)
MIX_BASE = FFN_UNITS
WO_BASE = MIX_BASE + MIX1
FFN2_BASE = WO_BASE + KD
UNITS = FFN2_BASE + FFN_UNITS

F32 = mybir.dt.float32
F32R = mybir.dt.float32r
ALU = mybir.AluOpType
ACT = mybir.ActivationFunctionType
AX = mybir.AxisListType

U_V, U_K, U_Q, U_GA, U_GB = 4, 5, 6, 10, 26
TOK_TILES = [(0, 128, 0), (128, 128, 0), (256, 16, 0), (272, 128, 1), (400, 112, 1), (512, 32, 1)]
STAGES = {3: ["poolctx", "kctx"], 6: ["uout"], 8: ["grp0", "grp1"], 9: ["vkout"], 11: ["S0"], 14: ["S1"], 15: ["T0"],
          16: ["PV0"], 17: ["S2"], 18: ["T1"], 19: ["PV1"], 20: ["S3"], 21: ["T2"], 22: ["PV2"],
          23: ["Sa", "Sb"], 24: ["T3"], 25: ["PV3"], 26: ["Ta", "Tb"], 28: ["PVs"]}
ROUNDS = [name for step in sorted(STAGES) for name in STAGES[step]]
READS = {"poolctx": NG, "kctx": 2, "uout": 2, "grp0": 4, "grp1": 4, "vkout": 4, "Sa": 3, "Sb": 3, "Ta": 3, "Tb": 3,
         "T0": 2, "PVs": 1}
READS |= {f"S{n}": 4 for n in range(NBLK)} | {f"T{n}": 4 for n in range(1, NBLK)} | {f"PV{n}": 1 for n in range(NBLK)}


def freed(name):
    return sum(READS[r] for r in ROUNDS[:ROUNDS.index(name) + 1])


def freed_before(name):
    return freed(name) - READS[name]


def written(name):
    return ROUNDS.index(name) + 1



def program(nc, a, out):
    ctx = ExitStack()
    with ctx:
        def sb(name, shape, dt=F32, where=None):
            return (where or ctx).enter_context(nc.sbuf_tensor(name, shape, dt))

        def sem(name):
            return ctx.enter_context(nc.semaphore(name))

        act_hi = sb("act_hi", [P, KD, T], F32R)
        act_lo = sb("act_lo", [P, KD, T], F32R)
        y = sb("y", [P, KD, T])
        ring_hi = sb("ring_hi", [P, SLOTS, KD, P], F32R)
        ring_lo = sb("ring_lo", [P, SLOTS, KD, P], F32R)
        raw = sb("raw", [P, RAWS, KD, P])
        cos_sin = sb("cos_sin", [P, 2, T])
        band = sb("band", [P, 2 * WIN])
        smask = sb("smask", [P, SKEYS])
        ident = sb("ident", [P, P])
        mean_w = sb("mean_w", [P, P + 1])
        inv_cnt = sb("inv_cnt", [P, NG, max(WINDOWS)])
        ln_gb = sb("ln_gb", [P, 6, KD])
        pscale = sb("pscale", [P, NG])
        sinks = sb("sinks", [P, H])
        sinks_s = sb("sinks_s", [P, KV])
        soft = sb("soft", [P, 2, 6, H])
        fsum = sb("fsum", [P, 2, C])
        rstd = sb("rstd", [P, C])
        p0 = sb("p0", [P, KD * C])
        tmp_a = sb("tmp_a", [P, 2, C])
        tmp_v = sb("tmp_v", [P, 2, C])
        tmp_r = sb("tmp_r", [P, C])
        sq = p0[:, :].rearrange("p (o t) -> p o t", o=KD)
        MAX, NEG_MAX, SINK, SUM, DEN, REC = range(6)

        with ExitStack() as ffn_mem:
            ext_hi = sb("ext_hi", [P, SLOTS, KF - KD, P], F32R, ffn_mem)
            ext_lo = sb("ext_lo", [P, SLOTS, KF - KD, P], F32R, ffn_mem)
            ext_raw = sb("ext_raw", [P, RAWS, KF - KD, P], F32, ffn_mem)
            hid_hi = sb("hid_hi", [P, KF, T], F32R, ffn_mem)
            hid_lo = sb("hid_lo", [P, KF, T], F32R, ffn_mem)
            xin = sb("xin", [P, len(TOK_TILES), D], F32, ffn_mem)
        with ExitStack() as mix_mem:
            m1 = sb("m1", [P, KD, T], F32, mix_mem)
            att_lo = sb("att_lo", [P, GQ, T], F32R, mix_mem)
            with ExitStack() as q_mem:
                qT = sb("qT", [P, GQ, T], F32, q_mem)
            att_hi = sb("att_hi", [P, GQ, T], F32R, mix_mem)
            with ExitStack() as branch_mem:
                pz_hi = sb("pz_hi", [P, NG, T], F32R, branch_mem)
                pz_lo = sb("pz_lo", [P, NG, T], F32R, branch_mem)
                p1 = sb("p1", [P, H * 2 * WIN], F32, branch_mem)
                with ExitStack() as line_mem:
                    line = sb("line", [P, NG, LINE], F32, line_mem)
                pT = sb("pT", [P, 4 * LINE], F32, branch_mem)
                kT = sb("kT", [P, T], F32, branch_mem)
                vT = sb("vT", [P, T], F32, branch_mem)
                vN = sb("vN", [P, NBLK + 1, P], F32, branch_mem)
                kctxT = sb("kctxT", [P, CTXK], F32, branch_mem)
                vctx = sb("vctx", [P, DB, P], F32, branch_mem)
                grp_w = sb("grp_w", [P, NG, P], F32, branch_mem)
                u_new = sb("u_new", [P, NG, NS], F32, branch_mem)
                q_new = sb("q_new", [P, GQ * NS], F32, branch_mem)
            m_hi = sb("m_hi", [P, KD, T], F32R, mix_mem)
            m_lo = sb("m_lo", [P, KD, T], F32R, mix_mem)
        kctx = [m1[:, i, 0:4 * WIN].rearrange("p (b n) -> p b n", n=P) for i in range(2)]
        rows_k = p0[:, 2 * POOLW:2 * POOLW + 2 * P].rearrange("p (a n) -> p a n", a=2)
        uctx = p1[:, 0:POOLW]
        rows_u = p0[:, 0:2 * POOLW].rearrange("p (a n) -> p a n", a=2)
        psum = ctx.enter_context(nc.psum_tensor("psum", [P, 8, 512], F32))

        ident_in = sem("ident_in")
        consts_in = sem("consts_in")
        x_in = [sem(f"x_in{i}") for i in range(len(TOK_TILES))]
        raw_in = [sem(f"raw_in{i}") for i in range(RAWS)]
        mixer_in = sem("mixer_in")
        hi_done = sem("hi_done")
        lo_done = sem("lo_done")
        mm_done = [sem(f"mm_done{c}") for c in range(2)]
        evac = [sem(f"evac{c}") for c in range(2)]
        hid_hi_done = [sem(f"hid_hi_done{c}") for c in range(2)]
        hid_done = [sem(f"hid_done{c}") for c in range(2)]
        y_done = [sem(f"y_done{c}") for c in range(2)]
        fsum_step = sem("fsum_step")
        fsum_done = [sem(f"fsum_done{c}") for c in range(2)]
        mean_done = [sem(f"mean_done{c}") for c in range(2)]
        cent_done = sem("cent_done")
        sq_done = sem("sq_done")
        sqsum_done = sem("sqsum_done")
        var_done = sem("var_done")
        std_done = sem("std_done")
        norm_done = sem("norm_done")
        aff_done = sem("aff_done")
        act_ready = [sem(f"act_ready{c}") for c in range(2)]
        turn_done = sem("turn_done")
        turn_read = sem("turn_read")
        v_step = sem("v_step")
        win_step = sem("win_step")
        win_done = sem("win_done")
        win_read = sem("win_read")
        q_new_done = sem("q_new_done")
        z_done = sem("z_done")
        poolz_done = sem("poolz_done")
        m_done = [sem(f"m_done{c}") for c in range(2)]
        att_mm = sem("att_mm")
        att_free = sem("att_free")
        neg_done = sem("neg_done")
        exp_done = sem("exp_done")
        prob_done = sem("prob_done")
        yout_done = sem("yout_done")
        side_stored = sem("side_stored")
        stored = sem("stored")

        block = ctx.enter_context(nc.Block())

        def tok(c):
            return slice(c * C, c * C + C)

        def unit_kind(u):
            for base in (0, FFN2_BASE):
                if base <= u < base + FFN_UNITS:
                    return KD if (u - base) % (UP + DOWN) < UP else KF
            m = u - MIX_BASE
            return NG if U_GA <= m < MIX1 and (m - U_GA) % 2 == 1 else KD

        def bank_of(u, c):
            if MIX_BASE <= u < FFN2_BASE:
                return 2 * c + u % 2
            return 4 * c + u % 4

        def stat_bank(l, c):
            return 7 if c else (0, 4, 0)[l]

        def y_before(l):
            return (DOWN, 2 * DOWN, 4 * DOWN)[l]

        @block.sync
        def _(sp):
            def w_tiles(w, k0, kn):
                return w[0, k0 * P:(k0 + kn) * P, :].rearrange("(k p) n -> p k n", p=P)

            def load(slot, src, kn, cols):
                first = kn // 2 if kn <= KD else KD
                sp.dma_start(raw[:, slot, 0:first, :], src[:, 0:first, cols]).then_inc(raw_in[slot], 16)
                dst = raw[:, slot, first:kn, :] if kn <= KD else ext_raw[:, slot, :, :]
                sp.dma_start(dst, src[:, first:kn, cols]).then_inc(raw_in[slot], 16)

            def raw_free(u):
                sp.wait_ge(lo_done, u - (RAWS - 1))

            def ffn_loads(base, w1, w3, w2):
                w1k, w3k = w_tiles(w1, 0, KD), w_tiles(w3, 0, KD)
                for half in range(2):
                    b, c0 = base + half * (UP + DOWN), half * KF * P
                    for n, w in enumerate((w1k, w3k)):
                        if b + n >= RAWS:
                            raw_free(b + n)
                        load(n, w, KD, slice(c0, c0 + P))
                    with sp.Fori(1, KF) as f:
                        for n, w in enumerate((w1k, w3k)):
                            raw_free(f * 2 + (b + n))
                            load(n, w, KD, bass.ds(f * P + c0, P))
                    w2k = w_tiles(w2, half * KF, KF)
                    with sp.Fori(0, DOWN // 2) as o:
                        for n in range(2):
                            raw_free(o * 2 + (b + UP + n))
                            load(n, w2k, KF, bass.ds(o * (2 * P) + n * P, P))

            for i, (t0, n, _) in enumerate(TOK_TILES):
                src = a["x_prompt"][0, t0:t0 + n, :] if t0 < SEQ else a["x_sample"].rearrange("b t d -> (b t) d")
                sp.dma_start(xin[0:n, i, :], src).then_inc(x_in[i], 16)
                if i == 0:
                    sp.dma_start(ident[:, :], a["c_ident"]).then_inc(ident_in, 16)
            ffn_loads(0, a["ffn1_w1"], a["ffn1_w3"], a["ffn1_w2"])

            win_k = w_tiles(a["w_in"], 0, KD)
            wpo_k = w_tiles(a["w_pool_out"], 0, NG)
            wo_k = w_tiles(a["w_out"], 0, KD)
            first_cols = [g * P for g in range(NG)] + [VOFF, KOFF]
            for m in range(MIX1):
                u = MIX_BASE + m
                slot = u % RAWS
                raw_free(u)
                o = (m - (U_GB if m >= U_GB else U_GA)) // 2
                if m < U_Q:
                    load(slot, win_k, KD, slice(first_cols[m], first_cols[m] + P))
                elif m < U_GA:
                    for kv in range(KV):
                        c0 = QOFF + kv * GQ * HD + (m - U_Q) * HD
                        sp.dma_start(raw[:, slot, :, kv * HD:(kv + 1) * HD],
                                     win_k[:, :, c0:c0 + HD]).then_inc(raw_in[slot], 16)
                elif (m - U_GA) % 2 == 0:
                    c0 = GOFF + (m >= U_GB) * D + o * P
                    load(slot, win_k, KD, slice(c0, c0 + P))
                elif m < U_GB:
                    load(slot, wpo_k, NG, slice(o * P, o * P + P))
                else:
                    for kv in range(KV):
                        src = a["w_attn_out"][0, kv * GQ * HD:(kv + 1) * GQ * HD, o * P:o * P + P]
                        sp.dma_start(raw[kv * HD:(kv + 1) * HD, slot, 0:GQ, :],
                                     src.rearrange("(j d) n -> d j n", d=HD)).then_inc(raw_in[slot], 16)
            for o in range(KD):
                raw_free(WO_BASE + o)
                load((WO_BASE + o) % RAWS, wo_k, KD, slice(o * P, o * P + P))
            ffn_loads(FFN2_BASE, a["ffn2_w1"], a["ffn2_w3"], a["ffn2_w2"])

            for i, (t0, n, _) in enumerate(TOK_TILES):
                sp.wait_ge(yout_done, 2 * i + 2)
                dst = out["y_prompt"][0, t0:t0 + n, :] if t0 < SEQ else out["y_sample"].rearrange("b t d -> (b t) d")
                sp.dma_start(dst, xin[0:n, i, :]).then_inc(stored, 16)
            sp.wait_ge(stored, 16 * len(TOK_TILES))
            sp.wait_ge(side_stored, 16 * SIDE_STORES)

        @block.gpsimd
        def _(pool):
            loads = [(mean_w[:, :], a["c_mean"]), (cos_sin[:, :, :], a["c_cos_sin"]), (band[:, :], a["c_band"]),
                     (smask[:, :], a["c_smask"]), (inv_cnt[:, :, :], a["c_inv_cnt"]),
                     (pscale[:, :], a["pool_scale"][0].rearrange("(g p) -> p g", p=P)),
                     (sinks[:, :], a["attn_sinks"][0:1, :].broadcast_to([P, H]))]
            for j in range(GQ):
                src = a["attn_sinks"][0:1, :].rearrange("a (k j) -> a j k", j=GQ)[:, j, :]
                loads.append((sinks_s[j * NS:(j + 1) * NS, :], src.broadcast_to([NS, KV])))
            for i, name in enumerate(("ln1_g", "ln1_b", "ln2_g", "ln2_b", "ln3_g", "ln3_b")):
                loads.append((ln_gb[:, i, :], a[name][0].rearrange("(k p) -> p k", p=P)))
            assert len(loads) == CONST_DMAS
            for dst, src in loads:
                pool.dma_start(dst, src, allow_slow_non_contiguous=True).then_inc(consts_in, 16)

            def feature_sum(l, c):
                for o in range(1, KD):
                    pool.wait_ge(y_done[c], y_before(l) + o + 1)
                    if o == 1:
                        first = y[:, 0, tok(c)]
                        if l:
                            pool.wait_ge(mean_done[c], l)
                    else:
                        first = fsum[:, c, :]
                        pool.wait_ge(fsum_step, (2 * l + c) * (KD - 2) + o - 1)
                    ins = pool.tensor_tensor(fsum[:, c, :], first, y[:, o, tok(c)], ALU.add)
                    ins.then_inc(fsum_step if o < KD - 1 else fsum_done[c], 1)

            feature_sum(0, 0)
            feature_sum(0, 1)

            pool.wait_ge(mm_done[0], FFN_UNITS)
            pool.wait_ge(mm_done[1], FFN_UNITS)
            pool.memset(line[:, :, 0:BUF], 0.0).then_inc(win_step, 1)
            pool.dma_start(uctx[0:DB * BUF, :], a["cache_pool_u"][0].rearrange("b t w -> (b t) w")) \
                .then_inc(mixer_in, 16)
            for i in range(2):
                pool.dma_start(kctx[i], a["cache_k_win"][0, 4 * i:4 * i + 4].rearrange("b t h d -> t b (h d)")) \
                    .then_inc(mixer_in, 16)
            pool.dma_start(vctx[:, :, :], a["cache_v_win"][0].rearrange("b t h d -> t b (h d)")).then_inc(mixer_in, 16)
            pool.dma_start(grp_w[:, :, :], a["pool_w_grp"][0].rearrange("g c d -> c g d")).then_inc(mixer_in, 16)
            for name, src, n in (("k_win_sample", "cache_k_win", WIN), ("v_win_sample", "cache_v_win", WIN),
                                 ("pool_u_sample", "cache_pool_u", BUF)):
                pool.dma_start(out[name][0, :, 0:n - DS], a[src][0, :, DS:n]).then_inc(side_stored, 16)

            sums = [p1[:, i * LINE:(i + 1) * LINE] for i in range(3)]
            pool.wait_ge(evac[0], MIX_BASE + NG)
            pool.wait_ge(evac[1], MIX_BASE + NG)
            pool.wait_ge(att_free, freed("poolctx"))
            steps = 1
            pool.wait_ge(win_step, steps)
            for g in range(NG):
                if g:
                    pool.wait_ge(win_done, g)
                src = line[:, g, :]
                for i in range(g + 1):
                    sh = 1 << i
                    lo = 2 * sh - 1
                    if i:
                        pool.wait_ge(win_step, steps)
                    if i == g and g:
                        pool.wait_ge(win_read, g)
                    dst = sums[2] if i == g else sums[i % 2]
                    ins = pool.tensor_tensor(dst[:, lo:LINE], src[:, lo:LINE], src[:, lo - sh:LINE - sh], ALU.add)
                    ins.then_inc(win_done if i == g else win_step, 1)
                    steps += i < g
                    src = dst

            pool.wait_ge(att_free, freed("uout"))
            pool.dma_start(out["pool_u_prompt"][0, 0], rows_u[0:BUF, 0, :]).then_inc(side_stored, 16)
            for b in range(DB):
                pool.dma_start(out["pool_u_sample"][0, b, BUF - DS:BUF], rows_u[b * DS:(b + 1) * DS, 1, :]) \
                    .then_inc(side_stored, 16)
            pool.wait_ge(att_free, freed("vkout"))
            for name, row in (("k_win_prompt", rows_k[:, 0, :]), ("v_win_prompt", vN[:, NBLK - 1, :])):
                pool.dma_start(out[name][0, 0].rearrange("t h d -> t (h d)"), row).then_inc(side_stored, 16)
            for name, row in (("k_win_sample", rows_k[0:NS, 1, :]), ("v_win_sample", vN[0:NS, NBLK, :])):
                for b in range(DB):
                    pool.dma_start(out[name][0, b, WIN - DS:WIN].rearrange("t h d -> t (h d)"),
                                   row[b * DS:(b + 1) * DS]).then_inc(side_stored, 16)

            for l in (1, 2):
                feature_sum(l, 0)
                feature_sum(l, 1)

        @block.scalar
        def _(act):
            def split(u, kn, at=None):
                s, r = (u if at is None else at) % SLOTS, (u if at is None else at) % RAWS
                act.wait_ge(raw_in[r], u * (32 // RAWS) + (32 - r * (32 // RAWS)))
                if at is not None or u >= SLOTS:
                    act.wait_ge(mm_done[1], u - (SLOTS - 1))
                n = min(kn, KD)
                ins = act.activation(ring_hi[:, s, 0:n, :], raw[:, r, 0:n, :], ACT.Copy)
                if kn > KD:
                    ins = act.activation(ext_hi[:, s, :, :], ext_raw[:, r, :, :], ACT.Copy)
                ins.then_inc(hi_done, 1)

            def norm_squares(l, c):
                for i in range(2):
                    act.wait_ge(cent_done, 4 * l + 2 * c + i + 1)
                    act.activation(sq[:, 4 * i:4 * i + 4, :], y[:, 4 * i:4 * i + 4, tok(c)], ACT.Square) \
                        .then_inc(sq_done, 1)

            def norm_affine(l, c):
                act.wait_ge(var_done, 2 * l + c + 1)
                act.activation(rstd[:, :], psum[:, stat_bank(l, c), 0:C], ACT.Sqrt, bias=mean_w[:, P:P + 1]) \
                    .then_inc(std_done, 1)
                for o in range(KD):
                    act.wait_ge(norm_done, 4 * l + 2 * c + o // 4 + 1)
                    act.activation(y[:, o, tok(c)], y[:, o, tok(c)], ACT.Identity, bias=ln_gb[:, 2 * l + 1, o:o + 1],
                                   scale=ln_gb[:, 2 * l, o:o + 1]).then_inc(aff_done, 1)

            def through(u, c, func, at=None, scale=1.0):
                act.wait_ge(mm_done[c], u + 1)
                act.wait_ge(evac[c], u)
                act.activation(tmp_a[:, c, :], psum[:, bank_of(u if at is None else at, c), 0:C], func, scale=scale) \
                    .then_inc(evac[c], 1)

            def residual(u, c, n, scale):
                if n:
                    act.wait_ge(y_done[c], n)
                through(u, c, ACT.Copy, scale=scale)

            def ffn(l, base, y_n):
                for half in range(2):
                    b = base + half * (UP + DOWN)

                    def up_step(s, u, kn):
                        if s % 2 == 0 and s < UP:
                            through(u, 0, ACT.Silu, at=b + s)
                        if s % 2 == 0 and s >= LAG:
                            through(u - LAG, 1, ACT.Silu, at=b + s - LAG)
                        if kn:
                            split(u + 2, kn, at=b + s + 2)

                    if y_n:
                        act.wait_ge(y_done[0], y_n)
                        act.wait_ge(y_done[1], y_n)
                    up_step(0, b, 0)
                    if l == 2 and half == 0:
                        norm_affine(1, 1)
                    with act.Fori(0, 4) as i:
                        for j in range(4):
                            up_step(2 + j, i * 4 + (b + 2 + j), KD)
                    for s in range(18, UP + LAG):
                        up_step(s, b + s, unit_kind(b + s + 2))
                    b += UP
                    for s in range(DOWN + LAG):
                        if s < DOWN:
                            residual(b + s, 0, y_n + s, 0.5)
                        if s >= LAG:
                            residual(b + s - LAG, 1, y_n + s - LAG, 0.5)
                            if b + s + 2 < UNITS:
                                split(b + s + 2, unit_kind(b + s + 2))
                        if half == 1 and s == DOWN - 1:
                            norm_squares(l, 0)
                        if half == 1 and s == DOWN:
                            norm_affine(l, 0)
                    y_n += DOWN

            act.wait_ge(consts_in, 16 * CONST_DMAS)
            for i, (t0, n, _) in enumerate(TOK_TILES):
                act.wait_ge(turn_done, i + 1)
                for h in range(2):
                    ins = act.activation(y[:, 4 * h:4 * h + 4, t0:t0 + n],
                                         psum[:, 2 * (i % 4) + h, 0:4 * n].rearrange("p (o t) -> p o t", o=4), ACT.Copy)
                ins.then_inc(turn_read, 1)
                if i in (2, 3, 4, 5):
                    split(i - 2, KD)
            ffn(0, 0, 0)
            norm_squares(0, 1)

            def epilogue(m, c):
                u = MIX_BASE + m
                bank = bank_of(u, c)
                if m < U_V:
                    act.wait_ge(mm_done[c], u + 1)
                    act.wait_ge(evac[c], u)
                    n = C if c == 0 else SEQ - C
                    ins = act.activation(line[:, m, BUF + c * C:BUF + c * C + n], psum[:, bank, 0:n], ACT.Copy)
                    if c == 1:
                        seg = line[:, m, BUF + SEQ:LINE].rearrange("p (b s) -> p b s", s=SEG)[:, :, BUF:SEG]
                        act.activation(seg, psum[:, bank, n:C].rearrange("p (b s) -> p b s", s=DS), ACT.Copy)
                        ins = act.activation(u_new[:, m, :], psum[:, bank, n:C], ACT.Copy)
                    ins.then_inc(evac[c], 1)
                elif m == U_V:
                    act.wait_ge(mm_done[c], u + 1)
                    act.wait_ge(evac[c], u)
                    act.activation(vT[:, tok(c)], psum[:, bank, 0:C], ACT.Copy).then_inc(evac[c], 1)
                elif m >= U_GA and (m - U_GA) % 2 == 0:
                    through(u, c, ACT.Sigmoid)

            def copy_out(dst, src):
                act.activation(dst, src, ACT.Copy).then_inc(att_free, 1)

            def att_copies(name):
                act.wait_ge(att_mm, written(name))
                if name == "poolctx":
                    segs = line[:, :, BUF + SEQ:LINE].rearrange("p g (b s) -> p g b s", s=SEG)
                    for g in range(NG):
                        copy_out(segs[:, g, :, 0:BUF],
                                 psum[:, 4, g * P:g * P + DB * BUF].rearrange("p (b s) -> p b s", s=BUF))
                elif name == "kctx":
                    for h in range(2):
                        copy_out(kctxT[:, 512 * h:512 * h + 512], psum[:, 5 + h, :])
                elif name == "uout":
                    copy_out(rows_u[0:BUF, 0, :], psum[0:BUF, 4, :])
                    copy_out(rows_u[0:NS, 1, :], psum[0:NS, 5, :])
                elif name == "vkout":
                    copy_out(vN[:, 0:NBLK, :], psum[:, 4, :].rearrange("p (n d) -> p n d", d=P))
                    copy_out(vN[0:NS, NBLK, :], psum[0:NS, 5, 0:P])
                    copy_out(rows_k[:, 0, :], psum[:, 6, 0:P])
                    copy_out(rows_k[0:NS, 1, :], psum[0:NS, 7, 0:P])
                elif name in ("Ta", "Tb"):
                    k0 = (name == "Tb") * (DB + 1) * P
                    for h in range(2):
                        copy_out(pT[:, k0 + 512 * h:k0 + 512 * h + 512], psum[:, 4 + h, :])
                    copy_out(pT[0:NS, k0 + CTXK:k0 + CTXK + P], psum[0:NS, 6, 0:P])
                elif name[0] == "T":
                    for b in range(2 if name == "T0" else 0, 4):
                        copy_out(pT[:, b * 512:(b + 1) * 512], psum[:, 4 + b, :])

            def exps(i):
                act.wait_ge(neg_done, i + 1)
                st = soft[:, i % 2]
                if i == NBLK:
                    parts = [(p0[:, kv * SKEYS:(kv + 1) * SKEYS], kv) for kv in range(KV)]
                else:
                    pb = (p0, p1)[i % 2][:, 0:H * 2 * WIN].rearrange("p (h k) -> p h k", h=H)
                    parts = [(pb[:, h, (WIN if i == 0 else 0):2 * WIN], h) for h in range(H)]
                for part, h in parts:
                    act.activation(part, part, ACT.Exp, bias=st[:, NEG_MAX, h:h + 1], accum_out=st[:, SUM, h:h + 1])
                act.activation(st[:, SINK, 0:len(parts)], st[:, SINK, 0:len(parts)], ACT.Exp).then_inc(exp_done, 1)

            for s in range(MIX1 + LAG):
                if s < MIX1:
                    epilogue(s, 0)
                if s == 0:
                    norm_affine(0, 1)
                if s >= LAG:
                    epilogue(s - LAG, 1)
                    split(MIX_BASE + s + 2, unit_kind(MIX_BASE + s + 2))
                for name in STAGES.get(s, []):
                    if name in ("poolctx", "kctx", "uout", "vkout") or name[0] == "T":
                        att_copies(name)
                    if name in EXP_AFTER:
                        exps(EXP_AFTER.index(name))
            for s in range(KD + LAG):
                if s < KD:
                    residual(WO_BASE + s, 0, y_before(1) + s, 1.0)
                if s >= LAG:
                    residual(WO_BASE + s - LAG, 1, y_before(1) + s - LAG, 1.0)
                    split(WO_BASE + s + 2, unit_kind(WO_BASE + s + 2))
                if s == KD - 1:
                    norm_squares(1, 0)
                if s == KD:
                    norm_affine(1, 0)
            norm_squares(1, 1)
            ffn(2, FFN2_BASE, 3 * DOWN)
            norm_squares(2, 1)
            for i, (t0, n, c) in enumerate(TOK_TILES):
                if i == 3:
                    norm_affine(2, 1)
                act.wait_ge(turn_done, len(TOK_TILES) + i + 1)
                for h in range(2):
                    act.activation(xin[0:n, i, 512 * h:512 * h + 512], psum[0:n, out_bank(i) + h, :], ACT.Copy) \
                        .then_inc(yout_done, 1)

        @block.vector
        def _(dve):
            steps = [0]

            def step(ins):
                ins.then_inc(v_step, 1)
                steps[0] += 1
                dve.wait_ge(v_step, steps[0])

            def split(u, kn, at=None):
                s, r = (u if at is None else at) % SLOTS, (u if at is None else at) % RAWS
                dve.wait_ge(hi_done, u + 1)
                n = min(kn, KD)
                ins = dve.tensor_tensor(ring_lo[:, s, 0:n, :], raw[:, r, 0:n, :], ring_hi[:, s, 0:n, :], ALU.subtract)
                if kn > KD:
                    ins = dve.tensor_tensor(ext_lo[:, s, :, :], ext_raw[:, r, :, :], ext_hi[:, s, :, :], ALU.subtract)
                ins.then_inc(lo_done, 1)

            def hidden(u, c, n, f, at):
                dve.wait_ge(mm_done[c], u + 1)
                dve.wait_ge(evac[c], u)
                if not isinstance(n, int) or n:
                    dve.wait_ge(hid_done[c], n)
                dve.tensor_tensor(tmp_v[:, c, :], psum[:, bank_of(at, c), 0:C], tmp_a[:, c, :], ALU.mult) \
                    .then_inc(evac[c], 1)
                dve.wait_ge(evac[c], u + 1)
                hi = hid_hi[:, f, tok(c)] if isinstance(f, int) else hid_hi[:, bass.ds(f, 1), tok(c)]
                lo = hid_lo[:, f, tok(c)] if isinstance(f, int) else hid_lo[:, bass.ds(f, 1), tok(c)]
                v = tmp_v[:, c, :] if isinstance(f, int) else tmp_v[:, c:c + 1, :]
                dve.tensor_copy(hi, v).then_inc(hid_hi_done[c], 1)
                dve.wait_ge(hid_hi_done[c], n + 1)
                dve.tensor_tensor(lo, v, hi, ALU.subtract).then_inc(hid_done[c], 1)

            def residual(u, c, o, factor):
                dve.wait_ge(evac[c], u + 1)
                dve.scalar_tensor_tensor(out=y[:, o, tok(c)], in0=y[:, o, tok(c)], scalar=factor,
                                         in1=tmp_a[:, c, :], op0=ALU.mult, op1=ALU.add).then_inc(y_done[c], 1)

            def norm_center(l, c):
                dve.wait_ge(mean_done[c], l + 1)
                mean = psum[:, stat_bank(l, c):stat_bank(l, c) + 1, 0:C].broadcast_to([P, 4, C])
                for i in range(2):
                    half = y[:, 4 * i:4 * i + 4, tok(c)]
                    dve.tensor_tensor(half, half, mean, ALU.subtract).then_inc(cent_done, 1)
                dve.wait_ge(sq_done, 4 * l + 2 * c + 2)
                step(dve.tensor_tensor(sq[:, 0:4, :], sq[:, 0:4, :], sq[:, 4:8, :], ALU.add))
                step(dve.tensor_tensor(sq[:, 0:2, :], sq[:, 0:2, :], sq[:, 2:4, :], ALU.add))
                dve.tensor_tensor(sq[:, 0, :], sq[:, 0, :], sq[:, 1, :], ALU.add).then_inc(sqsum_done, 1)

            def norm_scale(l, c):
                dve.wait_ge(std_done, 2 * l + c + 1)
                step(dve.reciprocal(rstd[:, :], rstd[:, :]))
                r = rstd[:, :].rearrange("p (a t) -> p a t", a=1).broadcast_to([P, 4, C])
                for i in range(2):
                    half = y[:, 4 * i:4 * i + 4, tok(c)]
                    dve.tensor_tensor(half, half, r, ALU.mult).then_inc(norm_done, 1)
                if l < 2:
                    split_act(l + 1, c)

            def split_act(l, c):
                for i in range(KD // 2):
                    if l:
                        dve.wait_ge(aff_done, KD * (2 * (l - 1) + c) + 2 * i + 2)
                    hi, v = act_hi[:, 2 * i:2 * i + 2, tok(c)], y[:, 2 * i:2 * i + 2, tok(c)]
                    step(dve.tensor_copy(hi, v))
                    dve.tensor_tensor(act_lo[:, 2 * i:2 * i + 2, tok(c)], v, hi, ALU.subtract).then_inc(act_ready[c], 1)

            def ffn(l, base, hid_n):
                for half in range(2):
                    b = base + half * (UP + DOWN)

                    def up_step(s, u, n, kn, f=None):
                        f = s // 2 if f is None else f
                        if s % 2 == 1 and s < UP:
                            hidden(u, 0, n, f, b + s)
                        if s % 2 == 1 and s >= LAG:
                            hidden(u - LAG, 1, n - 1, f - 1, b + s - LAG)
                        if kn:
                            split(u + 2, kn, at=b + s + 2)

                    if l == 2 and half == 0:
                        norm_scale(1, 1)
                    up_step(1, b + 1, hid_n, 0)
                    with dve.Fori(0, 4) as i:
                        for j in range(4):
                            s = 2 + j
                            up_step(s, i * 4 + (b + s), i * 2 + (hid_n + s // 2), KD, i * 2 + s // 2)
                    for s in range(18, UP + LAG):
                        up_step(s, b + s, hid_n + s // 2, unit_kind(b + s + 2))
                    hid_n += KF
                    b += UP
                    for s in range(DOWN + LAG):
                        if s < DOWN:
                            residual(b + s, 0, s, 1.0 if half else ALPHA)
                        if s >= LAG:
                            residual(b + s - LAG, 1, s - LAG, 1.0 if half else ALPHA)
                            if b + s + 2 < UNITS:
                                split(b + s + 2, unit_kind(b + s + 2))
                        if half == 1 and s == DOWN - 1:
                            norm_center(l, 0)
                        if half == 1 and s == DOWN:
                            norm_scale(l, 0)

            for c in range(2):
                if c:
                    for u in range(2):
                        split(u, KD)
                dve.wait_ge(turn_read, 3 * c + 3)
                split_act(0, c)
            for u in range(2, SLOTS):
                split(u, KD)
            ffn(0, 0, 0)
            norm_center(0, 1)

            def rotate(u, c, dst):
                dve.wait_ge(mm_done[c], u + 1)
                dve.wait_ge(evac[c], u)
                dve.wait_ge(evac[1 - c], u - LAG if c == 0 else u + LAG + 1)
                x = psum[:, bank_of(u, c), 0:C]
                step(dve.tensor_tensor(tmp_v[:, c, :], x, cos_sin[:, 0, tok(c)], ALU.mult))
                half = HD // 2
                for q in range(0, P, half):
                    to = q + half if q % HD == 0 else q - half
                    ins = dve.tensor_tensor(tmp_r[to:to + half, :], x[q:q + half, :],
                                            cos_sin[q:q + half, 1, tok(c)], ALU.mult)
                step(ins)
                dve.tensor_tensor(dst, tmp_v[:, c, :], tmp_r[:, :], ALU.add).then_inc(evac[c], 1)

            def epilogue(m, c):
                u = MIX_BASE + m
                if m == U_K:
                    rotate(u, c, kT[:, tok(c)])
                elif U_Q <= m < U_GA:
                    rotate(u, c, qT[:, m - U_Q, tok(c)])
                    if m == U_GA - 1 and c == 1:
                        dve.wait_ge(evac[1], u + 1)
                        dve.tensor_copy(q_new[:, :].rearrange("p (j t) -> p j t", j=GQ), qT[:, :, SEQ:T]) \
                            .then_inc(q_new_done, 1)
                elif m >= U_GA and (m - U_GA) % 2 == 1:
                    dve.wait_ge(mm_done[c], u + 1)
                    dve.wait_ge(evac[c], u)
                    prod = psum[:, bank_of(u, c), 0:C]
                    if m < U_GB:
                        dve.tensor_tensor(m1[:, (m - U_GA) // 2, tok(c)], prod, tmp_a[:, c, :], ALU.mult) \
                            .then_inc(evac[c], 1)
                        return
                    o = (m - U_GB) // 2
                    if o:
                        dve.wait_ge(m_done[c], o)
                    dve.tensor_tensor(tmp_v[:, c, :], prod, tmp_a[:, c, :], ALU.mult).then_inc(evac[c], 1)
                    dve.wait_ge(evac[c], u + 1)
                    step(dve.tensor_tensor(tmp_v[:, c, :], tmp_v[:, c, :], m1[:, o, tok(c)], ALU.add))
                    step(dve.tensor_copy(m_hi[:, o, tok(c)], tmp_v[:, c, :]))
                    dve.tensor_tensor(m_lo[:, o, tok(c)], tmp_v[:, c, :], m_hi[:, o, tok(c)], ALU.subtract) \
                        .then_inc(m_done[c], 1)

            def pooled():
                dve.wait_ge(att_mm, written("uout"))
                for g, w in enumerate(WINDOWS):
                    dve.wait_ge(win_done, g + 1)
                    total = p1[:, 2 * LINE:3 * LINE]
                    head = slice(BUF, BUF + max(WINDOWS))
                    tail = slice(BUF + max(WINDOWS), LINE)
                    if g:
                        dve.wait_ge(z_done, g)
                    step(dve.tensor_tensor(rstd[:, 0:max(WINDOWS)], total[:, head], inv_cnt[:, g, :], ALU.mult))
                    dve.tensor_tensor(line[:, g, head], rstd[:, 0:max(WINDOWS)], line[:, g, head], ALU.subtract) \
                        .then_inc(z_done, 1)
                    dve.scalar_tensor_tensor(out=line[:, g, tail], in0=total[:, tail], scalar=1.0 / w,
                                             in1=line[:, g, tail], op0=ALU.mult, op1=ALU.subtract) \
                        .then_inc(win_read, 1)

            def grouped(name):
                dve.wait_ge(att_mm, written(name))
                before = freed_before(name)
                for i in range(2):
                    g = 2 * (name == "grp1") + i
                    for c in range(2):
                        v = rstd[:, :]
                        if g or c:
                            dve.wait_ge(poolz_done, 2 * g + c)
                        dve.tensor_scalar(v, psum[:, 4 + 2 * i + c, 0:C], pscale[:, g:g + 1], None, ALU.mult) \
                            .then_inc(att_free, 1)
                        dve.wait_ge(att_free, before + 2 * i + c + 1)
                        step(dve.tensor_copy(pz_hi[:, g, tok(c)], v))
                        dve.tensor_tensor(pz_lo[:, g, tok(c)], v, pz_hi[:, g, tok(c)], ALU.subtract) \
                            .then_inc(poolz_done, 1)

            def scores(name):
                dve.wait_ge(att_mm, written(name))
                if name in ("Sa", "Sb"):
                    i, kv = NBLK, "ab".index(name[1])
                    if kv == 0:
                        dve.wait_ge(att_mm, written("T2"))
                    for n, (bank, k0, kn) in enumerate(((4, 0, 512), (5, 512, 512), (6, CTXK, NS))):
                        dve.scalar_tensor_tensor(out=p0[:, kv * SKEYS + k0:kv * SKEYS + k0 + kn],
                                                 in0=psum[:, bank, 0:kn], scalar=HD ** -0.5,
                                                 in1=smask[:, k0:k0 + kn], op0=ALU.mult, op1=ALU.add) \
                            .then_inc(att_free, 1)
                    if kv == 0:
                        return
                    pb, hn, sink = p0[:, 0:KV * SKEYS].rearrange("p (h k) -> p h k", h=KV), KV, sinks_s
                else:
                    i = int(name[1])
                    if i == 0:
                        dve.wait_ge(side_stored, 16 * SIDE_STORES)
                    k0 = WIN if i == 0 else 0
                    pb = (p0, p1)[i % 2][:, 0:H * 2 * WIN].rearrange("p (h k) -> p h k", h=H)[:, :, k0:2 * WIN]
                    hn, sink = H, sinks
                    mask = band[:, k0:2 * WIN].rearrange("p (a k) -> p a k", a=1).broadcast_to([P, 2, 2 * WIN - k0])
                    for b in range(4):
                        src = psum[:, 4 + b, :].rearrange("p (h k) -> p h k", h=2)[:, :, k0:2 * WIN]
                        dve.scalar_tensor_tensor(out=pb[:, 2 * b:2 * b + 2, :], in0=src, scalar=HD ** -0.5, in1=mask,
                                                 op0=ALU.mult, op1=ALU.add).then_inc(att_free, 1)
                dve.wait_ge(att_free, freed(name))
                st = soft[:, i % 2]
                step(dve.tensor_reduce(st[:, MAX, 0:hn], pb, AX.X, ALU.max))
                step(dve.tensor_tensor(st[:, MAX, 0:hn], st[:, MAX, 0:hn], sink[:, 0:hn], ALU.max))
                dve.tensor_scalar(st[:, NEG_MAX, 0:hn], st[:, MAX, 0:hn], -1.0, None, ALU.mult)
                dve.tensor_tensor(st[:, SINK, 0:hn], sink[:, 0:hn], st[:, MAX, 0:hn], ALU.subtract) \
                    .then_inc(neg_done, 1)

            def divide(i):
                dve.wait_ge(exp_done, i + 1)
                st = soft[:, i % 2]
                if i == NBLK:
                    pb, hn = p0[:, 0:KV * SKEYS].rearrange("p (h k) -> p h k", h=KV), KV
                else:
                    k0 = WIN if i == 0 else 0
                    pb = (p0, p1)[i % 2][:, 0:H * 2 * WIN].rearrange("p (h k) -> p h k", h=H)[:, :, k0:2 * WIN]
                    hn = H
                step(dve.tensor_tensor(st[:, DEN, 0:hn], st[:, SUM, 0:hn], st[:, SINK, 0:hn], ALU.add))
                step(dve.reciprocal(st[:, REC, 0:hn], st[:, DEN, 0:hn]))
                for h in range(hn):
                    ins = dve.tensor_scalar(pb[:, h, :], pb[:, h, :], st[:, REC, h:h + 1], None, ALU.mult)
                ins.then_inc(prob_done, 1)

            def attended(name):
                dve.wait_ge(att_mm, written(name))
                if name == "PVs":
                    t0, n = SEQ, NS
                else:
                    t0, n = int(name[2]) * WIN, WIN
                o = psum[:, 4, 0:GQ * n].rearrange("p (j t) -> p j t", j=GQ)
                step(dve.tensor_copy(att_hi[:, :, t0:t0 + n], o))
                dve.tensor_tensor(att_lo[:, :, t0:t0 + n], o, att_hi[:, :, t0:t0 + n], ALU.subtract) \
                    .then_inc(att_free, 1)

            for s in range(MIX1 + LAG):
                if s < MIX1:
                    epilogue(s, 0)
                if s == 0:
                    norm_scale(0, 1)
                if s >= LAG:
                    epilogue(s - LAG, 1)
                    split(MIX_BASE + s + 2, unit_kind(MIX_BASE + s + 2))
                for name in STAGES.get(s, []):
                    if name == "uout":
                        pooled()
                    elif name in ("grp0", "grp1"):
                        grouped(name)
                    elif name[0] == "S":
                        scores(name)
                    elif name[0:2] == "PV":
                        attended(name)
                for i, step_n in enumerate(DIVIDE_AT):
                    if step_n == s:
                        divide(i)
            for s in range(KD + LAG):
                if s < KD:
                    residual(WO_BASE + s, 0, s, ALPHA)
                if s >= LAG:
                    residual(WO_BASE + s - LAG, 1, s - LAG, ALPHA)
                    split(WO_BASE + s + 2, unit_kind(WO_BASE + s + 2))
                if s == KD - 1:
                    norm_center(1, 0)
                if s == KD:
                    norm_scale(1, 0)
            norm_center(1, 1)
            ffn(2, FFN2_BASE, 2 * KF)
            norm_center(2, 1)
            norm_scale(2, 1)

        @block.tensor
        def _(pe):
            def weights(s, k, hi):
                if k < KD:
                    return (ring_hi if hi else ring_lo)[:, s, k, :]
                return (ext_hi if hi else ext_lo)[:, s, k - KD, :]

            def part(u, c, kn, x_hi, x_lo, at=None, ready=None):
                s = (u if at is None else at) % SLOTS
                banks = 2 if MIX_BASE <= (u if at is None else at) < FFN2_BASE else 4
                bank = bank_of(u if at is None else at, c)
                pe.wait_ge(lo_done, u + 1)
                if at is not None or u >= banks:
                    pe.wait_ge(evac[c], u - (banks - 1))
                for k in range(kn):
                    if ready:
                        ready(k)
                    o = psum[:, bank, 0:C]
                    pe.matmul(o, weights(s, k, True), x_hi[:, k, tok(c)], start=k == 0, stop=False)
                    pe.matmul(o, weights(s, k, True), x_lo[:, k, tok(c)], start=False, stop=False)
                    ins = pe.matmul(o, weights(s, k, False), x_hi[:, k, tok(c)], start=False, stop=k == kn - 1)
                ins.then_inc(mm_done[c], 1)

            def act_wait(l, c):
                return lambda k: pe.wait_ge(act_ready[c], (KD // 2) * l + k // 2 + 1) if k % 2 == 0 else None

            def mean(l, c):
                pe.wait_ge(fsum_done[c], l + 1)
                pe.wait_ge(consts_in, 16 * CONST_DMAS)
                pe.wait_ge(evac[1], (FFN_UNITS - LAG if c == 0 else FFN_UNITS) if l == 0 else 0) if l == 0 else None
                pe.matmul(psum[:, stat_bank(l, c), 0:C], mean_w[:, 0:P], fsum[:, c, :], start=True, stop=True) \
                    .then_inc(mean_done[c], 1)

            def variance(l, c):
                pe.wait_ge(sqsum_done, 2 * l + c + 1)
                pe.matmul(psum[:, stat_bank(l, c), 0:C], mean_w[:, 0:P], sq[:, 0, :], start=True, stop=True) \
                    .then_inc(var_done, 1)

            def ffn(l, base, act_l, hid_n):
                for half in range(2):
                    b = base + half * (UP + DOWN)
                    fresh = half == 0

                    def up(s, u, c):
                        ready = act_wait(act_l, c) if isinstance(u, int) and u == base else None
                        part(u, c, KD, act_hi, act_lo, at=s, ready=ready)

                    def up_static(s, c):
                        part(b + s, c, KD, act_hi, act_lo, ready=act_wait(act_l, c) if fresh and s == 0 else None)

                    up_static(0, 0)
                    up_static(1, 0)
                    if l == 2 and half == 0:
                        variance(1, 1)
                    for s in range(LAG, LAG + 4):
                        up_static(s, 0)
                        up_static(s - LAG, 1)
                    with pe.Fori(0, 4) as i:
                        for j in range(4):
                            s = LAG + 4 + j
                            part(i * 4 + (b + s), 0, KD, act_hi, act_lo, at=b + s)
                            part(i * 4 + (b + s - LAG), 1, KD, act_hi, act_lo, at=b + s - LAG)
                    for s in range(UP, UP + LAG):
                        up_static(s - LAG, 1)
                    b += UP

                    def hid_wait(c):
                        return lambda k: pe.wait_ge(hid_done[c], hid_n + k + 1)

                    for s in range(DOWN + LAG):
                        if s < DOWN:
                            part(b + s, 0, KF, hid_hi, hid_lo, ready=hid_wait(0) if s == 0 else None)
                        if s >= LAG:
                            part(b + s - LAG, 1, KF, hid_hi, hid_lo, ready=hid_wait(1) if s == LAG else None)
                        if half == 1 and s == DOWN - 1:
                            mean(l, 0)
                        if half == 1 and s == DOWN:
                            variance(l, 0)
                    hid_n += KF
                mean(l, 1)

            def turn_in(i, t0, n):
                pe.wait_ge(x_in[i], 16)
                if i >= 4:
                    pe.wait_ge(turn_read, i - 3)
                for o in range(KD):
                    ins = pe.transpose(psum[:, 2 * (i % 4) + o // 4, (o % 4) * n:(o % 4 + 1) * n],
                                       xin[0:n, i, o * P:(o + 1) * P], ident[0:n, 0:n])
                ins.then_inc(turn_done, 1)

            def turn_out(i, t0, n, c):
                pe.wait_ge(aff_done, KD * (4 + c + 1))
                if c == 0:
                    pe.wait_ge(evac[0], UNITS)
                if i >= 3:
                    pe.wait_ge(yout_done, 2 * (i - 3) + 2)
                for o in range(KD):
                    ins = pe.transpose(psum[0:n, out_bank(i) + o // 4, (o % 4) * P:(o % 4 + 1) * P],
                                       y[:, o, t0:t0 + n], ident[:, :])
                ins.then_inc(turn_done, 1)

            pe.wait_ge(ident_in, 16)
            for i, (t0, n, _) in enumerate(TOK_TILES):
                turn_in(i, t0, n)
            pe.wait_ge(turn_read, len(TOK_TILES))
            ffn(0, 0, 0, 0)

            def attend(name):
                if name != ROUNDS[0]:
                    pe.wait_ge(att_free, freed_before(name))
                if name == "poolctx":
                    pe.wait_ge(act_ready[1], KD)
                    pe.wait_ge(mixer_in, 16 * 5)
                    for g in range(NG):
                        ins = pe.transpose(psum[:, 4, g * P:g * P + DB * BUF], uctx[0:DB * BUF, g * P:(g + 1) * P],
                                           ident[0:DB * BUF, 0:DB * BUF])
                elif name == "kctx":
                    for b in range(DB):
                        ins = pe.transpose(psum[:, 5 + b // 4, (b % 4) * P:(b % 4 + 1) * P], kctx[b // 4][:, b % 4, :],
                                           ident[:, :])
                elif name == "uout":
                    for c in range(2):
                        pe.wait_ge(evac[c], MIX_BASE + NG)
                    for g in range(NG):
                        pe.transpose(psum[0:BUF, 4, g * P:(g + 1) * P], line[:, g, SEQ:SEQ + BUF], ident[:, :])
                        ins = pe.transpose(psum[0:NS, 5, g * P:(g + 1) * P], u_new[:, g, :], ident[:, :])
                elif name == "vkout":
                    for c in range(2):
                        pe.wait_ge(evac[c], MIX_BASE + U_K + 1)
                    for n in range(NBLK):
                        pe.transpose(psum[:, 4, n * P:(n + 1) * P], vT[:, n * WIN:(n + 1) * WIN], ident[:, :])
                    pe.transpose(psum[0:NS, 5, 0:P], vT[:, SEQ:T], ident[:, :])
                    pe.transpose(psum[:, 6, 0:P], kT[:, SEQ - WIN:SEQ], ident[:, :])
                    ins = pe.transpose(psum[0:NS, 7, 0:P], kT[:, SEQ:T], ident[:, :])
                elif name in ("grp0", "grp1"):
                    g0 = 2 * (name == "grp1")
                    pe.wait_ge(win_read, g0 + 2)
                    pe.wait_ge(z_done, g0 + 2)
                    for i in range(2):
                        z = line[:, g0 + i, :]
                        w = grp_w[:, g0 + i, :]
                        n = SEQ - C
                        seg = z[:, BUF + SEQ:LINE].rearrange("p (b s) -> p b s", s=SEG)[:, :, BUF:SEG]
                        pe.matmul(psum[:, 4 + 2 * i, 0:C], w, z[:, BUF:BUF + C], start=True, stop=True)
                        pe.matmul(psum[:, 5 + 2 * i, 0:n], w, z[:, BUF + C:BUF + SEQ], start=True, stop=True)
                        ins = pe.matmul(psum[:, 5 + 2 * i, n:C], w, seg, start=True, stop=True)
                elif name in ("Sa", "Sb"):
                    kv = "ab".index(name[1])
                    h = slice(kv * HD, (kv + 1) * HD)
                    q = q_new[h, :]
                    pe.wait_ge(q_new_done, 1)
                    pe.matmul(psum[:, 4, :], q, kctxT[h, 0:512], start=True, stop=True)
                    pe.matmul(psum[:, 5, :], q, kctxT[h, 512:1024], start=True, stop=True)
                    ins = pe.matmul(psum[:, 6, 0:NS], q, kT[h, SEQ:T], start=True, stop=True)
                elif name[0] == "S":
                    n = int(name[1])
                    if n == 0:
                        for c in range(2):
                            pe.wait_ge(evac[c], MIX_BASE + U_GA)
                    k0 = WIN if n == 0 else 0
                    keys = slice((n - 1) * WIN + k0, (n + 1) * WIN)
                    for kv in range(KV):
                        h = slice(kv * HD, (kv + 1) * HD)
                        for j in range(GQ):
                            at = (j % 2) * 2 * WIN
                            ins = pe.matmul(psum[:, 4 + 2 * kv + j // 2, at + k0:at + 2 * WIN],
                                            qT[h, j, n * WIN:(n + 1) * WIN], kT[h, keys], start=True, stop=True)
                elif name in ("Ta", "Tb"):
                    kv = "ab".index(name[1])
                    pe.wait_ge(prob_done, NBLK + 1)
                    pk = p0[:, kv * SKEYS:(kv + 1) * SKEYS]
                    for b in range(DB):
                        pe.transpose(psum[:, 4 + b // 4, (b % 4) * P:(b % 4 + 1) * P], pk[:, b * WIN:(b + 1) * WIN],
                                     ident[:, :])
                    ins = pe.transpose(psum[0:NS, 6, 0:P], pk[:, CTXK:SKEYS], ident[:, :])
                elif name[0] == "T":
                    n = int(name[1])
                    pe.wait_ge(prob_done, n + 1)
                    pb = (p0, p1)[n % 2][:, 0:H * 2 * WIN].rearrange("p (h k) -> p h k", h=H)
                    for kt in range(1 if n == 0 else 0, 2):
                        for h in range(H):
                            ins = pe.transpose(psum[:, 4 + 2 * kt + h // GQ, (h % GQ) * P:(h % GQ + 1) * P],
                                               pb[:, h, kt * WIN:(kt + 1) * WIN], ident[:, :])
                elif name == "PVs":
                    for kv in range(KV):
                        h = slice(kv * HD, (kv + 1) * HD)
                        pk = pT[:, kv * (DB + 1) * P:(kv + 1) * (DB + 1) * P]
                        for b in range(DB):
                            pe.matmul(psum[h, 4, 0:P], vctx[:, b, h], pk[:, b * P:(b + 1) * P], start=b == 0, stop=False)
                        ins = pe.matmul(psum[h, 4, 0:P], vN[0:NS, NBLK, h], pk[0:NS, CTXK:CTXK + P], start=False,
                                        stop=True)
                else:
                    n = int(name[2])
                    first = 1 if n == 0 else 0
                    for kv in range(KV):
                        h = slice(kv * HD, (kv + 1) * HD)
                        for kt in range(first, 2):
                            ins = pe.matmul(psum[h, 4, :], vN[:, n - 1 + kt, h],
                                            pT[:, (2 * kt + kv) * 512:(2 * kt + kv + 1) * 512], start=kt == first,
                                            stop=kt == 1)
                ins.then_inc(att_mm, 1)

            def mix_part(m, c):
                u = MIX_BASE + m
                if m < U_GA or (m - U_GA) % 2 == 0:
                    part(u, c, KD, act_hi, act_lo, ready=act_wait(1, c) if m == 0 else None)
                elif m < U_GB:
                    if m == U_GA + 1:
                        pe.wait_ge(poolz_done, 2 * NG)
                    part(u, c, NG, pz_hi, pz_lo)
                else:
                    if m == U_GB + 1:
                        pe.wait_ge(att_free, freed("PVs" if c else "PV2"))
                    part(u, c, NG, att_hi, att_lo)

            for s in range(MIX1 + LAG):
                if s < MIX1:
                    mix_part(s, 0)
                if s == 1:
                    variance(0, 1)
                if s >= LAG:
                    mix_part(s - LAG, 1)
                for name in STAGES.get(s, []):
                    attend(name)
            for s in range(KD + LAG):
                def m_wait(c):
                    return lambda k: pe.wait_ge(m_done[c], k + 1)
                if s < KD:
                    part(WO_BASE + s, 0, KD, m_hi, m_lo, ready=m_wait(0) if s == 0 else None)
                if s >= LAG:
                    part(WO_BASE + s - LAG, 1, KD, m_hi, m_lo, ready=m_wait(1) if s == LAG else None)
                if s == KD - 1:
                    mean(1, 0)
                if s == KD:
                    variance(1, 0)
            mean(1, 1)
            ffn(2, FFN2_BASE, 2, 2 * KF)
            for i, (t0, n, c) in enumerate(TOK_TILES):
                if i == 3:
                    variance(2, 1)
                turn_out(i, t0, n, c)


def out_bank(i):
    return 2 * (i % 3)


CONST_DMAS = 7 + GQ + 6
SIDE_STORES = 3 + 1 + DB + 2 + 2 * DB
EXP_AFTER = ["S0", "S1", "S2", "S3", "Sb"]
DIVIDE_AT = [12, 14, 17, 20, 24]


def constants():
    f = np.float32
    tok_pos = np.concatenate([np.arange(SEQ), PAST + np.tile(np.arange(DS), DB)]).astype(f)
    freqs = f(THETA) ** (f(-2.0) * np.arange(HD // 2, dtype=f) / f(HD))
    ang = tok_pos[None, :] * freqs[:, None].astype(f)
    cos, sin = np.cos(ang), np.sin(ang)
    cos_sin = np.stack([np.concatenate([cos, cos] * KV), np.concatenate([sin, -sin] * KV)], axis=1).astype(f)
    q = np.arange(WIN)[:, None]
    k = np.arange(WIN)[None, :]
    band = np.concatenate([np.where(k >= q, 0, NEG), np.where(k <= q, 0, NEG)], axis=1).astype(f)
    b, t = np.arange(P)[:, None] % NS // DS, np.arange(P)[:, None] % DS
    ck, nk = np.arange(CTXK)[None, :], np.arange(NS)[None, :]
    smask = np.concatenate([np.where((ck // WIN == b) & (ck % WIN >= t), 0, NEG),
                            np.where((nk // DS == b) & (nk % DS <= t), 0, NEG)], axis=1).astype(f)
    cnt = np.stack([np.minimum(np.arange(max(WINDOWS)) + 1, w) for w in WINDOWS])
    inv = np.broadcast_to((1.0 / cnt).astype(f), (P, NG, max(WINDOWS)))
    return {"c_ident": np.eye(P, dtype=f), "c_mean": np.concatenate([np.full((P, P), 1.0 / D), np.full((P, 1), EPS)], axis=1).astype(f), "c_cos_sin": cos_sin,
            "c_band": band, "c_smask": smask, "c_inv_cnt": np.ascontiguousarray(inv)}


INS = ["x_prompt", "x_sample", "cache_pool_u", "cache_k_win", "cache_v_win", "w_in", "pool_w_grp", "pool_scale",
       "attn_sinks", "w_pool_out", "w_attn_out", "w_out", "ffn1_w1", "ffn1_w3", "ffn1_w2", "ffn2_w1", "ffn2_w3",
       "ffn2_w2", "ln1_g", "ln1_b", "ln2_g", "ln2_b", "ln3_g", "ln3_b"]
OUTS = {"y_prompt": (1, SEQ, D), "y_sample": (DB, DS, D), "pool_u_prompt": (1, 1, BUF, POOLW),
        "k_win_prompt": (1, 1, WIN, KV, HD), "v_win_prompt": (1, 1, WIN, KV, HD),
        "pool_u_sample": (1, DB, BUF, POOLW), "k_win_sample": (1, DB, WIN, KV, HD),
        "v_win_sample": (1, DB, WIN, KV, HD)}


def kernel(**inputs):
    import concourse.bacc as bacc
    from concourse.bass_utils import run_bass_kernel_spmd

    nc = bacc.Bacc("TRN2", target_bir_lowering=False, num_devices=1)
    arrays = {name: np.ascontiguousarray(inputs[name]) for name in INS}
    arrays.update(constants())
    a = {name: nc.dram_tensor(f"in_{name}", v.shape, F32, kind="ExternalInput").ap() for name, v in arrays.items()}
    out = {name: nc.dram_tensor(f"out_{name}", shape, F32, kind="ExternalOutput").ap() for name, shape in OUTS.items()}
    program(nc, a, out)
    r = run_bass_kernel_spmd(nc, [{f"in_{name}": v for name, v in arrays.items()}], core_ids=[0])
    return tuple(r.results[0][f"out_{name}"] for name in OUTS)
```

```python
from contextlib import ExitStack

import numpy as np

import concourse.bass as bass
from concourse import mybir

P = 128
D = 1024
KD = D // P
SEQ = 512
DB, DS = 8, 4
NS = DB * DS
T = SEQ + NS
C = T // 2
PAST = 2048
FF = 2816
KF = FF // P // 2
POOLW = 512
WINDOWS = (2, 4, 8, 16)
NG = len(WINDOWS)
BUF = 15
SEG = BUF + DS
LINE = BUF + SEQ + DB * SEG
H, KV, HD = 8, 2, 64
GQ = H // KV
WIN = 128
NBLK = SEQ // WIN
CTXK = DB * WIN
SKEYS = CTXK + NS
QOFF, KOFF = POOLW, POOLW + H * HD
VOFF, GOFF = KOFF + KV * HD, KOFF + 2 * KV * HD
ALPHA = 2.0 ** 0.25
EPS = 1e-5
THETA = 10000.0
NEG = -1e30

SLOTS = 4
RAWS = 4
LAG = 2
UP, DOWN = 2 * KF, KD
MIX1 = 42
FFN_UNITS = 2 * (UP + DOWN)
MIX_BASE = FFN_UNITS
WO_BASE = MIX_BASE + MIX1
FFN2_BASE = WO_BASE + KD
UNITS = FFN2_BASE + FFN_UNITS

F32 = mybir.dt.float32
F32R = mybir.dt.float32r
ALU = mybir.AluOpType
ACT = mybir.ActivationFunctionType
AX = mybir.AxisListType

U_V, U_K, U_Q, U_GA, U_PA, U_GB = 4, 5, 6, 10, 18, 26
TOK_TILES = [(0, 128, 0), (128, 128, 0), (256, 16, 0), (272, 128, 1), (400, 112, 1), (512, 32, 1)]
STAGES = {1: ["poolctx"], 2: ["kctx"], 6: ["uout"], 8: ["vkout"], 9: ["grp0"], 10: ["S0"], 11: ["grp1"], 12: ["T0"], 13: ["S1"],
          14: ["PV0"], 15: ["T1"], 16: ["S2"], 17: ["PV1"], 18: ["T2"], 20: ["S3"], 21: ["PV2"],
          23: ["T3"], 24: ["Sa", "Sb"], 25: ["PV3"], 26: ["Ta", "Tb"], 27: ["PVs"]}
POOLED_AT = {7: (3, 2), 8: (1, 0)}
EXP_AT = [11, 14, 17, 21, 25]
GROUPS = {"grp0": (0, 1), "grp1": (2, 3)}
ROUNDS = [name for step in sorted(STAGES) for name in STAGES[step]]
READS = {"poolctx": NG, "kctx": 2, "uout": 2, "grp0": 4, "grp1": 4, "vkout": 4, "Sa": 3, "Sb": 3, "Ta": 3, "Tb": 3,
         "T0": 2, "PVs": 1}
READS |= {f"S{n}": 4 for n in range(NBLK)} | {f"T{n}": 4 for n in range(1, NBLK)} | {f"PV{n}": 1 for n in range(NBLK)}


def freed(name):
    return sum(READS[r] for r in ROUNDS[:ROUNDS.index(name) + 1])


def freed_before(name):
    return freed(name) - READS[name]


def written(name):
    return ROUNDS.index(name) + 1



def is_proj(m):
    return U_PA <= m < U_GB or m >= U_GB and (m - U_GB) % 2 == 1


def program(nc, a, out):
    ctx = ExitStack()
    with ctx:
        def sb(name, shape, dt=F32, where=None):
            return (where or ctx).enter_context(nc.sbuf_tensor(name, shape, dt))

        def sem(name):
            return ctx.enter_context(nc.semaphore(name))

        act_hi = sb("act_hi", [P, KD, T], F32R)
        act_lo = sb("act_lo", [P, KD, T], F32R)
        y = sb("y", [P, KD, T])
        ring_hi = sb("ring_hi", [P, SLOTS, KD, P], F32R)
        ring_lo = sb("ring_lo", [P, SLOTS, KD, P], F32R)
        raw = sb("raw", [P, RAWS, KD, P])
        band = sb("band", [P, 2 * WIN])
        smask = sb("smask", [P, SKEYS])
        ident = sb("ident", [P, P])
        mean_w = sb("mean_w", [P, P + 1])
        inv_cnt = sb("inv_cnt", [P, NG, max(WINDOWS)])
        vecs = sb("vecs", [P, VEC_ROWS])
        ln_gb = vecs[:, 0:6 * KD].rearrange("p (i k) -> p i k", i=6)
        pscale = vecs[:, 6 * KD:VEC_ROWS]
        sinks = sb("sinks", [P, H])
        sinks_s = sb("sinks_s", [P, KV])
        soft = sb("soft", [P, 2, 6, H])
        fsum = sb("fsum", [P, 2, C])
        rstd = sb("rstd", [P, C])
        p0 = sb("p0", [P, KD * C])
        tmp_a = sb("tmp_a", [P, 2, C])
        tmp_v = sb("tmp_v", [P, 2, C])
        tmp_r = sb("tmp_r", [P, C])
        sq = p0[:, :].rearrange("p (o t) -> p o t", o=KD)
        vec_rows = p0[0:VEC_ROWS, 0:P]
        MAX, NEG_MAX, SINK, SUM, DEN, REC = range(6)

        with ExitStack() as ffn_mem:
            ext_hi = sb("ext_hi", [P, SLOTS, KF - KD, P], F32R, ffn_mem)
            ext_lo = sb("ext_lo", [P, SLOTS, KF - KD, P], F32R, ffn_mem)
            ext_raw = sb("ext_raw", [P, RAWS, KF - KD, P], F32, ffn_mem)
            with ExitStack() as x_mem:
                xin = sb("xin", [P, len(TOK_TILES), D], F32, x_mem)
            hid_hi = sb("hid_hi", [P, KF, T], F32R, ffn_mem)
            hid_lo = sb("hid_lo", [P, KF, T], F32R, ffn_mem)
        with ExitStack() as mix_mem:
            m1 = sb("m1", [P, KD, T], F32, mix_mem)
            with ExitStack() as early_mem:
                cos_sin = sb("cos_sin", [P, 2, T], F32, early_mem)
                vT = sb("vT", [P, T], F32, early_mem)
                grp_w = sb("grp_w", [P, NG, P], F32, early_mem)
            att_lo = sb("att_lo", [P, GQ, T], F32R, mix_mem)
            with ExitStack() as q_mem:
                qT = sb("qT", [P, GQ, T], F32, q_mem)
            att_hi = sb("att_hi", [P, GQ, T], F32R, mix_mem)
            with ExitStack() as win_mem:
                wins = sb("wins", [P, NG + 2, LINE], F32, win_mem)
            with ExitStack() as branch_mem:
                pz_hi = sb("pz_hi", [P, NG, T], F32R, branch_mem)
                pz_lo = sb("pz_lo", [P, NG, T], F32R, branch_mem)
                p1 = sb("p1", [P, H * 2 * WIN], F32, branch_mem)
                with ExitStack() as line_mem:
                    line = sb("line", [P, NG, LINE], F32, line_mem)
                pT = sb("pT", [P, 4 * LINE], F32, branch_mem)
                kT = sb("kT", [P, T], F32, branch_mem)
                vN = sb("vN", [P, NBLK + 1, P], F32, branch_mem)
                kctxT = sb("kctxT", [P, CTXK], F32, branch_mem)
                vctx = sb("vctx", [P, DB, P], F32, branch_mem)
                u_new = sb("u_new", [P, NG, NS], F32, branch_mem)
                q_new = sb("q_new", [P, GQ * NS], F32, branch_mem)
            m_hi = sb("m_hi", [P, KD, T], F32R, mix_mem)
            m_lo = sb("m_lo", [P, KD, T], F32R, mix_mem)
        kctx = [m1[:, i, 0:4 * WIN].rearrange("p (b n) -> p b n", n=P) for i in range(2)]
        rows_k = p0[:, 2 * POOLW:2 * POOLW + 2 * P].rearrange("p (a n) -> p a n", a=2)
        scaled = p1[:, 0:3 * T].rearrange("p (g t) -> p g t", g=3)
        uctx = p1[:, 0:POOLW]
        rows_u = p0[:, 0:2 * POOLW].rearrange("p (a n) -> p a n", a=2)
        psum = ctx.enter_context(nc.psum_tensor("psum", [P, 8, 512], F32))

        ident_in = sem("ident_in")
        consts_in = sem("consts_in")
        x_in = [sem(f"x_in{i}") for i in range(len(TOK_TILES))]
        raw_in = [sem(f"raw_in{i}") for i in range(RAWS)]
        vec_in = sem("vec_in")
        vecs_done = sem("vecs_done")
        mixer_in = sem("mixer_in")
        hi_done = sem("hi_done")
        lo_done = sem("lo_done")
        mm_done = [sem(f"mm_done{c}") for c in range(2)]
        evac = [sem(f"evac{c}") for c in range(2)]
        hid_hi_done = [sem(f"hid_hi_done{c}") for c in range(2)]
        hid_done = [sem(f"hid_done{c}") for c in range(2)]
        y_done = [sem(f"y_done{c}") for c in range(2)]
        fsum_step = sem("fsum_step")
        fsum_done = [sem(f"fsum_done{c}") for c in range(2)]
        mean_done = [sem(f"mean_done{c}") for c in range(2)]
        cent_done = sem("cent_done")
        sq_done = sem("sq_done")
        sqsum_done = sem("sqsum_done")
        var_done = sem("var_done")
        std_done = sem("std_done")
        norm_done = sem("norm_done")
        aff_done = sem("aff_done")
        act_ready = [sem(f"act_ready{c}") for c in range(2)]
        turn_done = sem("turn_done")
        turn_read = sem("turn_read")
        v_step = sem("v_step")
        win_step = sem("win_step")
        win_done = sem("win_done")
        q_new_done = sem("q_new_done")
        z_done = sem("z_done")
        poolz_done = sem("poolz_done")
        m_done = [sem(f"m_done{c}") for c in range(2)]
        att_mm = sem("att_mm")
        att_free = sem("att_free")
        neg_done = sem("neg_done")
        exp_done = sem("exp_done")
        prob_done = sem("prob_done")
        yout_done = sem("yout_done")
        side_stored = sem("side_stored")
        stored = sem("stored")

        block = ctx.enter_context(nc.Block())

        def tok(c):
            return slice(c * C, c * C + C)

        def unit_kind(u):
            for base in (0, FFN2_BASE):
                if base <= u < base + FFN_UNITS:
                    return KD if (u - base) % (UP + DOWN) < UP else KF
            m = u - MIX_BASE
            return NG if m < MIX1 and is_proj(m) else KD

        def bank_of(u, c):
            if MIX_BASE <= u < FFN2_BASE:
                return 2 * c + u % 2
            return 4 * c + u % 4

        def stat_bank(l, c):
            return 7 if c else (0, 4, 0)[l]

        def y_before(l):
            return (DOWN, 2 * DOWN, 4 * DOWN)[l]

        @block.sync
        def _(sp):
            def w_tiles(w, k0, kn):
                return w[0, k0 * P:(k0 + kn) * P, :].rearrange("(k p) n -> p k n", p=P)

            def load(slot, src, kn, cols):
                first = kn // 2 if kn <= KD else KD
                sp.dma_start(raw[:, slot, 0:first, :], src[:, 0:first, cols]).then_inc(raw_in[slot], 16)
                dst = raw[:, slot, first:kn, :] if kn <= KD else ext_raw[:, slot, :, :]
                sp.dma_start(dst, src[:, first:kn, cols]).then_inc(raw_in[slot], 16)

            def raw_free(u):
                if not isinstance(u, int) or u >= RAWS:
                    sp.wait_ge(lo_done, u - (RAWS - 1))

            def ffn_loads(base, w1, w3, w2):
                w1k, w3k = w_tiles(w1, 0, KD), w_tiles(w3, 0, KD)
                for half in range(2):
                    b, c0 = base + half * (UP + DOWN), half * KF * P
                    for n in range(6):
                        if b + n:
                            raw_free(b + n)
                            load((b + n) % RAWS, (w1k, w3k)[n % 2], KD,
                                 slice(c0 + n // 2 * P, c0 + (n // 2 + 1) * P))
                    with sp.Fori(1, (KF - 1) // 2) as i:
                        for n in range(4):
                            raw_free(i * 4 + (b + 2 + n))
                            load((b + 2 + n) % RAWS, (w1k, w3k)[n % 2], KD,
                                 bass.ds(i * (2 * P) + (c0 + (1 + n // 2) * P), P))
                    w2k = w_tiles(w2, half * KF, KF)
                    with sp.Fori(0, DOWN // 4) as o:
                        for n in range(4):
                            raw_free(o * 4 + (b + UP + n))
                            load((b + UP + n) % RAWS, w2k, KF, bass.ds(o * (4 * P) + n * P, P))

            for i, (t0, n, _) in enumerate(TOK_TILES):
                src = a["x_prompt"][0, t0:t0 + n, :] if t0 < SEQ else a["x_sample"].rearrange("b t d -> (b t) d")
                sp.dma_start(xin[0:n, i, :], src).then_inc(x_in[i], 16)
                if i == 0:
                    sp.dma_start(ident[:, :], a["c_ident"]).then_inc(ident_in, 16)
                if i == 2:
                    load(0, w_tiles(a["ffn1_w1"], 0, KD), KD, slice(0, P))
            ffn_loads(0, a["ffn1_w1"], a["ffn1_w3"], a["ffn1_w2"])

            win_k = w_tiles(a["w_in"], 0, KD)
            wpo_k = w_tiles(a["w_pool_out"], 0, NG)
            wo_k = w_tiles(a["w_out"], 0, KD)
            first_cols = [g * P for g in reversed(range(NG))] + [VOFF, KOFF]
            for m in range(MIX1):
                u = MIX_BASE + m
                slot = u % RAWS
                raw_free(u)
                o = (m - U_GB) // 2 if m >= U_GB else m - (U_PA if m >= U_PA else U_GA)
                if m < U_Q:
                    load(slot, win_k, KD, slice(first_cols[m], first_cols[m] + P))
                elif m < U_GA:
                    for kv in range(KV):
                        c0 = QOFF + kv * GQ * HD + (m - U_Q) * HD
                        sp.dma_start(raw[:, slot, :, kv * HD:(kv + 1) * HD],
                                     win_k[:, :, c0:c0 + HD]).then_inc(raw_in[slot], 16)
                elif not is_proj(m):
                    c0 = GOFF + (m >= U_GB) * D + o * P
                    load(slot, win_k, KD, slice(c0, c0 + P))
                elif m < U_GB:
                    load(slot, wpo_k, NG, slice(o * P, o * P + P))
                else:
                    for kv in range(KV):
                        src = a["w_attn_out"][0, kv * GQ * HD:(kv + 1) * GQ * HD, o * P:o * P + P]
                        sp.dma_start(raw[kv * HD:(kv + 1) * HD, slot, 0:GQ, :],
                                     src.rearrange("(j d) n -> d j n", d=HD)).then_inc(raw_in[slot], 16)
            for o in range(KD):
                raw_free(WO_BASE + o)
                load((WO_BASE + o) % RAWS, wo_k, KD, slice(o * P, o * P + P))
            ffn_loads(FFN2_BASE, a["ffn2_w1"], a["ffn2_w3"], a["ffn2_w2"])

            for i, (t0, n, _) in enumerate(TOK_TILES):
                sp.wait_ge(yout_done, 2 * i + 2)
                dst = out["y_prompt"][0, t0:t0 + n, :] if t0 < SEQ else out["y_sample"].rearrange("b t d -> (b t) d")
                sp.dma_start(dst, xin[0:n, i, :]).then_inc(stored, 16)
            sp.wait_ge(stored, 16 * len(TOK_TILES))
            sp.wait_ge(side_stored, 16 * SIDE_STORES)

        @block.gpsimd
        def _(pool):
            pool.wait_ge(x_in[-1], 16)
            for i, name in enumerate(("ln1_g", "ln1_b", "ln2_g", "ln2_b", "ln3_g", "ln3_b")):
                pool.dma_start(p0[i * KD:(i + 1) * KD, 0:P], a[name][0].rearrange("(k p) -> k p", p=P)) \
                    .then_inc(vec_in, 16)
            pool.dma_start(p0[6 * KD:VEC_ROWS, 0:P], a["pool_scale"][0].rearrange("(g p) -> g p", p=P)) \
                .then_inc(vec_in, 16)
            loads = [(mean_w[:, :], a["c_mean"]), (band[:, :], a["c_band"]), (smask[:, :], a["c_smask"]),
                     (sinks[:, :], a["attn_sinks"][0:1, :].broadcast_to([P, H]))]
            for j in range(GQ):
                src = a["attn_sinks"][0:1, :].rearrange("a (k j) -> a j k", j=GQ)[:, j, :]
                loads.append((sinks_s[j * NS:(j + 1) * NS, :], src.broadcast_to([NS, KV])))
            assert len(loads) == CONST_DMAS
            for dst, src in loads:
                pool.dma_start(dst, src, allow_slow_non_contiguous=True).then_inc(consts_in, 16)

            def feature_sum(l, c):
                for o in range(1, KD):
                    pool.wait_ge(y_done[c], y_before(l) + o + 1)
                    if o == 1:
                        first = y[:, 0, tok(c)]
                        if l:
                            pool.wait_ge(mean_done[c], l)
                    else:
                        first = fsum[:, c, :]
                        pool.wait_ge(fsum_step, (2 * l + c) * (KD - 2) + o - 1)
                    ins = pool.tensor_tensor(fsum[:, c, :], first, y[:, o, tok(c)], ALU.add)
                    ins.then_inc(fsum_step if o < KD - 1 else fsum_done[c], 1)

            feature_sum(0, 0)
            feature_sum(0, 1)

            pool.wait_ge(mm_done[0], FFN_UNITS)
            pool.wait_ge(mm_done[1], FFN_UNITS)
            pool.memset(line[:, :, 0:BUF], 0.0).then_inc(win_step, 1)
            pool.dma_start(uctx[0:DB * BUF, :], a["cache_pool_u"][0].rearrange("b t w -> (b t) w")) \
                .then_inc(mixer_in, 16)
            for i in range(2):
                pool.dma_start(kctx[i], a["cache_k_win"][0, 4 * i:4 * i + 4].rearrange("b t h d -> t b (h d)")) \
                    .then_inc(mixer_in, 16)
            pool.dma_start(vctx[:, :, :], a["cache_v_win"][0].rearrange("b t h d -> t b (h d)")).then_inc(mixer_in, 16)
            pool.dma_start(inv_cnt[:, :, :], a["c_inv_cnt"]).then_inc(mixer_in, 16)
            pool.dma_start(cos_sin[:, :, :], a["c_cos_sin"]).then_inc(mixer_in, 16)
            pool.dma_start(grp_w[:, :, :], a["pool_w_grp"][0].rearrange("g c d -> c g d")).then_inc(mixer_in, 16)
            for name, src, n in (("k_win_sample", "cache_k_win", WIN), ("v_win_sample", "cache_v_win", WIN),
                                 ("pool_u_sample", "cache_pool_u", BUF)):
                pool.dma_start(out[name][0, :, 0:n - DS], a[src][0, :, DS:n]).then_inc(side_stored, 16)

            pool.wait_ge(att_free, freed("poolctx"))
            steps = 1
            for n, g in enumerate(reversed(range(NG))):
                for c in range(2):
                    pool.wait_ge(evac[c], MIX_BASE + n + 1)
                pool.wait_ge(win_step, steps)
                if n:
                    pool.wait_ge(win_done, n)
                src = line[:, g, :]
                for i in range(g + 1):
                    sh = 1 << i
                    lo = 2 * sh - 1
                    if i:
                        pool.wait_ge(win_step, steps)
                    dst = wins[:, g if i == g else NG + i % 2, :]
                    ins = pool.tensor_tensor(dst[:, lo:LINE], src[:, lo:LINE], src[:, lo - sh:LINE - sh], ALU.add)
                    ins.then_inc(win_done if i == g else win_step, 1)
                    steps += i < g
                    src = dst

            pool.wait_ge(att_free, freed("uout"))
            pool.dma_start(out["pool_u_prompt"][0, 0], rows_u[0:BUF, 0, :]).then_inc(side_stored, 16)
            for b in range(DB):
                pool.dma_start(out["pool_u_sample"][0, b, BUF - DS:BUF], rows_u[b * DS:(b + 1) * DS, 1, :]) \
                    .then_inc(side_stored, 16)
            pool.wait_ge(att_free, freed("vkout"))
            for name, row in (("k_win_prompt", rows_k[:, 0, :]), ("v_win_prompt", vN[:, NBLK - 1, :])):
                pool.dma_start(out[name][0, 0].rearrange("t h d -> t (h d)"), row).then_inc(side_stored, 16)
            for name, row in (("k_win_sample", rows_k[0:NS, 1, :]), ("v_win_sample", vN[0:NS, NBLK, :])):
                for b in range(DB):
                    pool.dma_start(out[name][0, b, WIN - DS:WIN].rearrange("t h d -> t (h d)"),
                                   row[b * DS:(b + 1) * DS]).then_inc(side_stored, 16)

            for l in (1, 2):
                feature_sum(l, 0)
                feature_sum(l, 1)

        @block.scalar
        def _(act):
            def split(u, kn, at=None):
                s, r = (u if at is None else at) % SLOTS, (u if at is None else at) % RAWS
                act.wait_ge(raw_in[r], u * (32 // RAWS) + (32 - r * (32 // RAWS)))
                if at is not None or u >= SLOTS:
                    act.wait_ge(mm_done[1], u - (SLOTS - 1))
                n = min(kn, KD)
                ins = act.activation(ring_hi[:, s, 0:n, :], raw[:, r, 0:n, :], ACT.Copy)
                if kn > KD:
                    ins = act.activation(ext_hi[:, s, :, :], ext_raw[:, r, :, :], ACT.Copy)
                ins.then_inc(hi_done, 1)

            def norm_squares(l, c):
                for i in range(2):
                    act.wait_ge(cent_done, 4 * l + 2 * c + i + 1)
                    act.activation(sq[:, 4 * i:4 * i + 4, :], y[:, 4 * i:4 * i + 4, tok(c)], ACT.Square) \
                        .then_inc(sq_done, 1)

            def norm_affine(l, c):
                act.wait_ge(var_done, 2 * l + c + 1)
                act.activation(rstd[:, :], psum[:, stat_bank(l, c), 0:C], ACT.Sqrt, bias=mean_w[:, P:P + 1]) \
                    .then_inc(std_done, 1)
                for o in range(KD):
                    act.wait_ge(norm_done, 4 * l + 2 * c + o // 4 + 1)
                    act.activation(y[:, o, tok(c)], y[:, o, tok(c)], ACT.Identity, bias=ln_gb[:, 2 * l + 1, o:o + 1],
                                   scale=ln_gb[:, 2 * l, o:o + 1]).then_inc(aff_done, 1)

            def through(u, c, func, at=None, scale=1.0):
                act.wait_ge(mm_done[c], u + 1)
                act.wait_ge(evac[c], u)
                act.activation(tmp_a[:, c, :], psum[:, bank_of(u if at is None else at, c), 0:C], func, scale=scale) \
                    .then_inc(evac[c], 1)

            def residual(u, c, n, scale):
                if n:
                    act.wait_ge(y_done[c], n)
                through(u, c, ACT.Copy, scale=scale)

            def ffn(l, base, y_n):
                for half in range(2):
                    b = base + half * (UP + DOWN)

                    def up_step(s, u, kn):
                        if s % 2 == 0 and s < UP:
                            through(u, 0, ACT.Silu, at=b + s)
                        if s % 2 == 0 and s >= LAG:
                            through(u - LAG, 1, ACT.Silu, at=b + s - LAG)
                        if kn:
                            split(u + 2, kn, at=b + s + 2)

                    if y_n:
                        act.wait_ge(y_done[0], y_n)
                        act.wait_ge(y_done[1], y_n)
                    up_step(0, b, 0)
                    if l == 2 and half == 0:
                        norm_affine(1, 1)
                    with act.Fori(0, 4) as i:
                        for j in range(4):
                            up_step(2 + j, i * 4 + (b + 2 + j), KD)
                    for s in range(18, UP + LAG):
                        up_step(s, b + s, unit_kind(b + s + 2))
                    b += UP
                    if l == 0 and half == 0:
                        act.wait_ge(turn_done, len(TOK_TILES) + 1)
                        act.activation(vecs[:, :], psum[:, VEC_BANK, 0:VEC_ROWS], ACT.Copy).then_inc(vecs_done, 1)
                    for s in range(DOWN + LAG):
                        if s < DOWN:
                            residual(b + s, 0, y_n + s, 0.5)
                        if s >= LAG:
                            residual(b + s - LAG, 1, y_n + s - LAG, 0.5)
                            if b + s + 2 < UNITS:
                                split(b + s + 2, unit_kind(b + s + 2))
                        if half == 1 and s == DOWN - 1:
                            norm_squares(l, 0)
                        if half == 1 and s == DOWN:
                            norm_affine(l, 0)
                    y_n += DOWN

            for i, (t0, n, _) in enumerate(TOK_TILES):
                act.wait_ge(turn_done, i + 1)
                for h in range(2):
                    ins = act.activation(y[:, 4 * h:4 * h + 4, t0:t0 + n],
                                         psum[:, in_bank(i) + h, 0:4 * n].rearrange("p (o t) -> p o t", o=4), ACT.Copy)
                ins.then_inc(turn_read, 1)
                if i == 2:
                    split(0, KD)
                    split(1, KD)
            split(2, KD)
            split(3, KD)
            ffn(0, 0, 0)
            norm_squares(0, 1)

            def epilogue(m, c):
                u = MIX_BASE + m
                bank = bank_of(u, c)
                if m < U_V:
                    act.wait_ge(mm_done[c], u + 1)
                    act.wait_ge(evac[c], u)
                    n = C if c == 0 else SEQ - C
                    ins = act.activation(line[:, NG - 1 - m, BUF + c * C:BUF + c * C + n], psum[:, bank, 0:n], ACT.Copy)
                    if c == 1:
                        seg = line[:, NG - 1 - m, BUF + SEQ:LINE].rearrange("p (b s) -> p b s", s=SEG)[:, :, BUF:SEG]
                        act.activation(seg, psum[:, bank, n:C].rearrange("p (b s) -> p b s", s=DS), ACT.Copy)
                        ins = act.activation(u_new[:, NG - 1 - m, :], psum[:, bank, n:C], ACT.Copy)
                    ins.then_inc(evac[c], 1)
                elif m == U_V:
                    act.wait_ge(mm_done[c], u + 1)
                    act.wait_ge(evac[c], u)
                    act.activation(vT[:, tok(c)], psum[:, bank, 0:C], ACT.Copy).then_inc(evac[c], 1)
                elif U_GA <= m < U_PA:
                    act.wait_ge(mm_done[c], u + 1)
                    act.wait_ge(evac[c], u)
                    act.activation(m1[:, m - U_GA, tok(c)], psum[:, bank, 0:C], ACT.Sigmoid).then_inc(evac[c], 1)
                elif m >= U_GB and not is_proj(m):
                    through(u, c, ACT.Sigmoid)

            def copy_out(dst, src):
                act.activation(dst, src, ACT.Copy).then_inc(att_free, 1)

            def att_copies(name):
                act.wait_ge(att_mm, written(name))
                if name == "poolctx":
                    segs = line[:, :, BUF + SEQ:LINE].rearrange("p g (b s) -> p g b s", s=SEG)
                    for g in range(NG):
                        copy_out(segs[:, g, :, 0:BUF],
                                 psum[:, 4, g * P:g * P + DB * BUF].rearrange("p (b s) -> p b s", s=BUF))
                elif name == "kctx":
                    for h in range(2):
                        copy_out(kctxT[:, 512 * h:512 * h + 512], psum[:, 5 + h, :])
                elif name == "uout":
                    copy_out(rows_u[0:BUF, 0, :], psum[0:BUF, 4, :])
                    copy_out(rows_u[0:NS, 1, :], psum[0:NS, 5, :])
                elif name == "vkout":
                    copy_out(vN[:, 0:NBLK, :], psum[:, 4, :].rearrange("p (n d) -> p n d", d=P))
                    copy_out(vN[0:NS, NBLK, :], psum[0:NS, 5, 0:P])
                    copy_out(rows_k[:, 0, :], psum[:, 6, 0:P])
                    copy_out(rows_k[0:NS, 1, :], psum[0:NS, 7, 0:P])
                elif name in GROUPS:
                    for i, g in enumerate(GROUPS[name]):
                        prod = psum[:, 4 + 2 * i:6 + 2 * i, 0:C]
                        if g >= 3:
                            act.wait_ge(poolz_done, g - 2)
                        act.activation(scaled[:, g % 3, :].rearrange("p (c t) -> p c t", c=2), prod, ACT.Copy,
                                       scale=pscale[:, g:g + 1]).then_inc(att_free, 1)
                        act.activation(pz_hi[:, g, :].rearrange("p (c t) -> p c t", c=2), prod, ACT.Copy,
                                       scale=pscale[:, g:g + 1]).then_inc(att_free, 1)
                elif name in ("Ta", "Tb"):
                    k0 = (name == "Tb") * (DB + 1) * P
                    for h in range(2):
                        copy_out(pT[:, k0 + 512 * h:k0 + 512 * h + 512], psum[:, 4 + h, :])
                    copy_out(pT[0:NS, k0 + CTXK:k0 + CTXK + P], psum[0:NS, 6, 0:P])
                elif name[0] == "T":
                    for b in range(2 if name == "T0" else 0, 4):
                        copy_out(pT[:, b * 512:(b + 1) * 512], psum[:, 4 + b, :])

            def exps(i):
                act.wait_ge(neg_done, i + 1)
                st = soft[:, i % 2]
                if i == NBLK:
                    parts = [(p0[:, kv * SKEYS:(kv + 1) * SKEYS], kv) for kv in range(KV)]
                else:
                    pb = (p0, p1)[i % 2][:, 0:H * 2 * WIN].rearrange("p (h k) -> p h k", h=H)
                    parts = [(pb[:, h, (WIN if i == 0 else 0):2 * WIN], h) for h in range(H)]
                for part, h in parts:
                    act.activation(part, part, ACT.Exp, bias=st[:, NEG_MAX, h:h + 1], accum_out=st[:, SUM, h:h + 1])
                act.activation(st[:, SINK, 0:len(parts)], st[:, SINK, 0:len(parts)], ACT.Exp).then_inc(exp_done, 1)

            for s in range(MIX1 + LAG):
                if s < MIX1:
                    epilogue(s, 0)
                if s == 0:
                    norm_affine(0, 1)
                if s >= LAG:
                    epilogue(s - LAG, 1)
                    split(MIX_BASE + s + 2, unit_kind(MIX_BASE + s + 2))
                for name in STAGES.get(s, []):
                    if name in ("poolctx", "kctx", "uout", "vkout", *GROUPS) or name[0] == "T":
                        att_copies(name)
                if s in EXP_AT:
                    exps(EXP_AT.index(s))
            for s in range(KD + LAG):
                if s < KD:
                    residual(WO_BASE + s, 0, y_before(1) + s, 1.0)
                if s >= LAG:
                    residual(WO_BASE + s - LAG, 1, y_before(1) + s - LAG, 1.0)
                    split(WO_BASE + s + 2, unit_kind(WO_BASE + s + 2))
                if s == KD - 1:
                    norm_squares(1, 0)
                if s == KD:
                    norm_affine(1, 0)
            norm_squares(1, 1)
            ffn(2, FFN2_BASE, 3 * DOWN)
            norm_squares(2, 1)
            for i, (t0, n, c) in enumerate(TOK_TILES):
                if i == 3:
                    norm_affine(2, 1)
                act.wait_ge(turn_done, len(TOK_TILES) + i + 2)
                for h in range(2):
                    act.activation(xin[0:n, i, 512 * h:512 * h + 512], psum[0:n, out_bank(i) + h, :], ACT.Copy) \
                        .then_inc(yout_done, 1)

        @block.vector
        def _(dve):
            steps = [0]

            def step(ins):
                ins.then_inc(v_step, 1)
                steps[0] += 1
                dve.wait_ge(v_step, steps[0])

            def split(u, kn, at=None):
                s, r = (u if at is None else at) % SLOTS, (u if at is None else at) % RAWS
                dve.wait_ge(hi_done, u + 1)
                n = min(kn, KD)
                ins = dve.tensor_tensor(ring_lo[:, s, 0:n, :], raw[:, r, 0:n, :], ring_hi[:, s, 0:n, :], ALU.subtract)
                if kn > KD:
                    ins = dve.tensor_tensor(ext_lo[:, s, :, :], ext_raw[:, r, :, :], ext_hi[:, s, :, :], ALU.subtract)
                ins.then_inc(lo_done, 1)

            def hidden(u, c, n, f, at):
                dve.wait_ge(mm_done[c], u + 1)
                dve.wait_ge(evac[c], u)
                if not isinstance(n, int) or n:
                    dve.wait_ge(hid_done[c], n)
                dve.tensor_tensor(tmp_v[:, c, :], psum[:, bank_of(at, c), 0:C], tmp_a[:, c, :], ALU.mult) \
                    .then_inc(evac[c], 1)
                dve.wait_ge(evac[c], u + 1)
                hi = hid_hi[:, f, tok(c)] if isinstance(f, int) else hid_hi[:, bass.ds(f, 1), tok(c)]
                lo = hid_lo[:, f, tok(c)] if isinstance(f, int) else hid_lo[:, bass.ds(f, 1), tok(c)]
                v = tmp_v[:, c, :] if isinstance(f, int) else tmp_v[:, c:c + 1, :]
                dve.tensor_copy(hi, v).then_inc(hid_hi_done[c], 1)
                dve.wait_ge(hid_hi_done[c], n + 1)
                dve.tensor_tensor(lo, v, hi, ALU.subtract).then_inc(hid_done[c], 1)

            def residual(u, c, o, factor):
                dve.wait_ge(evac[c], u + 1)
                dve.scalar_tensor_tensor(out=y[:, o, tok(c)], in0=y[:, o, tok(c)], scalar=factor,
                                         in1=tmp_a[:, c, :], op0=ALU.mult, op1=ALU.add).then_inc(y_done[c], 1)

            def norm_center(l, c):
                dve.wait_ge(mean_done[c], l + 1)
                mean = psum[:, stat_bank(l, c):stat_bank(l, c) + 1, 0:C].broadcast_to([P, 4, C])
                for i in range(2):
                    half = y[:, 4 * i:4 * i + 4, tok(c)]
                    dve.tensor_tensor(half, half, mean, ALU.subtract).then_inc(cent_done, 1)
                dve.wait_ge(sq_done, 4 * l + 2 * c + 2)
                step(dve.tensor_tensor(sq[:, 0:4, :], sq[:, 0:4, :], sq[:, 4:8, :], ALU.add))
                step(dve.tensor_tensor(sq[:, 0:2, :], sq[:, 0:2, :], sq[:, 2:4, :], ALU.add))
                dve.tensor_tensor(sq[:, 0, :], sq[:, 0, :], sq[:, 1, :], ALU.add).then_inc(sqsum_done, 1)

            def norm_scale(l, c):
                dve.wait_ge(std_done, 2 * l + c + 1)
                step(dve.reciprocal(rstd[:, :], rstd[:, :]))
                r = rstd[:, :].rearrange("p (a t) -> p a t", a=1).broadcast_to([P, 4, C])
                for i in range(2):
                    half = y[:, 4 * i:4 * i + 4, tok(c)]
                    dve.tensor_tensor(half, half, r, ALU.mult).then_inc(norm_done, 1)
                if l < 2:
                    split_act(l + 1, c)

            def split_act(l, c):
                for i in range(KD // 2):
                    if l:
                        dve.wait_ge(aff_done, KD * (2 * (l - 1) + c) + 2 * i + 2)
                    hi, v = act_hi[:, 2 * i:2 * i + 2, tok(c)], y[:, 2 * i:2 * i + 2, tok(c)]
                    step(dve.tensor_copy(hi, v))
                    dve.tensor_tensor(act_lo[:, 2 * i:2 * i + 2, tok(c)], v, hi, ALU.subtract).then_inc(act_ready[c], 1)

            def ffn(l, base, hid_n):
                for half in range(2):
                    b = base + half * (UP + DOWN)

                    def up_step(s, u, n, kn, f=None):
                        f = s // 2 if f is None else f
                        if s % 2 == 1 and s < UP:
                            hidden(u, 0, n, f, b + s)
                        if s % 2 == 1 and s >= LAG:
                            hidden(u - LAG, 1, n - 1, f - 1, b + s - LAG)
                        if kn:
                            split(u + 2, kn, at=b + s + 2)

                    if l == 2 and half == 0:
                        norm_scale(1, 1)
                    up_step(1, b + 1, hid_n, 0)
                    with dve.Fori(0, 4) as i:
                        for j in range(4):
                            s = 2 + j
                            up_step(s, i * 4 + (b + s), i * 2 + (hid_n + s // 2), KD, i * 2 + s // 2)
                    for s in range(18, UP + LAG):
                        up_step(s, b + s, hid_n + s // 2, unit_kind(b + s + 2))
                    hid_n += KF
                    b += UP
                    for s in range(DOWN + LAG):
                        if s < DOWN:
                            residual(b + s, 0, s, 1.0 if half else ALPHA)
                        if s >= LAG:
                            residual(b + s - LAG, 1, s - LAG, 1.0 if half else ALPHA)
                            if b + s + 2 < UNITS:
                                split(b + s + 2, unit_kind(b + s + 2))
                        if half == 1 and s == DOWN - 1:
                            norm_center(l, 0)
                        if half == 1 and s == DOWN:
                            norm_scale(l, 0)

            for c in range(2):
                dve.wait_ge(turn_read, 3 * c + 3)
                split_act(0, c)
                for u in range(2 * c, 2 * c + 2):
                    split(u, KD)
            ffn(0, 0, 0)
            norm_center(0, 1)

            def rotate(u, c, dst):
                dve.wait_ge(mm_done[c], u + 1)
                dve.wait_ge(evac[c], u)
                dve.wait_ge(evac[1 - c], u - LAG if c == 0 else u + LAG + 1)
                x = psum[:, bank_of(u, c), 0:C]
                step(dve.tensor_tensor(tmp_v[:, c, :], x, cos_sin[:, 0, tok(c)], ALU.mult))
                half = HD // 2
                for q in range(0, P, half):
                    to = q + half if q % HD == 0 else q - half
                    ins = dve.tensor_tensor(tmp_r[to:to + half, :], x[q:q + half, :],
                                            cos_sin[q:q + half, 1, tok(c)], ALU.mult)
                step(ins)
                dve.tensor_tensor(dst, tmp_v[:, c, :], tmp_r[:, :], ALU.add).then_inc(evac[c], 1)

            def epilogue(m, c):
                u = MIX_BASE + m
                if m == U_K:
                    rotate(u, c, kT[:, tok(c)])
                elif U_Q <= m < U_GA:
                    rotate(u, c, qT[:, m - U_Q, tok(c)])
                    if m == U_GA - 1 and c == 1:
                        dve.wait_ge(evac[1], u + 1)
                        dve.tensor_copy(q_new[:, :].rearrange("p (j t) -> p j t", j=GQ), qT[:, :, SEQ:T]) \
                            .then_inc(q_new_done, 1)
                elif is_proj(m):
                    dve.wait_ge(mm_done[c], u + 1)
                    dve.wait_ge(evac[c], u)
                    prod = psum[:, bank_of(u, c), 0:C]
                    if m < U_GB:
                        gate = m1[:, m - U_PA, tok(c)]
                        dve.tensor_tensor(gate, prod, gate, ALU.mult) \
                            .then_inc(evac[c], 1)
                        return
                    o = (m - U_GB) // 2
                    if o:
                        dve.wait_ge(m_done[c], o)
                    dve.tensor_tensor(tmp_v[:, c, :], prod, tmp_a[:, c, :], ALU.mult).then_inc(evac[c], 1)
                    dve.wait_ge(evac[c], u + 1)
                    step(dve.tensor_tensor(tmp_v[:, c, :], tmp_v[:, c, :], m1[:, o, tok(c)], ALU.add))
                    step(dve.tensor_copy(m_hi[:, o, tok(c)], tmp_v[:, c, :]))
                    dve.tensor_tensor(m_lo[:, o, tok(c)], tmp_v[:, c, :], m_hi[:, o, tok(c)], ALU.subtract) \
                        .then_inc(m_done[c], 1)

            def pooled(g):
                n = NG - 1 - g
                if n == 0:
                    dve.wait_ge(att_mm, written("uout"))
                    dve.wait_ge(mixer_in, 16 * MIXER_DMAS)
                else:
                    dve.wait_ge(z_done, n)
                dve.wait_ge(win_done, n + 1)
                total = wins[:, g, :]
                head, tail = slice(BUF, BUF + max(WINDOWS)), slice(BUF + max(WINDOWS), LINE)
                step(dve.tensor_tensor(rstd[:, 0:max(WINDOWS)], total[:, head], inv_cnt[:, g, :], ALU.mult))
                dve.tensor_tensor(line[:, g, head], rstd[:, 0:max(WINDOWS)], line[:, g, head], ALU.subtract)
                dve.scalar_tensor_tensor(out=line[:, g, tail], in0=total[:, tail], scalar=1.0 / WINDOWS[g],
                                         in1=line[:, g, tail], op0=ALU.mult, op1=ALU.subtract).then_inc(z_done, 1)

            def grouped(name):
                for g in GROUPS[name]:
                    dve.wait_ge(att_free, freed_before(name) + 2 * (g - GROUPS[name][0]) + 2)
                    dve.tensor_tensor(pz_lo[:, g, :], scaled[:, g % 3, :], pz_hi[:, g, :], ALU.subtract) \
                        .then_inc(poolz_done, 1)

            def scores(name):
                dve.wait_ge(att_mm, written(name))
                if name in ("Sa", "Sb"):
                    i, kv = NBLK, "ab".index(name[1])
                    if kv == 0:
                        dve.wait_ge(att_mm, written("T2"))
                    for n, (bank, k0, kn) in enumerate(((4, 0, 512), (5, 512, 512), (6, CTXK, NS))):
                        dve.scalar_tensor_tensor(out=p0[:, kv * SKEYS + k0:kv * SKEYS + k0 + kn],
                                                 in0=psum[:, bank, 0:kn], scalar=HD ** -0.5,
                                                 in1=smask[:, k0:k0 + kn], op0=ALU.mult, op1=ALU.add) \
                            .then_inc(att_free, 1)
                    if kv == 0:
                        return
                    pb, hn, sink = p0[:, 0:KV * SKEYS].rearrange("p (h k) -> p h k", h=KV), KV, sinks_s
                else:
                    i = int(name[1])
                    if i == 0:
                        dve.wait_ge(side_stored, 16 * SIDE_STORES)
                    k0 = WIN if i == 0 else 0
                    pb = (p0, p1)[i % 2][:, 0:H * 2 * WIN].rearrange("p (h k) -> p h k", h=H)[:, :, k0:2 * WIN]
                    hn, sink = H, sinks
                    mask = band[:, k0:2 * WIN].rearrange("p (a k) -> p a k", a=1).broadcast_to([P, 2, 2 * WIN - k0])
                    for b in range(4):
                        src = psum[:, 4 + b, :].rearrange("p (h k) -> p h k", h=2)[:, :, k0:2 * WIN]
                        dve.scalar_tensor_tensor(out=pb[:, 2 * b:2 * b + 2, :], in0=src, scalar=HD ** -0.5, in1=mask,
                                                 op0=ALU.mult, op1=ALU.add).then_inc(att_free, 1)
                dve.wait_ge(att_free, freed(name))
                st = soft[:, i % 2]
                step(dve.tensor_reduce(st[:, MAX, 0:hn], pb, AX.X, ALU.max))
                step(dve.tensor_tensor(st[:, MAX, 0:hn], st[:, MAX, 0:hn], sink[:, 0:hn], ALU.max))
                dve.tensor_scalar(st[:, NEG_MAX, 0:hn], st[:, MAX, 0:hn], -1.0, None, ALU.mult)
                dve.tensor_tensor(st[:, SINK, 0:hn], sink[:, 0:hn], st[:, MAX, 0:hn], ALU.subtract) \
                    .then_inc(neg_done, 1)

            def divide(i):
                dve.wait_ge(exp_done, i + 1)
                st = soft[:, i % 2]
                if i == NBLK:
                    pb, hn = p0[:, 0:KV * SKEYS].rearrange("p (h k) -> p h k", h=KV), KV
                else:
                    k0 = WIN if i == 0 else 0
                    pb = (p0, p1)[i % 2][:, 0:H * 2 * WIN].rearrange("p (h k) -> p h k", h=H)[:, :, k0:2 * WIN]
                    hn = H
                step(dve.tensor_tensor(st[:, DEN, 0:hn], st[:, SUM, 0:hn], st[:, SINK, 0:hn], ALU.add))
                step(dve.reciprocal(st[:, REC, 0:hn], st[:, DEN, 0:hn]))
                for h in range(hn):
                    ins = dve.tensor_scalar(pb[:, h, :], pb[:, h, :], st[:, REC, h:h + 1], None, ALU.mult)
                ins.then_inc(prob_done, 1)

            def attended(name):
                dve.wait_ge(att_mm, written(name))
                if name == "PVs":
                    t0, n = SEQ, NS
                else:
                    t0, n = int(name[2]) * WIN, WIN
                o = psum[:, 4, 0:GQ * n].rearrange("p (j t) -> p j t", j=GQ)
                step(dve.tensor_copy(att_hi[:, :, t0:t0 + n], o))
                dve.tensor_tensor(att_lo[:, :, t0:t0 + n], o, att_hi[:, :, t0:t0 + n], ALU.subtract) \
                    .then_inc(att_free, 1)

            for s in range(MIX1 + LAG):
                if s < MIX1:
                    epilogue(s, 0)
                if s == 0:
                    norm_scale(0, 1)
                if s >= LAG:
                    epilogue(s - LAG, 1)
                    split(MIX_BASE + s + 2, unit_kind(MIX_BASE + s + 2))
                for name in STAGES.get(s, []):
                    if name in GROUPS:
                        grouped(name)
                    elif name[0] == "S":
                        scores(name)
                    elif name[0:2] == "PV":
                        attended(name)
                for g in POOLED_AT.get(s, ()):
                    pooled(g)
                if s in EXP_AT:
                    divide(EXP_AT.index(s))
            for s in range(KD + LAG):
                if s < KD:
                    residual(WO_BASE + s, 0, s, ALPHA)
                if s >= LAG:
                    residual(WO_BASE + s - LAG, 1, s - LAG, ALPHA)
                    split(WO_BASE + s + 2, unit_kind(WO_BASE + s + 2))
                if s == KD - 1:
                    norm_center(1, 0)
                if s == KD:
                    norm_scale(1, 0)
            norm_center(1, 1)
            ffn(2, FFN2_BASE, 2 * KF)
            norm_center(2, 1)
            norm_scale(2, 1)

        @block.tensor
        def _(pe):
            def weights(s, k, hi):
                if k < KD:
                    return (ring_hi if hi else ring_lo)[:, s, k, :]
                return (ext_hi if hi else ext_lo)[:, s, k - KD, :]

            def part(u, c, kn, x_hi, x_lo, at=None, ready=None):
                s = (u if at is None else at) % SLOTS
                banks = 2 if MIX_BASE <= (u if at is None else at) < FFN2_BASE else 4
                bank = bank_of(u if at is None else at, c)
                pe.wait_ge(lo_done, u + 1)
                if at is not None or u >= banks:
                    pe.wait_ge(evac[c], u - (banks - 1))
                for k in range(kn):
                    if ready:
                        ready(k)
                    o = psum[:, bank, 0:C]
                    pe.matmul(o, weights(s, k, True), x_hi[:, k, tok(c)], start=k == 0, stop=False)
                    pe.matmul(o, weights(s, k, True), x_lo[:, k, tok(c)], start=False, stop=False)
                    ins = pe.matmul(o, weights(s, k, False), x_hi[:, k, tok(c)], start=False, stop=k == kn - 1)
                ins.then_inc(mm_done[c], 1)

            def act_wait(l, c):
                return lambda k: pe.wait_ge(act_ready[c], (KD // 2) * l + k // 2 + 1) if k % 2 == 0 else None

            def mean(l, c):
                pe.wait_ge(fsum_done[c], l + 1)
                pe.wait_ge(consts_in, 16 * CONST_DMAS)
                pe.matmul(psum[:, stat_bank(l, c), 0:C], mean_w[:, 0:P], fsum[:, c, :], start=True, stop=True) \
                    .then_inc(mean_done[c], 1)

            def variance(l, c):
                pe.wait_ge(sqsum_done, 2 * l + c + 1)
                pe.matmul(psum[:, stat_bank(l, c), 0:C], mean_w[:, 0:P], sq[:, 0, :], start=True, stop=True) \
                    .then_inc(var_done, 1)

            def ffn(l, base, act_l, hid_n):
                for half in range(2):
                    b = base + half * (UP + DOWN)
                    fresh = half == 0

                    def up(s, u, c):
                        ready = act_wait(act_l, c) if isinstance(u, int) and u == base else None
                        part(u, c, KD, act_hi, act_lo, at=s, ready=ready)

                    def up_static(s, c):
                        part(b + s, c, KD, act_hi, act_lo, ready=act_wait(act_l, c) if fresh and s == 0 else None)

                    up_static(0, 0)
                    if l == 0 and half == 0:
                        for i in range(3, len(TOK_TILES)):
                            turn_in(i)
                    up_static(1, 0)
                    if l == 0 and half == 0:
                        pe.wait_ge(turn_read, len(TOK_TILES))
                    if l == 2 and half == 0:
                        variance(1, 1)
                    for s in range(LAG, LAG + 4):
                        up_static(s, 0)
                        up_static(s - LAG, 1)
                    with pe.Fori(0, 4) as i:
                        for j in range(4):
                            s = LAG + 4 + j
                            part(i * 4 + (b + s), 0, KD, act_hi, act_lo, at=b + s)
                            part(i * 4 + (b + s - LAG), 1, KD, act_hi, act_lo, at=b + s - LAG)
                    for s in range(UP, UP + LAG):
                        up_static(s - LAG, 1)
                    b += UP
                    if l == 0 and half == 0:
                        pe.wait_ge(vec_in, 16 * VEC_DMAS)
                        pe.wait_ge(evac[0], b - 2)
                        pe.transpose(psum[:, VEC_BANK, 0:VEC_ROWS], vec_rows, ident[0:VEC_ROWS, 0:VEC_ROWS]) \
                            .then_inc(turn_done, 1)

                    def hid_wait(c):
                        return lambda k: pe.wait_ge(hid_done[c], hid_n + k + 1)

                    for s in range(DOWN + LAG):
                        if l == 0 and half == 0 and s == 1:
                            pe.wait_ge(vecs_done, 1)
                        if s < DOWN:
                            part(b + s, 0, KF, hid_hi, hid_lo, ready=hid_wait(0) if s == 0 else None)
                        if s >= LAG:
                            part(b + s - LAG, 1, KF, hid_hi, hid_lo, ready=hid_wait(1) if s == LAG else None)
                        if half == 1 and s == DOWN - 1:
                            mean(l, 0)
                        if half == 1 and s == DOWN:
                            variance(l, 0)
                    hid_n += KF
                mean(l, 1)

            def turn_in(i):
                t0, n, _ = TOK_TILES[i]
                pe.wait_ge(x_in[i], 16)
                if i >= 3:
                    pe.wait_ge(turn_read, i - 2)
                for o in range(KD):
                    ins = pe.transpose(psum[:, in_bank(i) + o // 4, (o % 4) * n:(o % 4 + 1) * n],
                                       xin[0:n, i, o * P:(o + 1) * P], ident[0:n, 0:n])
                ins.then_inc(turn_done, 1)

            def turn_out(i, t0, n, c):
                pe.wait_ge(aff_done, KD * (4 + c + 1))
                if c == 0:
                    pe.wait_ge(evac[0], UNITS)
                if i >= 3:
                    pe.wait_ge(yout_done, 2 * (i - 3) + 2)
                for o in range(KD):
                    ins = pe.transpose(psum[0:n, out_bank(i) + o // 4, (o % 4) * P:(o % 4 + 1) * P],
                                       y[:, o, t0:t0 + n], ident[:, :])
                ins.then_inc(turn_done, 1)

            pe.wait_ge(ident_in, 16)
            for i in range(3):
                turn_in(i)
            ffn(0, 0, 0, 0)

            def attend(name):
                if name != ROUNDS[0]:
                    pe.wait_ge(att_free, freed_before(name))
                if name == "poolctx":
                    pe.wait_ge(evac[1], FFN_UNITS)
                    pe.wait_ge(mixer_in, 16 * MIXER_DMAS)
                    for g in range(NG):
                        ins = pe.transpose(psum[:, 4, g * P:g * P + DB * BUF], uctx[0:DB * BUF, g * P:(g + 1) * P],
                                           ident[0:DB * BUF, 0:DB * BUF])
                elif name == "kctx":
                    for b in range(DB):
                        ins = pe.transpose(psum[:, 5 + b // 4, (b % 4) * P:(b % 4 + 1) * P], kctx[b // 4][:, b % 4, :],
                                           ident[:, :])
                elif name == "uout":
                    for c in range(2):
                        pe.wait_ge(evac[c], MIX_BASE + NG)
                    for g in range(NG):
                        pe.transpose(psum[0:BUF, 4, g * P:(g + 1) * P], line[:, g, SEQ:SEQ + BUF], ident[:, :])
                        ins = pe.transpose(psum[0:NS, 5, g * P:(g + 1) * P], u_new[:, g, :], ident[:, :])
                elif name == "vkout":
                    for c in range(2):
                        pe.wait_ge(evac[c], MIX_BASE + U_K + 1)
                    for n in range(NBLK):
                        pe.transpose(psum[:, 4, n * P:(n + 1) * P], vT[:, n * WIN:(n + 1) * WIN], ident[:, :])
                    pe.transpose(psum[0:NS, 5, 0:P], vT[:, SEQ:T], ident[:, :])
                    pe.transpose(psum[:, 6, 0:P], kT[:, SEQ - WIN:SEQ], ident[:, :])
                    ins = pe.transpose(psum[0:NS, 7, 0:P], kT[:, SEQ:T], ident[:, :])
                elif name in GROUPS:
                    pe.wait_ge(z_done, NG)
                    for i, g in enumerate(GROUPS[name]):
                        z = line[:, g, :]
                        w = grp_w[:, g, :]
                        n = SEQ - C
                        seg = z[:, BUF + SEQ:LINE].rearrange("p (b s) -> p b s", s=SEG)[:, :, BUF:SEG]
                        pe.matmul(psum[:, 4 + 2 * i, 0:C], w, z[:, BUF:BUF + C], start=True, stop=True)
                        pe.matmul(psum[:, 5 + 2 * i, 0:n], w, z[:, BUF + C:BUF + SEQ], start=True, stop=True)
                        ins = pe.matmul(psum[:, 5 + 2 * i, n:C], w, seg, start=True, stop=True)
                elif name in ("Sa", "Sb"):
                    kv = "ab".index(name[1])
                    h = slice(kv * HD, (kv + 1) * HD)
                    q = q_new[h, :]
                    pe.wait_ge(q_new_done, 1)
                    pe.matmul(psum[:, 4, :], q, kctxT[h, 0:512], start=True, stop=True)
                    pe.matmul(psum[:, 5, :], q, kctxT[h, 512:1024], start=True, stop=True)
                    ins = pe.matmul(psum[:, 6, 0:NS], q, kT[h, SEQ:T], start=True, stop=True)
                elif name[0] == "S":
                    n = int(name[1])
                    if n in (0, 2):
                        pe.wait_ge(evac[n // 2], MIX_BASE + U_GA)
                    k0 = WIN if n == 0 else 0
                    keys = slice((n - 1) * WIN + k0, (n + 1) * WIN)
                    for kv in range(KV):
                        h = slice(kv * HD, (kv + 1) * HD)
                        for j in range(GQ):
                            at = (j % 2) * 2 * WIN
                            ins = pe.matmul(psum[:, 4 + 2 * kv + j // 2, at + k0:at + 2 * WIN],
                                            qT[h, j, n * WIN:(n + 1) * WIN], kT[h, keys], start=True, stop=True)
                elif name in ("Ta", "Tb"):
                    kv = "ab".index(name[1])
                    pe.wait_ge(prob_done, NBLK + 1)
                    pk = p0[:, kv * SKEYS:(kv + 1) * SKEYS]
                    for b in range(DB):
                        pe.transpose(psum[:, 4 + b // 4, (b % 4) * P:(b % 4 + 1) * P], pk[:, b * WIN:(b + 1) * WIN],
                                     ident[:, :])
                    ins = pe.transpose(psum[0:NS, 6, 0:P], pk[:, CTXK:SKEYS], ident[:, :])
                elif name[0] == "T":
                    n = int(name[1])
                    pe.wait_ge(prob_done, n + 1)
                    pb = (p0, p1)[n % 2][:, 0:H * 2 * WIN].rearrange("p (h k) -> p h k", h=H)
                    for kt in range(1 if n == 0 else 0, 2):
                        for h in range(H):
                            ins = pe.transpose(psum[:, 4 + 2 * kt + h // GQ, (h % GQ) * P:(h % GQ + 1) * P],
                                               pb[:, h, kt * WIN:(kt + 1) * WIN], ident[:, :])
                elif name == "PVs":
                    for kv in range(KV):
                        h = slice(kv * HD, (kv + 1) * HD)
                        pk = pT[:, kv * (DB + 1) * P:(kv + 1) * (DB + 1) * P]
                        for b in range(DB):
                            pe.matmul(psum[h, 4, 0:P], vctx[:, b, h], pk[:, b * P:(b + 1) * P], start=b == 0, stop=False)
                        ins = pe.matmul(psum[h, 4, 0:P], vN[0:NS, NBLK, h], pk[0:NS, CTXK:CTXK + P], start=False,
                                        stop=True)
                else:
                    n = int(name[2])
                    first = 1 if n == 0 else 0
                    for kv in range(KV):
                        h = slice(kv * HD, (kv + 1) * HD)
                        for kt in range(first, 2):
                            ins = pe.matmul(psum[h, 4, :], vN[:, n - 1 + kt, h],
                                            pT[:, (2 * kt + kv) * 512:(2 * kt + kv + 1) * 512], start=kt == first,
                                            stop=kt == 1)
                ins.then_inc(att_mm, 1)

            def mix_part(m, c):
                u = MIX_BASE + m
                if not is_proj(m):
                    part(u, c, KD, act_hi, act_lo, ready=act_wait(1, c) if m == 0 else None)
                elif m < U_GB:
                    if m == U_PA:
                        pe.wait_ge(poolz_done, NG)
                    part(u, c, NG, pz_hi, pz_lo)
                else:
                    if m == U_GB + 1:
                        pe.wait_ge(att_free, freed("PVs" if c else "PV2"))
                    part(u, c, NG, att_hi, att_lo)

            for s in range(MIX1 + LAG):
                if s < MIX1:
                    mix_part(s, 0)
                if s == 1:
                    variance(0, 1)
                if s >= LAG:
                    mix_part(s - LAG, 1)
                for name in STAGES.get(s, []):
                    attend(name)
            for s in range(KD + LAG):
                def m_wait(c):
                    return lambda k: pe.wait_ge(m_done[c], k + 1)
                if s < KD:
                    part(WO_BASE + s, 0, KD, m_hi, m_lo, ready=m_wait(0) if s == 0 else None)
                if s >= LAG:
                    part(WO_BASE + s - LAG, 1, KD, m_hi, m_lo, ready=m_wait(1) if s == LAG else None)
                if s == KD - 1:
                    mean(1, 0)
                if s == KD:
                    variance(1, 0)
            mean(1, 1)
            ffn(2, FFN2_BASE, 2, 2 * KF)
            for i, (t0, n, c) in enumerate(TOK_TILES):
                if i == 3:
                    variance(2, 1)
                turn_out(i, t0, n, c)


VEC_BANK = (UP + 1) % 4


def in_bank(i):
    return 2 + 2 * (i % 3)


def out_bank(i):
    return 2 * (i % 3)


CONST_DMAS = 4 + GQ
MIXER_DMAS = 7
VEC_DMAS = 7
VEC_ROWS = 6 * KD + NG
SIDE_STORES = 3 + 1 + DB + 2 + 2 * DB


def constants():
    f = np.float32
    tok_pos = np.concatenate([np.arange(SEQ), PAST + np.tile(np.arange(DS), DB)]).astype(f)
    freqs = f(THETA) ** (f(-2.0) * np.arange(HD // 2, dtype=f) / f(HD))
    ang = tok_pos[None, :] * freqs[:, None].astype(f)
    cos, sin = np.cos(ang), np.sin(ang)
    cos_sin = np.stack([np.concatenate([cos, cos] * KV), np.concatenate([sin, -sin] * KV)], axis=1).astype(f)
    q = np.arange(WIN)[:, None]
    k = np.arange(WIN)[None, :]
    band = np.concatenate([np.where(k >= q, 0, NEG), np.where(k <= q, 0, NEG)], axis=1).astype(f)
    b, t = np.arange(P)[:, None] % NS // DS, np.arange(P)[:, None] % DS
    ck, nk = np.arange(CTXK)[None, :], np.arange(NS)[None, :]
    smask = np.concatenate([np.where((ck // WIN == b) & (ck % WIN >= t), 0, NEG),
                            np.where((nk // DS == b) & (nk % DS <= t), 0, NEG)], axis=1).astype(f)
    cnt = np.stack([np.minimum(np.arange(max(WINDOWS)) + 1, w) for w in WINDOWS])
    inv = np.broadcast_to((1.0 / cnt).astype(f), (P, NG, max(WINDOWS)))
    return {"c_ident": np.eye(P, dtype=f), "c_mean": np.concatenate([np.full((P, P), 1.0 / D), np.full((P, 1), EPS)], axis=1).astype(f), "c_cos_sin": cos_sin,
            "c_band": band, "c_smask": smask, "c_inv_cnt": np.ascontiguousarray(inv)}


INS = ["x_prompt", "x_sample", "cache_pool_u", "cache_k_win", "cache_v_win", "w_in", "pool_w_grp", "pool_scale",
       "attn_sinks", "w_pool_out", "w_attn_out", "w_out", "ffn1_w1", "ffn1_w3", "ffn1_w2", "ffn2_w1", "ffn2_w3",
       "ffn2_w2", "ln1_g", "ln1_b", "ln2_g", "ln2_b", "ln3_g", "ln3_b"]
OUTS = {"y_prompt": (1, SEQ, D), "y_sample": (DB, DS, D), "pool_u_prompt": (1, 1, BUF, POOLW),
        "k_win_prompt": (1, 1, WIN, KV, HD), "v_win_prompt": (1, 1, WIN, KV, HD),
        "pool_u_sample": (1, DB, BUF, POOLW), "k_win_sample": (1, DB, WIN, KV, HD),
        "v_win_sample": (1, DB, WIN, KV, HD)}


def kernel(**inputs):
    import concourse.bacc as bacc
    from concourse.bass_utils import run_bass_kernel_spmd

    nc = bacc.Bacc("TRN2", target_bir_lowering=False, num_devices=1)
    arrays = {name: np.ascontiguousarray(inputs[name]) for name in INS}
    arrays.update(constants())
    a = {name: nc.dram_tensor(f"in_{name}", v.shape, F32, kind="ExternalInput").ap() for name, v in arrays.items()}
    out = {name: nc.dram_tensor(f"out_{name}", shape, F32, kind="ExternalOutput").ap() for name, shape in OUTS.items()}
    program(nc, a, out)
    r = run_bass_kernel_spmd(nc, [{f"in_{name}": v for name, v in arrays.items()}], core_ids=[0])
    return tuple(r.results[0][f"out_{name}"] for name in OUTS)
```

```python
from contextlib import ExitStack

import numpy as np

import concourse.bass as bass
from concourse import mybir

P = 128
D = 1024
KD = D // P
SEQ = 512
DB, DS = 8, 4
NS = DB * DS
T = SEQ + NS
C = T // 2
PAST = 2048
FF = 2816
KF = FF // P // 2
POOLW = 512
WINDOWS = (2, 4, 8, 16)
NG = len(WINDOWS)
BUF = 15
SEG = BUF + DS
LINE = BUF + SEQ + DB * SEG
H, KV, HD = 8, 2, 64
GQ = H // KV
WIN = 128
NBLK = SEQ // WIN
CTXK = DB * WIN
SKEYS = CTXK + NS
QOFF, KOFF = POOLW, POOLW + H * HD
VOFF, GOFF = KOFF + KV * HD, KOFF + 2 * KV * HD
ALPHA = 2.0 ** 0.25
EPS = 1e-5
THETA = 10000.0
NEG = -1e30

SLOTS = 4
RAWS = 4
LAST_AFFINE = 5
LAG = 2
UP, DOWN = 2 * KF, KD
MIX1 = 42
FFN_UNITS = 2 * (UP + DOWN)
MIX_BASE = FFN_UNITS
WO_BASE = MIX_BASE + MIX1
FFN2_BASE = WO_BASE + KD
UNITS = FFN2_BASE + FFN_UNITS

F32 = mybir.dt.float32
F32R = mybir.dt.float32r
ALU = mybir.AluOpType
ACT = mybir.ActivationFunctionType
AX = mybir.AxisListType

U_V, U_K, U_Q, U_GA, U_PA, U_GB = 4, 5, 6, 10, 18, 26
TOK_TILES = [(0, 128, 0), (128, 128, 0), (256, 16, 0), (272, 128, 1), (400, 112, 1), (512, 32, 1)]
STAGES = {1: ["poolctx"], 1.5: ["kctx"], 6: ["uout"], 8: ["vkout"], 9: ["grp0"], 10: ["grp1"], 10.5: ["S0"],
          11.5: ["S1"], 13: ["T0"], 14: ["S2"], 14.5: ["PV0"], 15: ["T1"], 16: ["S3"], 16.5: ["PV1"], 17: ["T2"],
          18: ["PV2"], 19: ["Sa"], 20.5: ["Sb"], 21: ["T3"], 22: ["PV3"], 24: ["Ta"], 25: ["Tb"], 27: ["PVs"]}
POOLED_AT = {7: (3, 2), 8: (1, 0)}
EXP_AT = [11, 12, 14.5, 17, 21]
DIVIDE_AT = [12, 13, 15, 18, 22.5]
GROUPS = {"grp0": (3, 2), "grp1": (1, 0)}
ROUNDS = [name for step in sorted(STAGES) for name in STAGES[step]]
READS = {"poolctx": NG, "kctx": 2, "uout": 2, "grp0": 4, "grp1": 4, "vkout": 4, "Sa": 3, "Sb": 3, "Ta": 3, "Tb": 3,
         "T0": 2, "PVs": 1}
READS |= {f"S{n}": 4 for n in range(NBLK)} | {f"T{n}": 4 for n in range(1, NBLK)} | {f"PV{n}": 1 for n in range(NBLK)}


def freed(name):
    return sum(READS[r] for r in ROUNDS[:ROUNDS.index(name) + 1])


def freed_before(name):
    return freed(name) - READS[name]


def written(name):
    return ROUNDS.index(name) + 1


def is_proj(m):
    return U_PA <= m < U_GB or m >= U_GB and (m - U_GB) % 2 == 1


def program(nc, a, out):
    ctx = ExitStack()
    with ctx:
        def sb(name, shape, dt=F32, where=None):
            return (where or ctx).enter_context(nc.sbuf_tensor(name, shape, dt))

        def sem(name):
            return ctx.enter_context(nc.semaphore(name))

        act_hi = sb("act_hi", [P, KD, T], F32R)
        act_lo = sb("act_lo", [P, KD, T], F32R)
        y = sb("y", [P, KD, T])
        ring_hi = sb("ring_hi", [P, SLOTS, KD, P], F32R)
        ring_lo = sb("ring_lo", [P, SLOTS, KD, P], F32R)
        raw = sb("raw", [P, RAWS, KD, P])
        band = sb("band", [P, 2 * WIN])
        smask = sb("smask", [P, SKEYS])
        ident = sb("ident", [P, P])
        mean_w = sb("mean_w", [P, P + 1])
        inv_cnt = sb("inv_cnt", [P, NG, max(WINDOWS)])
        vecs = sb("vecs", [P, VEC_ROWS])
        ln_gb = vecs[:, 0:6 * KD].rearrange("p (i k) -> p i k", i=6)
        pscale = vecs[:, 6 * KD:VEC_ROWS]
        sinks = sb("sinks", [P, H])
        sinks_s = sb("sinks_s", [P, KV])
        soft = sb("soft", [P, 2, 6, H])
        fsum = sb("fsum", [P, 2, C])
        stat = sb("stat", [P, 2, C])
        table = sb("table", [P, 3])
        p0 = sb("p0", [P, KD * C])
        tmp_a = sb("tmp_a", [P, 2, C])
        tmp_v = sb("tmp_v", [P, 2, C])
        sq = p0[:, :].rearrange("p (o t) -> p o t", o=KD)
        tmp_r, scratch = stat[:, 1, :], stat[:, 0, 0:max(WINDOWS)]
        vec_rows = p0[0:VEC_ROWS, 0:P]
        MAX, NEG_MAX, SINK, SUM, DEN, REC = range(6)

        with ExitStack() as ffn_mem:
            ext_hi = sb("ext_hi", [P, SLOTS, KF - KD, P], F32R, ffn_mem)
            ext_lo = sb("ext_lo", [P, SLOTS, KF - KD, P], F32R, ffn_mem)
            ext_raw = sb("ext_raw", [P, RAWS, KF - KD, P], F32, ffn_mem)
            with ExitStack() as x_mem:
                xin = sb("xin", [P, len(TOK_TILES), D], F32, x_mem)
            hid_hi = sb("hid_hi", [P, KF, T], F32R, ffn_mem)
            hid_lo = sb("hid_lo", [P, KF, T], F32R, ffn_mem)
        with ExitStack() as mix_mem:
            m1 = sb("m1", [P, KD, T], F32, mix_mem)
            with ExitStack() as early_mem:
                cos_sin = sb("cos_sin", [P, 2, T], F32, early_mem)
                vT = sb("vT", [P, T], F32, early_mem)
                grp_w = sb("grp_w", [P, NG, P], F32, early_mem)
            att_lo = sb("att_lo", [P, GQ, T], F32R, mix_mem)
            with ExitStack() as q_mem:
                qT = sb("qT", [P, GQ, T], F32, q_mem)
            att_hi = sb("att_hi", [P, GQ, T], F32R, mix_mem)
            with ExitStack() as win_mem:
                wins = sb("wins", [P, NG + 2, LINE], F32, win_mem)
            with ExitStack() as branch_mem:
                pz_hi = sb("pz_hi", [P, NG, T], F32R, branch_mem)
                pz_lo = sb("pz_lo", [P, NG, T], F32R, branch_mem)
                p1 = sb("p1", [P, H * 2 * WIN], F32, branch_mem)
                with ExitStack() as line_mem:
                    line = sb("line", [P, NG, LINE], F32, line_mem)
                pT = sb("pT", [P, 4 * LINE], F32, branch_mem)
                kT = sb("kT", [P, T], F32, branch_mem)
                vN = sb("vN", [P, NBLK + 1, P], F32, branch_mem)
                kctxT = sb("kctxT", [P, CTXK], F32, branch_mem)
                vctx = sb("vctx", [P, DB, P], F32, branch_mem)
                u_new = sb("u_new", [P, NG, NS], F32, branch_mem)
                q_new = sb("q_new", [P, GQ * NS], F32, branch_mem)
            m_hi = sb("m_hi", [P, KD, T], F32R, mix_mem)
            m_lo = sb("m_lo", [P, KD, T], F32R, mix_mem)
        kctx = [m1[:, i, 0:4 * WIN].rearrange("p (b n) -> p b n", n=P) for i in range(2)]
        rows_k = p0[:, 2 * POOLW:2 * POOLW + 2 * P].rearrange("p (a n) -> p a n", a=2)
        scaled = p1[:, 0:3 * T].rearrange("p (g t) -> p g t", g=3)
        uctx = p1[:, 0:POOLW]
        rows_u = p0[:, 0:2 * POOLW].rearrange("p (a n) -> p a n", a=2)
        psum = ctx.enter_context(nc.psum_tensor("psum", [P, 8, 512], F32))

        ident_in = sem("ident_in")
        consts_in = sem("consts_in")
        x_in = [sem(f"x_in{i}") for i in range(len(TOK_TILES))]
        raw_in = [sem(f"raw_in{i}") for i in range(RAWS)]
        vec_in = sem("vec_in")
        vecs_done = sem("vecs_done")
        mixer_in = sem("mixer_in")
        hi_done = sem("hi_done")
        lo_done = sem("lo_done")
        mm_done = [sem(f"mm_done{c}") for c in range(2)]
        evac = [sem(f"evac{c}") for c in range(2)]
        hid_hi_done = [sem(f"hid_hi_done{c}") for c in range(2)]
        hid_done = [sem(f"hid_done{c}") for c in range(2)]
        y_done = [sem(f"y_done{c}") for c in range(2)]
        fsum_done = [sem(f"fsum_done{c}") for c in range(2)]
        shift_mm = [sem(f"shift_mm{c}") for c in range(2)]
        shift_done = [sem(f"shift_done{c}") for c in range(2)]
        dev_done = [sem(f"dev_done{c}") for c in range(2)]
        sq_done = [sem(f"sq_done{c}") for c in range(2)]
        sqsum_done = [sem(f"sqsum_done{c}") for c in range(2)]
        stats_done = [sem(f"stats_done{c}") for c in range(2)]
        var_done = [sem(f"var_done{c}") for c in range(2)]
        std_done = [sem(f"std_done{c}") for c in range(2)]
        center_done = [sem(f"center_done{c}") for c in range(2)]
        rec_done = [sem(f"rec_done{c}") for c in range(2)]
        norm_done = [sem(f"norm_done{c}") for c in range(2)]
        biased = [sem(f"biased{c}") for c in range(2)]
        aff_v_done = sem("aff_v_done")
        aff_done = [sem(f"aff_done{c}") for c in range(2)]
        act_ready = [sem(f"act_ready{c}") for c in range(2)]
        turn_done = sem("turn_done")
        turn_read = sem("turn_read")
        in_hi_done = sem("in_hi_done")
        v_step = sem("v_step")
        win_step = sem("win_step")
        win_done = sem("win_done")
        q_new_done = sem("q_new_done")
        z_done = sem("z_done")
        poolz_done = sem("poolz_done")
        m_done = [sem(f"m_done{c}") for c in range(2)]
        att_mm = sem("att_mm")
        att_free = sem("att_free")
        neg_done = sem("neg_done")
        exp_done = sem("exp_done")
        prob_done = sem("prob_done")
        yout_done = sem("yout_done")
        yout_v_done = sem("yout_v_done")
        side_stored = sem("side_stored")
        stored = sem("stored")

        block = ctx.enter_context(nc.Block())

        def tok(c):
            return slice(c * C, c * C + C)

        def unit_kind(u):
            for base in (0, FFN2_BASE):
                if base <= u < base + FFN_UNITS:
                    return KD if (u - base) % (UP + DOWN) < UP else KF
            m = u - MIX_BASE
            return NG if m < MIX1 and is_proj(m) else KD

        def bank_of(u, c):
            if MIX_BASE <= u < FFN2_BASE:
                return 2 * c + u % 2
            return 4 * c + u % ring_of(u)

        def ring_of(u):
            return 2 if MIX_BASE - DOWN <= u < FFN2_BASE or u >= UNITS - DOWN else 4

        def stat_bank(l, c):
            return 7 if c else (2, 4, 2)[l]

        def sq_slot(c, o):
            return 4 * c + (o if o < 4 else 1 + (o - 4) % 3)

        def splits(b, s, fourth=False):
            norm_follows = b + DOWN in (MIX_BASE, FFN2_BASE, UNITS)
            if s < DOWN or not norm_follows:
                return [b + s + 2] if b + s + 2 < UNITS else []
            if s == DOWN or b + DOWN == UNITS:
                return []
            return [b + DOWN + 2, b + DOWN + 3] if fourth else [b + DOWN + 2]

        SQ_OPS = KD - 2

        def sq_op(l, o):
            return SQ_OPS * l + max(o - 1, 1)

        def y_before(l):
            return (DOWN, 2 * DOWN, 4 * DOWN)[l]

        @block.sync
        def _(sp):
            def w_tiles(w, k0, kn):
                return w[0, k0 * P:(k0 + kn) * P, :].rearrange("(k p) n -> p k n", p=P)

            def load(slot, src, kn, cols):
                first = kn // 2 if kn <= KD else KD
                sp.dma_start(raw[:, slot, 0:first, :], src[:, 0:first, cols]).then_inc(raw_in[slot], 16)
                dst = raw[:, slot, first:kn, :] if kn <= KD else ext_raw[:, slot, :, :]
                sp.dma_start(dst, src[:, first:kn, cols]).then_inc(raw_in[slot], 16)

            def raw_free(u):
                if not isinstance(u, int) or u >= RAWS:
                    sp.wait_ge(lo_done, u - (RAWS - 1))

            def ffn_loads(base, w1, w3, w2):
                w1k, w3k = w_tiles(w1, 0, KD), w_tiles(w3, 0, KD)
                for half in range(2):
                    b, c0 = base + half * (UP + DOWN), half * KF * P
                    for n in range(6):
                        if b + n:
                            raw_free(b + n)
                            load((b + n) % RAWS, (w1k, w3k)[n % 2], KD,
                                 slice(c0 + n // 2 * P, c0 + (n // 2 + 1) * P))
                    with sp.Fori(1, (KF - 1) // 2) as i:
                        for n in range(4):
                            raw_free(i * 4 + (b + 2 + n))
                            load((b + 2 + n) % RAWS, (w1k, w3k)[n % 2], KD,
                                 bass.ds(i * (2 * P) + (c0 + (1 + n // 2) * P), P))
                    w2k = w_tiles(w2, half * KF, KF)
                    with sp.Fori(0, DOWN // 4) as o:
                        for n in range(4):
                            raw_free(o * 4 + (b + UP + n))
                            load((b + UP + n) % RAWS, w2k, KF, bass.ds(o * (4 * P) + n * P, P))

            for i, (t0, n, _) in enumerate(TOK_TILES):
                src = a["x_prompt"][0, t0:t0 + n, :] if t0 < SEQ else a["x_sample"].rearrange("b t d -> (b t) d")
                sp.dma_start(xin[0:n, i, :], src).then_inc(x_in[i], 16)
                if i == 0:
                    sp.dma_start(ident[:, :], a["c_ident"]).then_inc(ident_in, 16)
                if i == 2:
                    load(0, w_tiles(a["ffn1_w1"], 0, KD), KD, slice(0, P))
            ffn_loads(0, a["ffn1_w1"], a["ffn1_w3"], a["ffn1_w2"])

            win_k = w_tiles(a["w_in"], 0, KD)
            wpo_k = w_tiles(a["w_pool_out"], 0, NG)
            wo_k = w_tiles(a["w_out"], 0, KD)
            first_cols = [g * P for g in reversed(range(NG))] + [VOFF, KOFF]
            for m in range(MIX1):
                u = MIX_BASE + m
                slot = u % RAWS
                raw_free(u)
                o = (m - U_GB) // 2 if m >= U_GB else m - (U_PA if m >= U_PA else U_GA)
                if m < U_Q:
                    load(slot, win_k, KD, slice(first_cols[m], first_cols[m] + P))
                elif m < U_GA:
                    for kv in range(KV):
                        c0 = QOFF + kv * GQ * HD + (m - U_Q) * HD
                        sp.dma_start(raw[:, slot, :, kv * HD:(kv + 1) * HD],
                                     win_k[:, :, c0:c0 + HD]).then_inc(raw_in[slot], 16)
                elif not is_proj(m):
                    c0 = GOFF + (m >= U_GB) * D + o * P
                    load(slot, win_k, KD, slice(c0, c0 + P))
                elif m < U_GB:
                    load(slot, wpo_k, NG, slice(o * P, o * P + P))
                else:
                    for kv in range(KV):
                        src = a["w_attn_out"][0, kv * GQ * HD:(kv + 1) * GQ * HD, o * P:o * P + P]
                        sp.dma_start(raw[kv * HD:(kv + 1) * HD, slot, 0:GQ, :],
                                     src.rearrange("(j d) n -> d j n", d=HD)).then_inc(raw_in[slot], 16)
            for o in range(KD):
                raw_free(WO_BASE + o)
                load((WO_BASE + o) % RAWS, wo_k, KD, slice(o * P, o * P + P))
            ffn_loads(FFN2_BASE, a["ffn2_w1"], a["ffn2_w3"], a["ffn2_w2"])

            for i, (t0, n, _) in enumerate(TOK_TILES):
                sp.wait_ge(yout_done, i + 4)
                if i >= 3:
                    sp.wait_ge(yout_v_done, i - 2)
                dst = out["y_prompt"][0, t0:t0 + n, :] if t0 < SEQ else out["y_sample"].rearrange("b t d -> (b t) d")
                sp.dma_start(dst, xin[0:n, i, :]).then_inc(stored, 16)
            sp.wait_ge(stored, 16 * len(TOK_TILES))
            sp.wait_ge(side_stored, 16 * SIDE_STORES)

        @block.gpsimd
        def _(pool):
            pool.wait_ge(x_in[-1], 16)
            for i, name in enumerate(("ln1_g", "ln1_b", "ln2_g", "ln2_b", "ln3_g", "ln3_b")):
                pool.dma_start(p0[i * KD:(i + 1) * KD, 0:P], a[name][0].rearrange("(k p) -> k p", p=P)) \
                    .then_inc(vec_in, 16)
            pool.dma_start(p0[6 * KD:VEC_ROWS, 0:P], a["pool_scale"][0].rearrange("(g p) -> g p", p=P)) \
                .then_inc(vec_in, 16)
            loads = [(mean_w[:, :], a["c_mean"]), (band[:, :], a["c_band"]), (smask[:, :], a["c_smask"]),
                     (sinks[:, :], a["attn_sinks"][0:1, :].broadcast_to([P, H]))]
            for j in range(GQ):
                src = a["attn_sinks"][0:1, :].rearrange("a (k j) -> a j k", j=GQ)[:, j, :]
                loads.append((sinks_s[j * NS:(j + 1) * NS, :], src.broadcast_to([NS, KV])))
            assert len(loads) == CONST_DMAS
            for dst, src in loads:
                pool.dma_start(dst, src, allow_slow_non_contiguous=True).then_inc(consts_in, 16)

            def norm_sums(l, c, o):
                if 1 <= o < KD - 1:
                    pool.wait_ge(y_done[c], y_before(l) + o + 1)
                    if o > 1:
                        pool.wait_ge(fsum_done[c], (KD - 2) * l + o - 1)
                    elif l:
                        pool.wait_ge(stats_done[c], l)
                    if o == 2:
                        pool.wait_ge(shift_mm[c], l + 1)
                    first = y[:, 0, tok(c)] if o == 1 else fsum[:, c, :]
                    pool.tensor_tensor(fsum[:, c, :], first, y[:, o, tok(c)], ALU.add).then_inc(fsum_done[c], 1)
                for k in range(1 if o == 3 else o, o + 1) if 3 <= o < KD - 1 else ():
                    pool.wait_ge(sq_done[c], sq_op(l, k))
                    if k > 1:
                        pool.wait_ge(sqsum_done[c], (KD - 2) * l + k - 1)
                    total = sq[:, 4 * c, :]
                    pool.tensor_tensor(total, total, sq[:, sq_slot(c, k), :], ALU.add).then_inc(sqsum_done[c], 1)

            def all_norm_sums(l):
                for s in range(DOWN + LAG):
                    norm_sums(l, 0, s)
                    norm_sums(l, 1, s - LAG)

            pool.wait_ge(mm_done[0], UP)
            for name, src, n in (("k_win_sample", "cache_k_win", WIN), ("v_win_sample", "cache_v_win", WIN),
                                 ("pool_u_sample", "cache_pool_u", BUF)):
                pool.dma_start(out[name][0, :, 0:n - DS], a[src][0, :, DS:n]).then_inc(side_stored, 16)

            def add_bias(l):
                for c in range(2):
                    for o in range(KD):
                        pool.wait_ge(act_ready[c], KD * (l + 1) + o + 1)
                        pool.tensor_scalar(y[:, o, tok(c)], y[:, o, tok(c)], ln_gb[:, 2 * l + 1, o:o + 1], None,
                                           ALU.add).then_inc(biased[c], 1)

            all_norm_sums(0)

            pool.wait_ge(mm_done[0], FFN_UNITS)
            pool.wait_ge(mm_done[1], FFN_UNITS)
            pool.memset(line[:, :, 0:BUF], 0.0).then_inc(win_step, 1)
            pool.dma_start(uctx[0:DB * BUF, :], a["cache_pool_u"][0].rearrange("b t w -> (b t) w")) \
                .then_inc(mixer_in, 16)
            for i in range(2):
                pool.dma_start(kctx[i], a["cache_k_win"][0, 4 * i:4 * i + 4].rearrange("b t h d -> t b (h d)")) \
                    .then_inc(mixer_in, 16)
            pool.dma_start(vctx[:, :, :], a["cache_v_win"][0].rearrange("b t h d -> t b (h d)")).then_inc(mixer_in, 16)
            pool.dma_start(inv_cnt[:, :, :], a["c_inv_cnt"]).then_inc(mixer_in, 16)
            pool.dma_start(cos_sin[:, :, :], a["c_cos_sin"]).then_inc(mixer_in, 16)
            pool.dma_start(grp_w[:, :, :], a["pool_w_grp"][0].rearrange("g c d -> c g d")).then_inc(mixer_in, 16)

            add_bias(0)
            pool.wait_ge(att_free, freed("poolctx"))
            steps = 1
            for n, g in enumerate(reversed(range(NG))):
                for c in range(2):
                    pool.wait_ge(evac[c], MIX_BASE + n + 1)
                pool.wait_ge(win_step, steps)
                if n:
                    pool.wait_ge(win_done, n)
                src = line[:, g, :]
                for i in range(g + 1):
                    sh = 1 << i
                    lo = 2 * sh - 1
                    if i:
                        pool.wait_ge(win_step, steps)
                    dst = wins[:, 2 + n if i == g else i % 2, :]
                    ins = pool.tensor_tensor(dst[:, lo:LINE], src[:, lo:LINE], src[:, lo - sh:LINE - sh], ALU.add)
                    ins.then_inc(win_done if i == g else win_step, 1)
                    steps += i < g
                    src = dst

            pool.wait_ge(att_free, freed("uout"))
            pool.dma_start(out["pool_u_prompt"][0, 0], rows_u[0:BUF, 0, :]).then_inc(side_stored, 16)
            for b in range(DB):
                pool.dma_start(out["pool_u_sample"][0, b, BUF - DS:BUF], rows_u[b * DS:(b + 1) * DS, 1, :]) \
                    .then_inc(side_stored, 16)
            pool.wait_ge(att_free, freed("vkout"))
            for name, row in (("k_win_prompt", rows_k[:, 0, :]), ("v_win_prompt", vN[:, NBLK - 1, :])):
                pool.dma_start(out[name][0, 0].rearrange("t h d -> t (h d)"), row).then_inc(side_stored, 16)
            for name, row in (("k_win_sample", rows_k[0:NS, 1, :]), ("v_win_sample", vN[0:NS, NBLK, :])):
                for b in range(DB):
                    pool.dma_start(out[name][0, b, WIN - DS:WIN].rearrange("t h d -> t (h d)"),
                                   row[b * DS:(b + 1) * DS]).then_inc(side_stored, 16)

            all_norm_sums(1)
            add_bias(1)
            all_norm_sums(2)

        @block.scalar
        def _(act):
            def split(u, kn, at=None):
                s, r = (u if at is None else at) % SLOTS, (u if at is None else at) % RAWS
                act.wait_ge(raw_in[r], u * (32 // RAWS) + (32 - r * (32 // RAWS)))
                if at is not None or u >= SLOTS:
                    act.wait_ge(mm_done[1], u - (SLOTS - 1))
                n = min(kn, KD)
                ins = act.activation(ring_hi[:, s, 0:n, :], raw[:, r, 0:n, :], ACT.Copy)
                if kn > KD:
                    ins = act.activation(ext_hi[:, s, :, :], ext_raw[:, r, :, :], ACT.Copy)
                ins.then_inc(hi_done, 1)

            def norm_beside(l, c, o):
                if o == 2:
                    act.wait_ge(shift_mm[c], l + 1)
                    act.activation(stat[:, c, :], psum[:, stat_bank(l, c), 0:C], ACT.Copy, scale=D / (2.0 * P)) \
                        .then_inc(shift_done[c], 1)
                    if c == 0:
                        act.activation(table[:, l:l + 1], mean_w[:, P:P + 1], ACT.Sqrt)
                if o >= 3:
                    for k in (2, 3) if o == 3 else (o,):
                        act.wait_ge(dev_done[c], sq_op(l, k))
                        x = sq[:, 4 * c:4 * c + 3, :] if k == 2 else sq[:, sq_slot(c, k), :]
                        act.activation(x, x, ACT.Square).then_inc(sq_done[c], 1)

            def norm_std(l, c):
                act.wait_ge(var_done[c], l + 1)
                act.activation(stat[:, c, :], stat[:, c, :], ACT.Sqrt, bias=mean_w[:, P:P + 1]) \
                    .then_inc(std_done[c], 1)

            def norm_affine(l, c):
                for o in range(LAST_AFFINE if (l, c) == (2, 1) else KD):
                    bias = ln_gb[:, 2 * l + 1, o:o + 1]
                    act.wait_ge(norm_done[c], KD * l + (o if l < 2 else o // 2) + 1)
                    if l < 2:
                        act.activation(act_hi[:, o, tok(c)], y[:, o, tok(c)], ACT.Identity, bias=bias) \
                            .then_inc(aff_done[c], 1)
                    else:
                        act.activation(y[:, o, tok(c)], y[:, o, tok(c)], ACT.Identity, bias=bias,
                                       scale=ln_gb[:, 2 * l, o:o + 1]).then_inc(aff_done[c], 1)

            def through(u, c, func, at=None, scale=1.0):
                act.wait_ge(mm_done[c], u + 1)
                act.wait_ge(evac[c], u)
                act.activation(tmp_a[:, c, :], psum[:, bank_of(u if at is None else at, c), 0:C], func, scale=scale) \
                    .then_inc(evac[c], 1)

            def residual(u, c, n, scale):
                if n:
                    act.wait_ge(y_done[c], n)
                through(u, c, ACT.Copy, scale=scale)

            def ffn(l, base, y_n):
                for half in range(2):
                    b = base + half * (UP + DOWN)

                    def up_step(s, u, kn):
                        if s % 2 == 0 and s < UP:
                            through(u, 0, ACT.Silu, at=b + s)
                        if s % 2 == 0 and s >= LAG:
                            through(u - LAG, 1, ACT.Silu, at=b + s - LAG)
                        if kn:
                            split(u + 2, kn, at=b + s + 2)

                    if y_n:
                        act.wait_ge(y_done[0], y_n)
                        act.wait_ge(y_done[1], y_n)
                    if l == 2 and half == 0:
                        norm_std(1, 1)
                    up_step(0, b, 0)
                    if l == 2 and half == 0:
                        norm_affine(1, 1)
                    with act.Fori(0, 4) as i:
                        for j in range(4):
                            up_step(2 + j, i * 4 + (b + 2 + j), KD)
                    for s in range(18, UP + LAG):
                        up_step(s, b + s, unit_kind(b + s + 2))
                    b += UP
                    if l == 0 and half == 0:
                        act.wait_ge(turn_done, len(TOK_TILES) + 1)
                        act.activation(vecs[:, :], psum[:, VEC_BANK, 0:VEC_ROWS], ACT.Copy).then_inc(vecs_done, 1)
                    for s in range(DOWN + LAG):
                        if s < DOWN:
                            residual(b + s, 0, y_n + s, 0.5)
                            if half == 1:
                                norm_beside(l, 0, s)
                        if half == 1 and s == DOWN:
                            norm_std(l, 0)
                        if s >= LAG:
                            residual(b + s - LAG, 1, y_n + s - LAG, 0.5)
                            if half == 1:
                                norm_beside(l, 1, s - LAG)
                            if half == 1 and s == DOWN + 1:
                                norm_affine(l, 0)
                            for u in splits(b, s, fourth=True):
                                split(u, unit_kind(u))
                    y_n += DOWN

            for i, (t0, n, _) in enumerate(TOK_TILES):
                act.wait_ge(turn_done, i + 1)
                for h in range(2):
                    ins = act.activation(y[:, 4 * h:4 * h + 4, t0:t0 + n],
                                         psum[:, in_bank(i) + h, 0:4 * n].rearrange("p (o t) -> p o t", o=4), ACT.Copy)
                ins.then_inc(turn_read, 1)
                if i in (2, 5):
                    act.wait_ge(turn_read, i + 1)
                    for k in range(KD // 2):
                        pair = slice(2 * k, 2 * k + 2)
                        act.activation(act_hi[:, pair, tok(i // 3)], y[:, pair, tok(i // 3)], ACT.Copy) \
                            .then_inc(in_hi_done, 1)
                        if k == 0:
                            split(3 * (i // 3), KD)
                if i == 2:
                    split(1, KD)
                    split(2, KD)
            ffn(0, 0, 0)

            def epilogue(m, c):
                u = MIX_BASE + m
                bank = bank_of(u, c)
                if m < U_V:
                    act.wait_ge(mm_done[c], u + 1)
                    act.wait_ge(evac[c], u)
                    n = C if c == 0 else SEQ - C
                    ins = act.activation(line[:, NG - 1 - m, BUF + c * C:BUF + c * C + n], psum[:, bank, 0:n], ACT.Copy)
                    if c == 1:
                        seg = line[:, NG - 1 - m, BUF + SEQ:LINE].rearrange("p (b s) -> p b s", s=SEG)[:, :, BUF:SEG]
                        act.activation(seg, psum[:, bank, n:C].rearrange("p (b s) -> p b s", s=DS), ACT.Copy)
                        ins = act.activation(u_new[:, NG - 1 - m, :], psum[:, bank, n:C], ACT.Copy)
                    ins.then_inc(evac[c], 1)
                elif m == U_V:
                    act.wait_ge(mm_done[c], u + 1)
                    act.wait_ge(evac[c], u)
                    act.activation(vT[:, tok(c)], psum[:, bank, 0:C], ACT.Copy).then_inc(evac[c], 1)
                elif U_GA <= m < U_PA:
                    act.wait_ge(mm_done[c], u + 1)
                    act.wait_ge(evac[c], u)
                    act.activation(m1[:, m - U_GA, tok(c)], psum[:, bank, 0:C], ACT.Sigmoid).then_inc(evac[c], 1)
                elif m >= U_GB and not is_proj(m):
                    through(u, c, ACT.Sigmoid)

            def copy_out(dst, src):
                act.activation(dst, src, ACT.Copy).then_inc(att_free, 1)

            def att_copies(name):
                act.wait_ge(att_mm, written(name))
                if name == "poolctx":
                    segs = line[:, :, BUF + SEQ:LINE].rearrange("p g (b s) -> p g b s", s=SEG)
                    for g in range(NG):
                        copy_out(segs[:, g, :, 0:BUF],
                                 psum[:, 4, g * P:g * P + DB * BUF].rearrange("p (b s) -> p b s", s=BUF))
                elif name == "kctx":
                    for h in range(2):
                        copy_out(kctxT[:, 512 * h:512 * h + 512], psum[:, 5 + h, :])
                elif name == "uout":
                    copy_out(rows_u[0:BUF, 0, :], psum[0:BUF, 4, :])
                    copy_out(rows_u[0:NS, 1, :], psum[0:NS, 5, :])
                elif name == "vkout":
                    copy_out(vN[:, 0:NBLK, :], psum[:, 4, :].rearrange("p (n d) -> p n d", d=P))
                    copy_out(vN[0:NS, NBLK, :], psum[0:NS, 5, 0:P])
                    copy_out(rows_k[:, 0, :], psum[:, 6, 0:P])
                    copy_out(rows_k[0:NS, 1, :], psum[0:NS, 7, 0:P])
                elif name in GROUPS:
                    for i, g in enumerate(GROUPS[name]):
                        prod = psum[:, 4 + 2 * i:6 + 2 * i, 0:C]
                        slot = (NG - 1 - g) % 3
                        if g == 0:
                            act.wait_ge(poolz_done, 1)
                        act.activation(scaled[:, slot, :].rearrange("p (c t) -> p c t", c=2), prod, ACT.Copy,
                                       scale=pscale[:, g:g + 1]).then_inc(att_free, 1)
                        act.activation(pz_hi[:, g, :].rearrange("p (c t) -> p c t", c=2), prod, ACT.Copy,
                                       scale=pscale[:, g:g + 1]).then_inc(att_free, 1)
                elif name in ("Ta", "Tb"):
                    k0 = (name == "Tb") * (DB + 1) * P
                    for h in range(2):
                        copy_out(pT[:, k0 + 512 * h:k0 + 512 * h + 512], psum[:, 4 + h, :])
                    copy_out(pT[0:NS, k0 + CTXK:k0 + CTXK + P], psum[0:NS, 6, 0:P])
                elif name[0] == "T":
                    for b in range(2 if name == "T0" else 0, 4):
                        copy_out(pT[:, b * 512:(b + 1) * 512], psum[:, 4 + b, :])

            def exps(i):
                act.wait_ge(neg_done, i + 1)
                st = soft[:, i % 2]
                if i == NBLK:
                    parts = [(p0[:, kv * SKEYS:(kv + 1) * SKEYS], kv) for kv in range(KV)]
                else:
                    pb = (p0, p1)[i % 2][:, 0:H * 2 * WIN].rearrange("p (h k) -> p h k", h=H)
                    parts = [(pb[:, h, (WIN if i == 0 else 0):2 * WIN], h) for h in range(H)]
                for part, h in parts:
                    act.activation(part, part, ACT.Exp, bias=st[:, NEG_MAX, h:h + 1], accum_out=st[:, SUM, h:h + 1])
                act.activation(st[:, SINK, 0:len(parts)], st[:, SINK, 0:len(parts)], ACT.Exp).then_inc(exp_done, 1)

            def beside(at):
                for name in STAGES.get(at, []):
                    if name in ("poolctx", "kctx", "uout", "vkout", *GROUPS) or name[0] == "T":
                        att_copies(name)
                if at in EXP_AT:
                    exps(EXP_AT.index(at))

            for s in range(MIX1 + LAG):
                if s < MIX1:
                    epilogue(s, 0)
                if s == 0:
                    norm_std(0, 1)
                if s == 1:
                    norm_affine(0, 1)
                beside(s - 0.5)
                if s >= LAG:
                    epilogue(s - LAG, 1)
                    split(MIX_BASE + s + 2, unit_kind(MIX_BASE + s + 2))
                beside(s)
            for s in range(KD + LAG):
                if s < KD:
                    residual(WO_BASE + s, 0, y_before(1) + s, 1.0)
                    norm_beside(1, 0, s)
                if s == KD:
                    norm_std(1, 0)
                if s >= LAG:
                    residual(WO_BASE + s - LAG, 1, y_before(1) + s - LAG, 1.0)
                    norm_beside(1, 1, s - LAG)
                    if s == KD + 1:
                        norm_affine(1, 0)
                    for u in splits(WO_BASE, s, fourth=True):
                        split(u, unit_kind(u))
            ffn(2, FFN2_BASE, 3 * DOWN)
            norm_std(2, 1)
            for c in range(2):
                if c:
                    norm_affine(2, 1)
                for h in range(2 - c):
                    act.wait_ge(turn_done, len(TOK_TILES) + 2 + 2 * c + h)
                    for i, (t0, n, _) in list(enumerate(TOK_TILES))[3 * c:3 * c + 3]:
                        act.activation(xin[0:n, i, 512 * h:512 * h + 512], psum[0:n, out_bank(i) + h, :], ACT.Copy) \
                            .then_inc(yout_done, 1)

        @block.vector
        def _(dve):
            steps = [0]

            def step(ins):
                ins.then_inc(v_step, 1)
                steps[0] += 1
                dve.wait_ge(v_step, steps[0])

            def split(u, kn, at=None):
                s, r = (u if at is None else at) % SLOTS, (u if at is None else at) % RAWS
                dve.wait_ge(hi_done, u + 1)
                n = min(kn, KD)
                ins = dve.tensor_tensor(ring_lo[:, s, 0:n, :], raw[:, r, 0:n, :], ring_hi[:, s, 0:n, :], ALU.subtract)
                if kn > KD:
                    ins = dve.tensor_tensor(ext_lo[:, s, :, :], ext_raw[:, r, :, :], ext_hi[:, s, :, :], ALU.subtract)
                ins.then_inc(lo_done, 1)

            def hidden(u, c, n, f, at):
                dve.wait_ge(mm_done[c], u + 1)
                dve.wait_ge(evac[c], u)
                if not isinstance(n, int) or n:
                    dve.wait_ge(hid_done[c], n)
                dve.tensor_tensor(tmp_v[:, c, :], psum[:, bank_of(at, c), 0:C], tmp_a[:, c, :], ALU.mult) \
                    .then_inc(evac[c], 1)
                dve.wait_ge(evac[c], u + 1)
                hi = hid_hi[:, f, tok(c)] if isinstance(f, int) else hid_hi[:, bass.ds(f, 1), tok(c)]
                lo = hid_lo[:, f, tok(c)] if isinstance(f, int) else hid_lo[:, bass.ds(f, 1), tok(c)]
                v = tmp_v[:, c, :] if isinstance(f, int) else tmp_v[:, c:c + 1, :]
                dve.tensor_copy(hi, v).then_inc(hid_hi_done[c], 1)
                dve.wait_ge(hid_hi_done[c], n + 1)
                dve.tensor_tensor(lo, v, hi, ALU.subtract).then_inc(hid_done[c], 1)

            def residual(u, c, o, factor):
                dve.wait_ge(evac[c], u + 1)
                dve.scalar_tensor_tensor(out=y[:, o, tok(c)], in0=y[:, o, tok(c)], scalar=factor,
                                         in1=tmp_a[:, c, :], op0=ALU.mult, op1=ALU.add).then_inc(y_done[c], 1)

            def deviation(l, c, o):
                if o < 3:
                    return
                for k in (2, 3) if o == 3 else (o,):
                    dve.wait_ge(y_done[c], y_before(l) + k + 1)
                    if k == 2:
                        dve.wait_ge(shift_done[c], l + 1)
                        if l:
                            dve.wait_ge(stats_done[c], l)
                        dve.tensor_tensor(sq[:, 4 * c:4 * c + 3, :], y[:, 0:3, tok(c)],
                                          stat[:, c:c + 1, :].broadcast_to([P, 3, C]), ALU.subtract) \
                            .then_inc(dev_done[c], 1)
                    else:
                        if k > 3:
                            dve.wait_ge(sqsum_done[c], (KD - 2) * l + k - 3)
                        dve.tensor_tensor(sq[:, sq_slot(c, k), :], y[:, k, tok(c)], stat[:, c, :], ALU.subtract) \
                            .then_inc(dev_done[c], 1)

            def norm_center(l, c):
                dve.wait_ge(stats_done[c], l + 1)
                bank = stat_bank(l, c)
                s = stat[:, c, :]
                step(dve.tensor_tensor(s, psum[:, bank, 0:C], s, ALU.subtract))
                step(dve.tensor_tensor(s, s, s, ALU.mult))
                dve.tensor_tensor(s, psum[:, bank ^ 1, 0:C], s, ALU.subtract).then_inc(var_done[c], 1)
                mean = psum[:, bank:bank + 1, 0:C].broadcast_to([P, 4, C])
                for i in range(2):
                    half = y[:, 4 * i:4 * i + 4, tok(c)]
                    ins = dve.tensor_tensor(half, half, mean, ALU.subtract)
                ins.then_inc(center_done[c], 1)

            def norm_reciprocal(l, c):
                dve.wait_ge(std_done[c], l + 1)
                dve.reciprocal(stat[:, c, :], stat[:, c, :]).then_inc(rec_done[c], 1)

            def norm_scale(l, c):
                dve.wait_ge(center_done[c], l + 1)
                dve.wait_ge(rec_done[c], l + 1)
                if l == 2:
                    r = stat[:, c:c + 1, :].broadcast_to([P, 2, C])
                    for i in range(KD // 2):
                        pair = y[:, 2 * i:2 * i + 2, tok(c)]
                        dve.tensor_tensor(pair, pair, r, ALU.mult).then_inc(norm_done[c], 1)
                    return
                for o in range(KD + 2):
                    if o < KD:
                        dve.scalar_tensor_tensor(out=y[:, o, tok(c)], in0=y[:, o, tok(c)],
                                                 scalar=ln_gb[:, 2 * l, o:o + 1], in1=stat[:, c, :],
                                                 op0=ALU.mult, op1=ALU.mult).then_inc(norm_done[c], 1)
                    if o >= 2:
                        k = o - 2
                        dve.wait_ge(aff_done[c], KD * l + k + 1)
                        dve.scalar_tensor_tensor(out=act_lo[:, k, tok(c)], in0=y[:, k, tok(c)],
                                                 scalar=ln_gb[:, 2 * l + 1, k:k + 1], in1=act_hi[:, k, tok(c)],
                                                 op0=ALU.add, op1=ALU.subtract).then_inc(act_ready[c], 1)

            def split_act(c):
                for i in range(KD // 2):
                    dve.wait_ge(in_hi_done, KD // 2 * c + i + 1)
                    hi, v = act_hi[:, 2 * i:2 * i + 2, tok(c)], y[:, 2 * i:2 * i + 2, tok(c)]
                    dve.tensor_tensor(act_lo[:, 2 * i:2 * i + 2, tok(c)], v, hi, ALU.subtract).then_inc(act_ready[c], 2)
                    if i == 0:
                        split(3 * c, KD)

            def ffn(l, base, hid_n):
                for half in range(2):
                    b = base + half * (UP + DOWN)

                    def up_step(s, u, n, kn, f=None):
                        f = s // 2 if f is None else f
                        if s % 2 == 1 and s < UP:
                            hidden(u, 0, n, f, b + s)
                        if s % 2 == 1 and s >= LAG:
                            hidden(u - LAG, 1, n - 1, f - 1, b + s - LAG)
                        if kn:
                            split(u + 2, kn, at=b + s + 2)

                    if l == 2 and half == 0:
                        norm_center(1, 1)
                        split(b + 3, KD)
                        norm_reciprocal(1, 1)
                        norm_scale(1, 1)
                    up_step(1, b + 1, hid_n, 0)
                    with dve.Fori(0, 4) as i:
                        for j in range(4):
                            s = 2 + j
                            up_step(s, i * 4 + (b + s), i * 2 + (hid_n + s // 2), KD, i * 2 + s // 2)
                    for s in range(18, UP + LAG):
                        up_step(s, b + s, hid_n + s // 2, unit_kind(b + s + 2))
                    hid_n += KF
                    b += UP
                    for s in range(DOWN + LAG):
                        if l == 2 and half == 0 and s in (0, LAG):
                            dve.wait_ge(biased[s // LAG], 2 * KD)
                        if s < DOWN:
                            residual(b + s, 0, s, 1.0 if half else ALPHA)
                            if half == 1:
                                deviation(l, 0, s)
                        if half == 1 and s == DOWN:
                            norm_center(l, 0)
                        if s >= LAG:
                            residual(b + s - LAG, 1, s - LAG, 1.0 if half else ALPHA)
                            if half == 1:
                                deviation(l, 1, s - LAG)
                            if half == 1 and s == DOWN:
                                norm_reciprocal(l, 0)
                            if half == 1 and s == DOWN + 1:
                                norm_scale(l, 0)
                            for u in splits(b, s):
                                split(u, unit_kind(u))

            split_act(0)
            split(1, KD)
            split(2, KD)
            split_act(1)
            ffn(0, 0, 0)

            def rotate(u, c, dst):
                dve.wait_ge(mm_done[c], u + 1)
                dve.wait_ge(evac[c], u)
                dve.wait_ge(evac[1 - c], u - LAG if c == 0 else u + LAG + 1)
                x = psum[:, bank_of(u, c), 0:C]
                step(dve.tensor_tensor(tmp_v[:, c, :], x, cos_sin[:, 0, tok(c)], ALU.mult))
                half = HD // 2
                for q in range(0, P, half):
                    to = q + half if q % HD == 0 else q - half
                    ins = dve.tensor_tensor(tmp_r[to:to + half], x[q:q + half, :],
                                            cos_sin[q:q + half, 1, tok(c)], ALU.mult)
                step(ins)
                dve.tensor_tensor(dst, tmp_v[:, c, :], tmp_r, ALU.add).then_inc(evac[c], 1)

            def epilogue(m, c):
                u = MIX_BASE + m
                if m == U_K:
                    rotate(u, c, kT[:, tok(c)])
                elif U_Q <= m < U_GA:
                    rotate(u, c, qT[:, m - U_Q, tok(c)])
                    if m == U_GA - 1 and c == 1:
                        dve.wait_ge(evac[1], u + 1)
                        dve.tensor_copy(q_new[:, :].rearrange("p (j t) -> p j t", j=GQ), qT[:, :, SEQ:T]) \
                            .then_inc(q_new_done, 1)
                elif is_proj(m):
                    dve.wait_ge(mm_done[c], u + 1)
                    dve.wait_ge(evac[c], u)
                    prod = psum[:, bank_of(u, c), 0:C]
                    if m < U_GB:
                        gate = m1[:, m - U_PA, tok(c)]
                        dve.tensor_tensor(gate, prod, gate, ALU.mult) \
                            .then_inc(evac[c], 1)
                        return
                    o = (m - U_GB) // 2
                    if o:
                        dve.wait_ge(m_done[c], o)
                    dve.tensor_tensor(tmp_v[:, c, :], prod, tmp_a[:, c, :], ALU.mult).then_inc(evac[c], 1)
                    dve.wait_ge(evac[c], u + 1)
                    step(dve.tensor_tensor(tmp_v[:, c, :], tmp_v[:, c, :], m1[:, o, tok(c)], ALU.add))
                    step(dve.tensor_copy(m_hi[:, o, tok(c)], tmp_v[:, c, :]))
                    dve.tensor_tensor(m_lo[:, o, tok(c)], tmp_v[:, c, :], m_hi[:, o, tok(c)], ALU.subtract) \
                        .then_inc(m_done[c], 1)

            def pooled(g):
                n = NG - 1 - g
                if n == 0:
                    dve.wait_ge(att_mm, written("uout"))
                    dve.wait_ge(mixer_in, 16 * MIXER_DMAS)
                else:
                    dve.wait_ge(z_done, n)
                dve.wait_ge(win_done, n + 1)
                total = wins[:, 2 + n, :]
                head, tail = slice(BUF, BUF + max(WINDOWS)), slice(BUF + max(WINDOWS), LINE)
                step(dve.tensor_tensor(scratch, total[:, head], inv_cnt[:, g, :], ALU.mult))
                dve.tensor_tensor(line[:, g, head], scratch, line[:, g, head], ALU.subtract)
                dve.scalar_tensor_tensor(out=line[:, g, tail], in0=total[:, tail], scalar=1.0 / WINDOWS[g],
                                         in1=line[:, g, tail], op0=ALU.mult, op1=ALU.subtract).then_inc(z_done, 1)

            def grouped(name):
                dve.wait_ge(z_done, NG)
                for i, g in enumerate(GROUPS[name]):
                    dve.wait_ge(att_free, freed_before(name) + 2 * i + 2)
                    dve.tensor_tensor(pz_lo[:, g, :], scaled[:, (NG - 1 - g) % 3, :], pz_hi[:, g, :], ALU.subtract) \
                        .then_inc(poolz_done, 1)

            def scores(name):
                dve.wait_ge(att_mm, written(name))
                if name in ("Sa", "Sb"):
                    i, kv = NBLK, "ab".index(name[1])
                    if kv == 0:
                        dve.wait_ge(att_mm, written("T2"))
                    for n, (bank, k0, kn) in enumerate(((4, 0, 512), (5, 512, 512), (6, CTXK, NS))):
                        dve.scalar_tensor_tensor(out=p0[:, kv * SKEYS + k0:kv * SKEYS + k0 + kn],
                                                 in0=psum[:, bank, 0:kn], scalar=HD ** -0.5,
                                                 in1=smask[:, k0:k0 + kn], op0=ALU.mult, op1=ALU.add) \
                            .then_inc(att_free, 1)
                    if kv == 0:
                        return
                    pb, hn, sink = p0[:, 0:KV * SKEYS].rearrange("p (h k) -> p h k", h=KV), KV, sinks_s
                else:
                    i = int(name[1])
                    if i == 0:
                        dve.wait_ge(side_stored, 16 * SIDE_STORES)
                    k0 = WIN if i == 0 else 0
                    pb = (p0, p1)[i % 2][:, 0:H * 2 * WIN].rearrange("p (h k) -> p h k", h=H)[:, :, k0:2 * WIN]
                    hn, sink = H, sinks
                    mask = band[:, k0:2 * WIN].rearrange("p (a k) -> p a k", a=1).broadcast_to([P, 2, 2 * WIN - k0])
                    for b in range(4):
                        src = psum[:, 4 + b, :].rearrange("p (h k) -> p h k", h=2)[:, :, k0:2 * WIN]
                        dve.scalar_tensor_tensor(out=pb[:, 2 * b:2 * b + 2, :], in0=src, scalar=HD ** -0.5, in1=mask,
                                                 op0=ALU.mult, op1=ALU.add).then_inc(att_free, 1)
                dve.wait_ge(att_free, freed(name))
                st = soft[:, i % 2]
                step(dve.tensor_reduce(st[:, MAX, 0:hn], pb, AX.X, ALU.max))
                step(dve.tensor_tensor(st[:, MAX, 0:hn], st[:, MAX, 0:hn], sink[:, 0:hn], ALU.max))
                dve.tensor_scalar(st[:, NEG_MAX, 0:hn], st[:, MAX, 0:hn], -1.0, None, ALU.mult)
                dve.tensor_tensor(st[:, SINK, 0:hn], sink[:, 0:hn], st[:, MAX, 0:hn], ALU.subtract) \
                    .then_inc(neg_done, 1)

            def divide(i):
                dve.wait_ge(exp_done, i + 1)
                st = soft[:, i % 2]
                if i == NBLK:
                    pb, hn = p0[:, 0:KV * SKEYS].rearrange("p (h k) -> p h k", h=KV), KV
                else:
                    k0 = WIN if i == 0 else 0
                    pb = (p0, p1)[i % 2][:, 0:H * 2 * WIN].rearrange("p (h k) -> p h k", h=H)[:, :, k0:2 * WIN]
                    hn = H
                step(dve.tensor_tensor(st[:, DEN, 0:hn], st[:, SUM, 0:hn], st[:, SINK, 0:hn], ALU.add))
                step(dve.reciprocal(st[:, REC, 0:hn], st[:, DEN, 0:hn]))
                for h in range(hn):
                    ins = dve.tensor_scalar(pb[:, h, :], pb[:, h, :], st[:, REC, h:h + 1], None, ALU.mult)
                ins.then_inc(prob_done, 1)

            def attended(name):
                dve.wait_ge(att_mm, written(name))
                if name == "PVs":
                    t0, n = SEQ, NS
                else:
                    t0, n = int(name[2]) * WIN, WIN
                o = psum[:, 4, 0:GQ * n].rearrange("p (j t) -> p j t", j=GQ)
                step(dve.tensor_copy(att_hi[:, :, t0:t0 + n], o))
                dve.tensor_tensor(att_lo[:, :, t0:t0 + n], o, att_hi[:, :, t0:t0 + n], ALU.subtract) \
                    .then_inc(att_free, 1)

            def beside(at):
                for name in STAGES.get(at, []):
                    if name in GROUPS:
                        grouped(name)
                    elif name[0] == "S":
                        scores(name)
                    elif name[0:2] == "PV":
                        attended(name)
                for g in POOLED_AT.get(at, ()):
                    pooled(g)
                if at in DIVIDE_AT:
                    divide(DIVIDE_AT.index(at))

            for s in range(MIX1 + LAG):
                if s < MIX1:
                    epilogue(s, 0)
                if s == 0:
                    norm_center(0, 1)
                    split(MIX_BASE + 3, KD)
                    norm_reciprocal(0, 1)
                    norm_scale(0, 1)
                beside(s - 0.5)
                if s >= LAG:
                    epilogue(s - LAG, 1)
                    split(MIX_BASE + s + 2, unit_kind(MIX_BASE + s + 2))
                beside(s)
            for s in range(KD + LAG):
                if s in (0, LAG):
                    dve.wait_ge(biased[s // LAG], KD)
                if s < KD:
                    residual(WO_BASE + s, 0, s, ALPHA)
                    deviation(1, 0, s)
                if s == KD:
                    norm_center(1, 0)
                if s >= LAG:
                    residual(WO_BASE + s - LAG, 1, s - LAG, ALPHA)
                    deviation(1, 1, s - LAG)
                    if s == KD:
                        norm_reciprocal(1, 0)
                    if s == KD + 1:
                        norm_scale(1, 0)
                    for u in splits(WO_BASE, s):
                        split(u, unit_kind(u))
            ffn(2, FFN2_BASE, 2 * KF)
            norm_center(2, 1)
            norm_reciprocal(2, 1)
            norm_scale(2, 1)
            for o in range(LAST_AFFINE, KD):
                dve.wait_ge(norm_done[1], 2 * KD + o // 2 + 1)
                dve.tensor_scalar(y[:, o, tok(1)], y[:, o, tok(1)], ln_gb[:, 4, o:o + 1], ln_gb[:, 5, o:o + 1],
                                  ALU.mult, ALU.add).then_inc(aff_v_done, 1)
            dve.wait_ge(turn_done, len(TOK_TILES) + 5)
            for i, (t0, n, _) in list(enumerate(TOK_TILES))[3:6]:
                dve.tensor_copy(xin[0:n, i, 512:1024], psum[0:n, out_bank(i) + 1, :]).then_inc(yout_v_done, 1)

        @block.tensor
        def _(pe):
            def weights(s, k, hi):
                if k < KD:
                    return (ring_hi if hi else ring_lo)[:, s, k, :]
                return (ext_hi if hi else ext_lo)[:, s, k - KD, :]

            def part(u, c, kn, x_hi, x_lo, at=None, ready=None):
                s = (u if at is None else at) % SLOTS
                banks = ring_of(u if at is None else at)
                bank = bank_of(u if at is None else at, c)
                pe.wait_ge(lo_done, u + 1)
                if at is not None or u >= banks:
                    pe.wait_ge(evac[c], u - (banks - 1))
                for k in range(kn):
                    if ready:
                        ready(k)
                    o = psum[:, bank, 0:C]
                    pe.matmul(o, weights(s, k, True), x_hi[:, k, tok(c)], start=k == 0, stop=False)
                    pe.matmul(o, weights(s, k, True), x_lo[:, k, tok(c)], start=False, stop=False)
                    ins = pe.matmul(o, weights(s, k, False), x_hi[:, k, tok(c)], start=False, stop=k == kn - 1)
                ins.then_inc(mm_done[c], 1)

            def act_wait(l, c):
                return lambda k: pe.wait_ge(act_ready[c], KD * l + k + 1)

            def shift(l, c):
                pe.wait_ge(fsum_done[c], (KD - 2) * l + 1)
                pe.wait_ge(consts_in, 16 * CONST_DMAS)
                pe.matmul(psum[:, stat_bank(l, c), 0:C], mean_w[:, 0:P], fsum[:, c, :], start=True, stop=True) \
                    .then_inc(shift_mm[c], 1)

            def stats(l, c):
                bank = stat_bank(l, c)
                pe.wait_ge(shift_done[c], l + 1)
                pe.wait_ge(fsum_done[c], (KD - 2) * (l + 1))
                pe.matmul(psum[:, bank, 0:C], mean_w[:, 0:P], fsum[:, c, :], start=True, stop=False)
                pe.wait_ge(sqsum_done[c], (KD - 2) * (l + 1))
                pe.matmul(psum[:, bank ^ 1, 0:C], mean_w[:, 0:P], sq[:, 4 * c, :], start=True, stop=False)
                pe.wait_ge(y_done[c], y_before(l) + KD)
                pe.matmul(psum[:, bank, 0:C], mean_w[:, 0:P], y[:, KD - 1, tok(c)], start=False, stop=True)
                pe.wait_ge(sq_done[c], sq_op(l, KD - 1))
                pe.matmul(psum[:, bank ^ 1, 0:C], mean_w[:, 0:P], sq[:, sq_slot(c, KD - 1), :], start=False,
                          stop=True).then_inc(stats_done[c], 1)

            def ffn(l, base, act_l, hid_n):
                for half in range(2):
                    b = base + half * (UP + DOWN)
                    fresh = half == 0

                    def up_static(s, c):
                        part(b + s, c, KD, act_hi, act_lo, ready=act_wait(act_l, c) if fresh and s == 0 else None)

                    if l == 2 and half == 0:
                        pe.wait_ge(evac[1], b - 1)
                    up_static(0, 0)
                    if l == 0 and half == 0:
                        for i in range(3, len(TOK_TILES)):
                            turn_in(i)
                    up_static(1, 0)
                    if l == 0 and half == 0:
                        pe.wait_ge(turn_read, len(TOK_TILES))
                    for s, c in ((2, 0), (3, 0), (0, 1), (1, 1), (4, 0), (2, 1), (5, 0), (3, 1)):
                        up_static(s, c)
                    with pe.Fori(0, 4) as i:
                        for j in range(4):
                            s = LAG + 4 + j
                            part(i * 4 + (b + s), 0, KD, act_hi, act_lo, at=b + s)
                            part(i * 4 + (b + s - LAG), 1, KD, act_hi, act_lo, at=b + s - LAG)
                    for s in range(UP, UP + LAG):
                        up_static(s - LAG, 1)
                    b += UP
                    if l == 0 and half == 0:
                        pe.wait_ge(vec_in, 16 * VEC_DMAS)
                        pe.wait_ge(evac[0], b - 2)
                        pe.transpose(psum[:, VEC_BANK, 0:VEC_ROWS], vec_rows, ident[0:VEC_ROWS, 0:VEC_ROWS]) \
                            .then_inc(turn_done, 1)

                    def hid_wait(c):
                        return lambda k: pe.wait_ge(hid_done[c], hid_n + k + 1)

                    for s in range(DOWN + LAG):
                        if l == 0 and half == 0 and s == 1:
                            pe.wait_ge(vecs_done, 1)
                        if s < DOWN:
                            part(b + s, 0, KF, hid_hi, hid_lo, ready=hid_wait(0) if s == 0 else None)
                        if half == 1 and s == 2:
                            shift(l, 0)
                        if s >= LAG:
                            part(b + s - LAG, 1, KF, hid_hi, hid_lo, ready=hid_wait(1) if s == LAG else None)
                        if half == 1 and s == 2 + LAG:
                            shift(l, 1)
                        if half == 1 and s == DOWN - 1:
                            stats(l, 0)
                    hid_n += KF
                stats(l, 1)

            def turn_in(i):
                t0, n, _ = TOK_TILES[i]
                pe.wait_ge(x_in[i], 16)
                if i >= 3:
                    pe.wait_ge(turn_read, i - 2)
                for o in range(KD):
                    ins = pe.transpose(psum[:, in_bank(i) + o // 4, (o % 4) * n:(o % 4 + 1) * n],
                                       xin[0:n, i, o * P:(o + 1) * P], ident[0:n, 0:n])
                ins.then_inc(turn_done, 1)

            def turn_out(c):
                if c == 0:
                    for b in range(2):
                        pe.wait_ge(evac[b], UNITS)
                else:
                    pe.wait_ge(yout_done, 6)
                for o in range(KD):
                    if c and o >= LAST_AFFINE:
                        pe.wait_ge(aff_v_done, o - LAST_AFFINE + 1)
                    else:
                        pe.wait_ge(aff_done[c], 2 * KD + o + 1)
                    for i, (t0, n, _) in list(enumerate(TOK_TILES))[3 * c:3 * c + 3]:
                        ins = pe.transpose(psum[0:n, out_bank(i) + o // 4, (o % 4) * P:(o % 4 + 1) * P],
                                           y[:, o, t0:t0 + n], ident[:, :])
                    if o % 4 == 3:
                        ins.then_inc(turn_done, 1)

            pe.wait_ge(ident_in, 16)
            for i in range(3):
                turn_in(i)
            ffn(0, 0, 0, 0)

            def attend(name):
                if name == "kctx":
                    pe.wait_ge(var_done[1], 1)
                elif name != ROUNDS[0]:
                    pe.wait_ge(att_free, freed_before(name))
                if name == "poolctx":
                    pe.wait_ge(evac[1], FFN_UNITS)
                    pe.wait_ge(mixer_in, 16 * MIXER_DMAS)
                    for g in range(NG):
                        ins = pe.transpose(psum[:, 4, g * P:g * P + DB * BUF], uctx[0:DB * BUF, g * P:(g + 1) * P],
                                           ident[0:DB * BUF, 0:DB * BUF])
                elif name == "kctx":
                    for b in range(DB):
                        ins = pe.transpose(psum[:, 5 + b // 4, (b % 4) * P:(b % 4 + 1) * P], kctx[b // 4][:, b % 4, :],
                                           ident[:, :])
                elif name == "uout":
                    for c in range(2):
                        pe.wait_ge(evac[c], MIX_BASE + NG)
                    for g in range(NG):
                        pe.transpose(psum[0:BUF, 4, g * P:(g + 1) * P], line[:, g, SEQ:SEQ + BUF], ident[:, :])
                        ins = pe.transpose(psum[0:NS, 5, g * P:(g + 1) * P], u_new[:, g, :], ident[:, :])
                elif name == "vkout":
                    for c in range(2):
                        pe.wait_ge(evac[c], MIX_BASE + U_K + 1)
                    for n in range(NBLK):
                        pe.transpose(psum[:, 4, n * P:(n + 1) * P], vT[:, n * WIN:(n + 1) * WIN], ident[:, :])
                    pe.transpose(psum[0:NS, 5, 0:P], vT[:, SEQ:T], ident[:, :])
                    pe.transpose(psum[:, 6, 0:P], kT[:, SEQ - WIN:SEQ], ident[:, :])
                    ins = pe.transpose(psum[0:NS, 7, 0:P], kT[:, SEQ:T], ident[:, :])
                elif name in GROUPS:
                    for i, g in enumerate(GROUPS[name]):
                        pe.wait_ge(z_done, NG - g)
                        z = line[:, g, :]
                        w = grp_w[:, g, :]
                        n = SEQ - C
                        seg = z[:, BUF + SEQ:LINE].rearrange("p (b s) -> p b s", s=SEG)[:, :, BUF:SEG]
                        pe.matmul(psum[:, 4 + 2 * i, 0:C], w, z[:, BUF:BUF + C], start=True, stop=True)
                        pe.matmul(psum[:, 5 + 2 * i, 0:n], w, z[:, BUF + C:BUF + SEQ], start=True, stop=True)
                        ins = pe.matmul(psum[:, 5 + 2 * i, n:C], w, seg, start=True, stop=True)
                elif name in ("Sa", "Sb"):
                    kv = "ab".index(name[1])
                    h = slice(kv * HD, (kv + 1) * HD)
                    q = q_new[h, :]
                    pe.wait_ge(q_new_done, 1)
                    pe.matmul(psum[:, 4, :], q, kctxT[h, 0:512], start=True, stop=True)
                    pe.matmul(psum[:, 5, :], q, kctxT[h, 512:1024], start=True, stop=True)
                    ins = pe.matmul(psum[:, 6, 0:NS], q, kT[h, SEQ:T], start=True, stop=True)
                elif name[0] == "S":
                    n = int(name[1])
                    if n in (0, 2):
                        pe.wait_ge(evac[n // 2], MIX_BASE + U_GA)
                    k0 = WIN if n == 0 else 0
                    keys = slice((n - 1) * WIN + k0, (n + 1) * WIN)
                    for kv in range(KV):
                        h = slice(kv * HD, (kv + 1) * HD)
                        for j in range(GQ):
                            at = (j % 2) * 2 * WIN
                            ins = pe.matmul(psum[:, 4 + 2 * kv + j // 2, at + k0:at + 2 * WIN],
                                            qT[h, j, n * WIN:(n + 1) * WIN], kT[h, keys], start=True, stop=True)
                elif name in ("Ta", "Tb"):
                    kv = "ab".index(name[1])
                    pe.wait_ge(prob_done, NBLK + 1)
                    pk = p0[:, kv * SKEYS:(kv + 1) * SKEYS]
                    for b in range(DB):
                        pe.transpose(psum[:, 4 + b // 4, (b % 4) * P:(b % 4 + 1) * P], pk[:, b * WIN:(b + 1) * WIN],
                                     ident[:, :])
                    ins = pe.transpose(psum[0:NS, 6, 0:P], pk[:, CTXK:SKEYS], ident[:, :])
                elif name[0] == "T":
                    n = int(name[1])
                    pe.wait_ge(prob_done, n + 1)
                    pb = (p0, p1)[n % 2][:, 0:H * 2 * WIN].rearrange("p (h k) -> p h k", h=H)
                    for kt in range(1 if n == 0 else 0, 2):
                        for h in range(H):
                            ins = pe.transpose(psum[:, 4 + 2 * kt + h // GQ, (h % GQ) * P:(h % GQ + 1) * P],
                                               pb[:, h, kt * WIN:(kt + 1) * WIN], ident[:, :])
                elif name == "PVs":
                    for kv in range(KV):
                        h = slice(kv * HD, (kv + 1) * HD)
                        pk = pT[:, kv * (DB + 1) * P:(kv + 1) * (DB + 1) * P]
                        for b in range(DB):
                            pe.matmul(psum[h, 4, 0:P], vctx[:, b, h], pk[:, b * P:(b + 1) * P], start=b == 0, stop=False)
                        ins = pe.matmul(psum[h, 4, 0:P], vN[0:NS, NBLK, h], pk[0:NS, CTXK:CTXK + P], start=False,
                                        stop=True)
                else:
                    n = int(name[2])
                    first = 1 if n == 0 else 0
                    for kv in range(KV):
                        h = slice(kv * HD, (kv + 1) * HD)
                        for kt in range(first, 2):
                            ins = pe.matmul(psum[h, 4, :], vN[:, n - 1 + kt, h],
                                            pT[:, (2 * kt + kv) * 512:(2 * kt + kv + 1) * 512], start=kt == first,
                                            stop=kt == 1)
                ins.then_inc(att_mm, 1)

            def mix_part(m, c):
                u = MIX_BASE + m
                if not is_proj(m):
                    part(u, c, KD, act_hi, act_lo, ready=act_wait(1, c) if m == 0 else None)
                elif m < U_GB:
                    if m == U_PA:
                        pe.wait_ge(poolz_done, NG)
                    part(u, c, NG, pz_hi, pz_lo)
                else:
                    if m == U_GB + 1:
                        pe.wait_ge(att_free, freed("PVs" if c else "PV2"))
                    part(u, c, NG, att_hi, att_lo)

            def beside(at):
                for name in STAGES.get(at, []):
                    attend(name)

            for s in range(MIX1 + LAG):
                if s < MIX1:
                    mix_part(s, 0)
                beside(s - 0.5)
                for m in (0, 1) if s == LAG + 1 else (s - LAG,) if s > LAG else ():
                    mix_part(m, 1)
                beside(s)
            for s in range(KD + LAG):
                def m_wait(c):
                    return lambda k: pe.wait_ge(m_done[c], k + 1)
                if s < KD:
                    part(WO_BASE + s, 0, KD, m_hi, m_lo, ready=m_wait(0) if s == 0 else None)
                if s == 2:
                    shift(1, 0)
                if s >= LAG:
                    part(WO_BASE + s - LAG, 1, KD, m_hi, m_lo, ready=m_wait(1) if s == LAG else None)
                if s == 2 + LAG:
                    shift(1, 1)
                if s == KD - 1:
                    stats(1, 0)
            stats(1, 1)
            ffn(2, FFN2_BASE, 2, 2 * KF)
            turn_out(0)
            turn_out(1)


VEC_BANK = (UP + 1) % 4


def in_bank(i):
    return 2 + 2 * (i % 3)


def out_bank(i):
    return 2 * (i % 3)


CONST_DMAS = 4 + GQ
MIXER_DMAS = 7
VEC_DMAS = 7
VEC_ROWS = 6 * KD + NG
SIDE_STORES = 3 + 1 + DB + 2 + 2 * DB


def constants():
    f = np.float32
    tok_pos = np.concatenate([np.arange(SEQ), PAST + np.tile(np.arange(DS), DB)]).astype(f)
    freqs = f(THETA) ** (f(-2.0) * np.arange(HD // 2, dtype=f) / f(HD))
    ang = tok_pos[None, :] * freqs[:, None].astype(f)
    cos, sin = np.cos(ang), np.sin(ang)
    cos_sin = np.stack([np.concatenate([cos, cos] * KV), np.concatenate([sin, -sin] * KV)], axis=1).astype(f)
    q = np.arange(WIN)[:, None]
    k = np.arange(WIN)[None, :]
    band = np.concatenate([np.where(k >= q, 0, NEG), np.where(k <= q, 0, NEG)], axis=1).astype(f)
    b, t = np.arange(P)[:, None] % NS // DS, np.arange(P)[:, None] % DS
    ck, nk = np.arange(CTXK)[None, :], np.arange(NS)[None, :]
    smask = np.concatenate([np.where((ck // WIN == b) & (ck % WIN >= t), 0, NEG),
                            np.where((nk // DS == b) & (nk % DS <= t), 0, NEG)], axis=1).astype(f)
    cnt = np.stack([np.minimum(np.arange(max(WINDOWS)) + 1, w) for w in WINDOWS])
    inv = np.broadcast_to((1.0 / cnt).astype(f), (P, NG, max(WINDOWS)))
    mean = np.concatenate([np.full((P, P), 1.0 / D), np.full((P, 1), EPS)], axis=1).astype(f)
    return {"c_ident": np.eye(P, dtype=f), "c_mean": mean, "c_cos_sin": cos_sin,
            "c_band": band, "c_smask": smask, "c_inv_cnt": np.ascontiguousarray(inv)}


INS = ["x_prompt", "x_sample", "cache_pool_u", "cache_k_win", "cache_v_win", "w_in", "pool_w_grp", "pool_scale",
       "attn_sinks", "w_pool_out", "w_attn_out", "w_out", "ffn1_w1", "ffn1_w3", "ffn1_w2", "ffn2_w1", "ffn2_w3",
       "ffn2_w2", "ln1_g", "ln1_b", "ln2_g", "ln2_b", "ln3_g", "ln3_b"]
OUTS = {"y_prompt": (1, SEQ, D), "y_sample": (DB, DS, D), "pool_u_prompt": (1, 1, BUF, POOLW),
        "k_win_prompt": (1, 1, WIN, KV, HD), "v_win_prompt": (1, 1, WIN, KV, HD),
        "pool_u_sample": (1, DB, BUF, POOLW), "k_win_sample": (1, DB, WIN, KV, HD),
        "v_win_sample": (1, DB, WIN, KV, HD)}


def kernel(**inputs):
    import concourse.bacc as bacc
    from concourse.bass_utils import run_bass_kernel_spmd

    nc = bacc.Bacc("TRN2", target_bir_lowering=False, num_devices=1)
    arrays = {name: np.ascontiguousarray(inputs[name]) for name in INS}
    arrays.update(constants())
    a = {name: nc.dram_tensor(f"in_{name}", v.shape, F32, kind="ExternalInput").ap() for name, v in arrays.items()}
    out = {name: nc.dram_tensor(f"out_{name}", shape, F32, kind="ExternalOutput").ap() for name, shape in OUTS.items()}
    program(nc, a, out)
    r = run_bass_kernel_spmd(nc, [{f"in_{name}": v for name, v in arrays.items()}], core_ids=[0])
    return tuple(r.results[0][f"out_{name}"] for name in OUTS)
```
